# Optimizing a Trainium2 kernel written in Bass

```python
import math
import jax, jax.numpy as jnp
from jax import lax
import numpy as np

D_MODEL = 1024
BATCH = 1
SEQ = 512
DEPTH = 2

N_A_LAYERS = DEPTH // 2
N_B_LAYERS = DEPTH - N_A_LAYERS

GDN_HEADS = 8
GDN_DK = 128
GDN_DV = 128
GDN_QK_WIDTH = GDN_HEADS * GDN_DK
GDN_V_WIDTH = GDN_HEADS * GDN_DV
GDN_CONV = 4
GDN_CHUNK = 64
GDN_IN_WIDTH = 2 * GDN_QK_WIDTH + 2 * GDN_V_WIDTH + 2 * GDN_HEADS

FOX_HEADS = 16
FOX_HD = 64
FOX_WIDTH = FOX_HEADS * FOX_HD
FOX_QBLOCK = 128
KV_WIDTH = 2 * FOX_WIDTH + FOX_HEADS

D_FF = int(math.ceil(8 * D_MODEL / 3 / 256) * 256)

RMS_EPS = 1e-6


def rms_norm(x, w):
    xf = x.astype(jnp.float32)
    y = xf * lax.rsqrt(jnp.mean(xf * xf, axis=-1, keepdims=True) + RMS_EPS)
    return (y * w.astype(jnp.float32)).astype(x.dtype)

def l2_normalize(x):
    xf = x.astype(jnp.float32)
    return xf * lax.rsqrt(jnp.sum(xf * xf, axis=-1, keepdims=True) + RMS_EPS)

def causal_depthwise_conv_silu(x, w):
    k_width = w.shape[0]
    y = lax.conv_general_dilated(
        x, w[:, None, :].astype(x.dtype), window_strides=(1,), padding=[(k_width - 1, 0)],
        dimension_numbers=("NWC", "WIO", "NWC"), feature_group_count=x.shape[-1])
    return jax.nn.silu(y)

def gated_delta_rule_chunked(q, k, v, g, beta):
    b_sz, t_len, n_h, d_k = q.shape
    d_v = v.shape[-1]
    c = GDN_CHUNK
    n_c = t_len // c

    def to_chunks(a):
        return a.reshape(b_sz, n_c, c, n_h, *a.shape[3:]).swapaxes(2, 3)

    qc, kc, vc, gc, bc = map(to_chunks, (q, k, v, g, beta))
    G = jnp.cumsum(gc, axis=-1)
    causal = jnp.tril(jnp.ones((c, c), dtype=bool))
    strict = jnp.tril(jnp.ones((c, c), dtype=bool), -1)
    diff = G[..., :, None] - G[..., None, :]
    decay_mat = jnp.where(causal, jnp.exp(jnp.where(causal, diff, 0.0)), 0.0)

    kk = jnp.einsum("bnhcd,bnhsd->bnhcs", kc, kc)
    a_strict = jnp.where(strict, bc[..., :, None] * kk * decay_mat, 0.0)
    rhs = jnp.concatenate([bc[..., None] * kc * jnp.exp(G)[..., None], bc[..., None] * vc], axis=-1)
    sol = lax.linalg.triangular_solve(a_strict, rhs, left_side=True, lower=True, unit_diagonal=True)
    w_c, u_c = sol[..., :d_k], sol[..., d_k:]

    a_qk = jnp.einsum("bnhcd,bnhsd->bnhcs", qc, kc) * decay_mat
    g_last = G[..., -1]
    q_dec = qc * jnp.exp(G)[..., None]
    k_dec = kc * jnp.exp(g_last[..., None] - G)[..., None]

    xs = tuple(jnp.moveaxis(a, 1, 0) for a in (q_dec, k_dec, u_c, w_c, a_qk, jnp.exp(g_last)))

    def step(state, inp):
        qg, kd, u_i, w_i, a_i, gl = inp
        v_new = u_i - jnp.einsum("bhcd,bhde->bhce", w_i, state)
        o = jnp.einsum("bhcd,bhde->bhce", qg, state) + jnp.einsum("bhcs,bhse->bhce", a_i, v_new)
        state = state * gl[..., None, None] + jnp.einsum("bhcd,bhce->bhde", kd, v_new)
        return state, o

    s0 = jnp.zeros((b_sz, n_h, d_k, d_v), jnp.float32)
    _, o = lax.scan(step, s0, xs)
    return o.transpose(1, 0, 3, 2, 4).reshape(b_sz, t_len, n_h, d_v)

def gated_deltanet_mixer(h, w_in, conv_w, a_log, dt_bias, out_norm, w_out):
    b_sz, t_len, _ = h.shape
    proj = h @ w_in
    o1 = 2 * GDN_QK_WIDTH + GDN_V_WIDTH
    o2 = o1 + GDN_V_WIDTH
    qkv = causal_depthwise_conv_silu(proj[..., :o1], conv_w)
    z = proj[..., o1:o2].reshape(b_sz, t_len, GDN_HEADS, GDN_DV)
    b_logit = proj[..., o2:o2 + GDN_HEADS]
    a_in = proj[..., o2 + GDN_HEADS:]
    q = qkv[..., :GDN_QK_WIDTH].reshape(b_sz, t_len, GDN_HEADS, GDN_DK)
    k = qkv[..., GDN_QK_WIDTH:2 * GDN_QK_WIDTH].reshape(b_sz, t_len, GDN_HEADS, GDN_DK)
    v = qkv[..., 2 * GDN_QK_WIDTH:].reshape(b_sz, t_len, GDN_HEADS, GDN_DV).astype(jnp.float32)
    q = l2_normalize(q) * (GDN_DK ** -0.5)
    k = l2_normalize(k)
    beta = jax.nn.sigmoid(b_logit.astype(jnp.float32))
    g = -jnp.exp(a_log.astype(jnp.float32)) * jax.nn.softplus(
        a_in.astype(jnp.float32) + dt_bias.astype(jnp.float32))
    o = gated_delta_rule_chunked(q, k, v, g, beta).astype(h.dtype)
    o = rms_norm(o, out_norm) * jax.nn.silu(z)
    return o.reshape(b_sz, t_len, GDN_V_WIDTH) @ w_out

def shared_kv(x, kv_norm, w_kv, b_forget):
    b_sz, t_len, _ = x.shape
    kvf = rms_norm(x, kv_norm) @ w_kv
    k = kvf[..., :FOX_WIDTH].reshape(b_sz, t_len, FOX_HEADS, FOX_HD).transpose(0, 2, 1, 3)
    v = kvf[..., FOX_WIDTH:2 * FOX_WIDTH].reshape(b_sz, t_len, FOX_HEADS, FOX_HD).transpose(0, 2, 1, 3)
    f_logit = (kvf[..., 2 * FOX_WIDTH:] + b_forget).astype(jnp.float32)
    log_f_cum = jnp.cumsum(jax.nn.log_sigmoid(f_logit), axis=1).transpose(0, 2, 1)
    return k, v, log_f_cum

def forgetting_attention_mixer(h, w_q, w_o, k, v, log_f_cum):
    b_sz, t_len, _ = h.shape
    q = (h @ w_q).reshape(b_sz, t_len, FOX_HEADS, FOX_HD).transpose(0, 2, 1, 3)
    scale = FOX_HD ** -0.5
    outs = []
    for blk in range(t_len // FOX_QBLOCK):
        s0 = blk * FOX_QBLOCK
        e = s0 + FOX_QBLOCK
        s = jnp.einsum("bhqd,bhkd->bhqk", q[:, :, s0:e], k[:, :, :e]).astype(jnp.float32) * scale
        s = s + log_f_cum[:, :, s0:e, None] - log_f_cum[:, :, None, :e]
        mask = (s0 + jnp.arange(FOX_QBLOCK))[:, None] >= jnp.arange(e)[None, :]
        p = jax.nn.softmax(jnp.where(mask, s, -jnp.inf), axis=-1)
        outs.append(jnp.einsum("bhqk,bhkd->bhqd", p.astype(v.dtype), v[:, :, :e]))
    o = jnp.concatenate(outs, axis=2)
    return o.transpose(0, 2, 1, 3).reshape(b_sz, t_len, FOX_WIDTH) @ w_o

def swiglu(h, w_in, w_out):
    gu = h @ w_in
    return (jax.nn.silu(gu[..., :D_FF]) * gu[..., D_FF:]) @ w_out

def first_inputs(seed: int = 0) -> dict:
    key = jax.random.key(seed)
    ks = jax.random.split(key, 20)
    f32 = jnp.float32

    def w(k, shape, fan_in):
        return jax.random.normal(k, shape, f32) * (fan_in ** -0.5)

    def gain(k, shape):
        return 1.0 + 0.1 * jax.random.normal(k, shape, f32)

    x = jax.random.normal(ks[0], (BATCH, SEQ, D_MODEL), f32)
    a_init = jax.random.uniform(ks[9], (N_A_LAYERS, GDN_HEADS), f32, 1.0, 16.0)
    dt = jnp.exp(jax.random.uniform(ks[10], (N_A_LAYERS, GDN_HEADS), f32, math.log(1e-3), math.log(0.1)))
    return {
        "x": x,
        "pre_mix_norm": gain(ks[1], (DEPTH, D_MODEL)),
        "post_mix_norm": gain(ks[2], (DEPTH, D_MODEL)),
        "pre_ffn_norm": gain(ks[3], (DEPTH, D_MODEL)),
        "post_ffn_norm": gain(ks[4], (DEPTH, D_MODEL)),
        "w_ffn_in": w(ks[5], (DEPTH, D_MODEL, 2 * D_FF), D_MODEL),
        "w_ffn_out": w(ks[6], (DEPTH, D_FF, D_MODEL), D_FF),
        "gdn_w_in": w(ks[7], (N_A_LAYERS, D_MODEL, GDN_IN_WIDTH), D_MODEL),
        "gdn_conv": w(ks[8], (N_A_LAYERS, GDN_CONV, 2 * GDN_QK_WIDTH + GDN_V_WIDTH), GDN_CONV),
        "gdn_a_log": jnp.log(a_init),
        "gdn_dt_bias": dt + jnp.log(-jnp.expm1(-dt)),
        "gdn_out_norm": gain(ks[11], (N_A_LAYERS, GDN_DV)),
        "gdn_w_out": w(ks[12], (N_A_LAYERS, GDN_V_WIDTH, D_MODEL), GDN_V_WIDTH),
        "kv_norm": gain(ks[13], (D_MODEL,)),
        "w_kv": w(ks[14], (D_MODEL, KV_WIDTH), D_MODEL),
        "b_forget": 2.0 + 0.5 * jax.random.normal(ks[15], (FOX_HEADS,), f32),
        "fox_w_q": w(ks[16], (N_B_LAYERS, D_MODEL, FOX_WIDTH), D_MODEL),
        "fox_w_o": w(ks[17], (N_B_LAYERS, FOX_WIDTH, D_MODEL), FOX_WIDTH),
    }

def first_block(x, pre_mix_norm, post_mix_norm, pre_ffn_norm, post_ffn_norm, w_ffn_in, w_ffn_out,
              gdn_w_in, gdn_conv, gdn_a_log, gdn_dt_bias, gdn_out_norm, gdn_w_out,
              kv_norm, w_kv, b_forget, fox_w_q, fox_w_o):
    k_sh = v_sh = c_sh = None
    for layer in range(DEPTH):
        h = rms_norm(x, pre_mix_norm[layer])
        if layer < N_A_LAYERS:
            i = layer
            mix = gated_deltanet_mixer(h, gdn_w_in[i], gdn_conv[i], gdn_a_log[i], gdn_dt_bias[i],
                                       gdn_out_norm[i], gdn_w_out[i])
        else:
            i = layer - N_A_LAYERS
            if i == 0:
                k_sh, v_sh, c_sh = shared_kv(x, kv_norm, w_kv, b_forget)
            mix = forgetting_attention_mixer(h, fox_w_q[i], fox_w_o[i], k_sh, v_sh, c_sh)
        x = x + rms_norm(mix, post_mix_norm[layer])
        f = swiglu(rms_norm(x, pre_ffn_norm[layer]), w_ffn_in[layer], w_ffn_out[layer])
        x = x + rms_norm(f, post_ffn_norm[layer])
    return x


DEPTH_2 = 1

CHUNK = 64
ROPE_THETA = 10000.0
NEG_INF = -1e30

A_HEADS = 8
A_HEAD_DIM = 64
A_WIDTH = A_HEADS * A_HEAD_DIM
IDX_HEADS = 8
IDX_DIM = 64
IDX_ROPE_DIM = 32
TOPK_MAX = 256
SPARSE_Q_BLOCK = 32

B_HEADS = 8
B_NOPE_DIM = 64
B_ROPE_DIM = 32
B_QK_DIM = B_NOPE_DIM + B_ROPE_DIM
B_V_DIM = 64
B_WIDTH = B_HEADS * B_V_DIM
Q_LORA = 384
KV_LORA = 256
DENSE_Q_BLOCK = 128

D_MIX = A_WIDTH + B_WIDTH
IN_SPLITS = (A_WIDTH, A_WIDTH, A_WIDTH, A_WIDTH, IDX_HEADS * IDX_DIM, IDX_DIM, IDX_HEADS,
             Q_LORA, KV_LORA, B_ROPE_DIM, B_WIDTH)
D_IN = 4 * A_WIDTH + IDX_HEADS * IDX_DIM + IDX_DIM + IDX_HEADS + Q_LORA + KV_LORA + B_ROPE_DIM + B_WIDTH


def rms_norm_2(x, g):
    xf = x.astype(jnp.float32)
    y = xf * lax.rsqrt(jnp.mean(xf * xf, axis=-1, keepdims=True) + RMS_EPS)
    return (y * g.astype(jnp.float32)).astype(x.dtype)

def rope(x, pos):
    d = x.shape[-1]
    half = d // 2
    freqs = jnp.power(ROPE_THETA, -jnp.arange(half, dtype=jnp.float32) * 2.0 / d)
    ang = pos.astype(jnp.float32)[:, None] * freqs[None, :]
    cos = jnp.cos(ang)[None, :, None, :]
    sin = jnp.sin(ang)[None, :, None, :]
    xf = x.astype(jnp.float32)
    x1, x2 = xf[..., :half], xf[..., half:]
    return jnp.concatenate([x1 * cos - x2 * sin, x2 * cos + x1 * sin], axis=-1).astype(x.dtype)

def chunk_limit(pos):
    return (pos // CHUNK + 1) * CHUNK

def indexer_sparse_attention(q, k, v, q_idx, k_idx, w_idx, pos):
    B, S, H, dh = q.shape
    topk = min(TOPK_MAX, S // 4)
    nblk = S // SPARSE_Q_BLOCK
    key_pos = jnp.arange(S, dtype=jnp.int32)
    idx_scale = (IDX_DIM * IDX_HEADS) ** -0.5
    att_scale = dh ** -0.5

    def to_blocks(a):
        return jnp.moveaxis(a.reshape(B, nblk, SPARSE_Q_BLOCK, *a.shape[2:]), 1, 0)

    def block(args):
        qb, qib, wb, pb = args
        limit = chunk_limit(pb)
        rel = jax.nn.relu(jnp.einsum('bqhd,bsd->bqhs', qib, k_idx).astype(jnp.float32))
        score = jnp.einsum('bqhs,bqh->bqs', rel, wb.astype(jnp.float32)) * idx_scale
        admissible = key_pos[None, :] < limit[:, None]
        score = jnp.where(admissible[None], score, NEG_INF)
        _, sel = lax.top_k(score, topk)
        valid = sel < limit[None, :, None]
        k_sel = jax.vmap(lambda kb, ib: kb[ib])(k, sel)
        v_sel = jax.vmap(lambda vb, ib: vb[ib])(v, sel)
        logits = jnp.einsum('bqhd,bqkhd->bhqk', qb, k_sel).astype(jnp.float32) * att_scale
        logits = jnp.where(valid[:, None], logits, NEG_INF)
        p = jax.nn.softmax(logits, axis=-1).astype(v.dtype)
        return jnp.einsum('bhqk,bqkhd->bqhd', p, v_sel)

    out = lax.map(block, (to_blocks(q), to_blocks(q_idx), to_blocks(w_idx),
                          pos.reshape(nblk, SPARSE_Q_BLOCK)))
    return jnp.moveaxis(out, 0, 1).reshape(B, S, H, dh)

def chunk_causal_attention(q, k, v, pos):
    B, S, H, dq = q.shape
    dv = v.shape[-1]
    nblk = S // DENSE_Q_BLOCK
    scale = dq ** -0.5

    def block(args):
        qb, pb = args
        logits = jnp.einsum('bqhd,bshd->bhqs', qb, k).astype(jnp.float32) * scale
        mask = pos[None, :] < chunk_limit(pb)[:, None]
        logits = jnp.where(mask[None, None], logits, NEG_INF)
        p = jax.nn.softmax(logits, axis=-1).astype(v.dtype)
        return jnp.einsum('bhqs,bshd->bqhd', p, v)

    qbl = jnp.moveaxis(q.reshape(B, nblk, DENSE_Q_BLOCK, H, dq), 1, 0)
    out = lax.map(block, (qbl, pos.reshape(nblk, DENSE_Q_BLOCK)))
    return jnp.moveaxis(out, 0, 1).reshape(B, S, H, dv)

def second_inputs(seed: int = 0) -> dict:
    key = jax.random.key(seed)
    ks = jax.random.split(key, 12)
    f32 = jnp.float32

    def gain(k, n):
        return 1.0 + 0.02 * jax.random.normal(k, (DEPTH_2, n), f32)

    x = jax.random.normal(ks[0], (BATCH, SEQ, D_MODEL), f32)
    norm_gain = gain(ks[1], D_MODEL)
    w_in = jax.random.normal(ks[2], (DEPTH_2, D_MODEL, D_IN), f32) * D_MODEL ** -0.5
    a_q_norm = gain(ks[3], A_HEAD_DIM)
    a_k_norm = gain(ks[4], A_HEAD_DIM)
    b_q_latent_norm = gain(ks[5], Q_LORA)
    b_kv_latent_norm = gain(ks[6], KV_LORA)
    w_uq = jax.random.normal(ks[7], (DEPTH_2, Q_LORA, B_HEADS * B_QK_DIM), f32) * Q_LORA ** -0.5
    w_ukv = jax.random.normal(ks[8], (DEPTH_2, KV_LORA, B_HEADS * (B_NOPE_DIM + B_V_DIM)), f32) * KV_LORA ** -0.5
    b_q_norm = gain(ks[9], B_QK_DIM)
    b_k_norm = gain(ks[10], B_QK_DIM)
    w_out = jax.random.normal(ks[11], (DEPTH_2, D_MIX, D_MODEL), f32) * D_MIX ** -0.5
    return {"x": x, "norm_gain": norm_gain, "w_in": w_in, "a_q_norm": a_q_norm,
            "a_k_norm": a_k_norm, "b_q_latent_norm": b_q_latent_norm,
            "b_kv_latent_norm": b_kv_latent_norm, "w_uq": w_uq, "w_ukv": w_ukv,
            "b_q_norm": b_q_norm, "b_k_norm": b_k_norm, "w_out": w_out}

def second_block(x, norm_gain, w_in, a_q_norm, a_k_norm, b_q_latent_norm, b_kv_latent_norm,
              w_uq, w_ukv, b_q_norm, b_k_norm, w_out):
    B, S, _ = x.shape
    pos = jnp.arange(S, dtype=jnp.int32)
    offsets = [int(o) for o in np.cumsum(IN_SPLITS)[:-1]]
    h = x
    for l in range(DEPTH_2):
        xn = rms_norm_2(h, norm_gain[l])
        proj = xn @ w_in[l]
        (q_a, k_a, v_a, g_a, q_i, k_i, w_i,
         c_q, c_kv, k_rope, g_b) = jnp.split(proj, offsets, axis=-1)

        q_a = rope(rms_norm_2(q_a.reshape(B, S, A_HEADS, A_HEAD_DIM), a_q_norm[l]), pos)
        k_a = rope(rms_norm_2(k_a.reshape(B, S, A_HEADS, A_HEAD_DIM), a_k_norm[l]), pos)
        v_a = v_a.reshape(B, S, A_HEADS, A_HEAD_DIM)
        q_i = q_i.reshape(B, S, IDX_HEADS, IDX_DIM)
        q_i = jnp.concatenate([rope(q_i[..., :IDX_ROPE_DIM], pos), q_i[..., IDX_ROPE_DIM:]], axis=-1)
        k_i = k_i[:, :, None, :]
        k_i = jnp.concatenate([rope(k_i[..., :IDX_ROPE_DIM], pos), k_i[..., IDX_ROPE_DIM:]], axis=-1)[:, :, 0, :]
        o_a = indexer_sparse_attention(q_a, k_a, v_a, q_i, k_i, w_i, pos)

        q_b = (rms_norm_2(c_q, b_q_latent_norm[l]) @ w_uq[l]).reshape(B, S, B_HEADS, B_QK_DIM)
        kv = (rms_norm_2(c_kv, b_kv_latent_norm[l]) @ w_ukv[l]).reshape(B, S, B_HEADS, B_NOPE_DIM + B_V_DIM)
        k_nope, v_b = kv[..., :B_NOPE_DIM], kv[..., B_NOPE_DIM:]
        k_rope_h = jnp.broadcast_to(k_rope[:, :, None, :], (B, S, B_HEADS, B_ROPE_DIM))
        k_b = jnp.concatenate([k_nope, k_rope_h], axis=-1)
        q_b = rms_norm_2(q_b, b_q_norm[l])
        k_b = rms_norm_2(k_b, b_k_norm[l])
        q_b = jnp.concatenate([q_b[..., :B_NOPE_DIM], rope(q_b[..., B_NOPE_DIM:], pos)], axis=-1)
        k_b = jnp.concatenate([k_b[..., :B_NOPE_DIM], rope(k_b[..., B_NOPE_DIM:], pos)], axis=-1)
        o_b = chunk_causal_attention(q_b, k_b, v_b, pos)

        mixed = jnp.concatenate([o_a.reshape(B, S, A_WIDTH) * jax.nn.silu(g_a),
                                 o_b.reshape(B, S, B_WIDTH) * jax.nn.silu(g_b)], axis=-1)
        h = h + mixed @ w_out[l]
    return h


def setup_inputs(seed=0):
    out = dict(first_inputs(seed))
    for name, value in second_inputs(seed + 1).items():
        if name != "x":
            out[name + "_2"] = value
    return out


def reference(
    x, pre_mix_norm, post_mix_norm, pre_ffn_norm, post_ffn_norm, w_ffn_in, w_ffn_out, gdn_w_in,
    gdn_conv, gdn_a_log, gdn_dt_bias, gdn_out_norm, gdn_w_out, kv_norm, w_kv, b_forget, fox_w_q,
    fox_w_o, norm_gain_2, w_in_2, a_q_norm_2, a_k_norm_2, b_q_latent_norm_2, b_kv_latent_norm_2,
    w_uq_2, w_ukv_2, b_q_norm_2, b_k_norm_2, w_out_2,
):
    x = first_block(
        x, pre_mix_norm, post_mix_norm, pre_ffn_norm, post_ffn_norm, w_ffn_in, w_ffn_out,
        gdn_w_in, gdn_conv, gdn_a_log, gdn_dt_bias, gdn_out_norm, gdn_w_out, kv_norm, w_kv,
        b_forget, fox_w_q, fox_w_o,
    )
    return second_block(
        x, norm_gain_2, w_in_2, a_q_norm_2, a_k_norm_2, b_q_latent_norm_2, b_kv_latent_norm_2,
        w_uq_2, w_ukv_2, b_q_norm_2, b_k_norm_2, w_out_2,
    )


_drawn_inputs = setup_inputs


def setup_inputs(seed=0):
    import zlib

    import numpy as np

    out = dict(_drawn_inputs(seed))
    spreads = {}
    factors = {'norm_gain_2': 8.0,
     'a_q_norm_2': 8.0,
     'a_k_norm_2': 8.0,
     'b_q_latent_norm_2': 8.0,
     'b_kv_latent_norm_2': 8.0,
     'w_uq_2': 2.952,
     'b_q_norm_2': 8.0,
     'b_k_norm_2': 8.0}
    for name, (base, spread) in spreads.items():
        noise = np.random.default_rng([zlib.crc32(name.encode()), seed]).standard_normal(out[name].shape)
        drawn = base * np.exp(spread * noise) if base else spread * noise
        out[name] = __import__('jax').numpy.asarray(drawn.astype(out[name].dtype))
    for name, factor in factors.items():
        out[name] = (out[name] * factor).astype(out[name].dtype)
    return out
```

```python
import math
from contextlib import ExitStack

import numpy as np

import concourse.bass as bass
from concourse import mybir

F32 = mybir.dt.float32
F32R = mybir.dt.float32r
ALU = mybir.AluOpType
ACT = mybir.ActivationFunctionType
AX_X = mybir.AxisListType.X

P = 128
D = 1024
SEQ = 512
TT = SEQ // P
KT = D // P
SLOT = 2048
GH, GD = 8, 128
FH, FD = 16, 64
DFF = int(math.ceil(8 * D / 3 / 256) * 256)
FT = DFF // P
AH, AD = 8, 64
TOPK = min(256, SEQ // 4)
BH, BN, BR, BV = 8, 64, 32, 64
BQ = BN + BR
QL, KVL = 384, 256
EPS = 1e-6
NEG = -1e30
MAX_NEG = -3.4028234663852886e38
LEVELS = 6

STAGES = [("qkv", 12), ("z", 4), ("gout", 4), ("fin0", FT), ("fout0", FT // 2), ("fk", 4), ("fv", 4),
          ("fq", 4), ("fo", 4), ("fin1", FT), ("fout1", FT // 2), ("in2", 8), ("uq", 2), ("ukv", 1),
          ("in2b", 8), ("out2", 4)]
BASE = {}
NSLOT = 0
for _name, _count in STAGES:
    BASE[_name] = NSLOT
    NSLOT += _count

CONSTS = [("ident", 128), ("upto", 512), ("strict", 128), ("tril", 128), ("negcausal", 128), ("negchunk", 128),
          ("cosa", 128), ("sina", 128), ("cosb", 64), ("sinb", 64)]
CAT = {}
NCONST = 0
for _name, _count in CONSTS:
    CAT[_name] = (NCONST, _count)
    NCONST += _count
NMASK = LEVELS + 2

IN2_BLOCKS = [(2560, 3016), (3016, 3304), (2048, 2560), (0, 512), (512, 1024), (1024, 1536), (1536, 2048), (3304, 3816)]

KB = 1024
AT_X = 0
AT_WRAW, AT_WHI, AT_WLO = 16 * KB, 32 * KB, 48 * KB
AT_CONST, AT_WS, AT_SMALL = 64 * KB, 70 * KB, 72 * KB
AT_HHI, AT_HLO = 80 * KB, 96 * KB
AT_GAIN = 112 * KB
AT_XN = 120 * KB
AT_JUNK = 128 * KB
AT_ARENA = 132 * KB


def program(nc, x_in, wpack, wba, wf, gains, convw, vecs, consts, masks, out):
    ctx = ExitStack()
    with ctx:
        base = (nc.sbuf_base + 63) // 64 * 64

        def at(name, offset, shape, dt=F32):
            return nc.alloc_sbuf_tensor_at(name, shape, dt, offset=base + offset)

        sems = {}

        def sem(name):
            if name not in sems:
                sems[name] = ctx.enter_context(nc.semaphore(name))
            return sems[name]

        x_sb = at("x_sb", AT_X, [P, TT, D])
        wraw = [at(f"wraw{i}", AT_WRAW + 8 * KB * i, [P, SLOT]) for i in range(2)]
        whi = [at(f"whi{i}", AT_WHI + 8 * KB * i, [P, SLOT], F32R) for i in range(2)]
        wlo = [at(f"wlo{i}", AT_WLO + 8 * KB * i, [P, SLOT], F32R) for i in range(2)]
        csb = at("csb", AT_CONST, [P, NCONST])
        hT_hi = at("hT_hi", AT_HHI, [P, KT, SEQ], F32R)
        hT_lo = at("hT_lo", AT_HLO, [P, KT, SEQ], F32R)
        gain = [at(f"gain{i}", AT_GAIN + 4 * KB * i, [P, D]) for i in range(2)]
        xn = [at(f"xn{i}", AT_XN + 4 * KB * i, [P, D]) for i in range(2)]
        junk = at("junk", AT_JUNK, [P, D])
        small = at("small", AT_SMALL, [P, 2 * KB])
        PS = ctx.enter_context(nc.psum_tensor("PS", [P, 8, 512], F32))

        def const(name):
            a, n = CAT[name]
            return csb[:, a:a + n]

        ident = const("ident")
        ones = const("upto")[:, 128:256]
        small_at = [0]

        def stat(n):
            a = small_at[0]
            small_at[0] += n
            assert small_at[0] <= 2 * KB
            return small[:, a:a + n]

        w_hi, w_lo, w_used = sem("w_hi"), sem("w_lo"), sem("w_used")
        w_loaded = [sem("w_loaded0"), sem("w_loaded1")]

        def act_split(n, static=None, i=0):
            q = n if static is None else static
            act = nc.scalar
            act.wait_ge(w_loaded[q % 2], 16 * (q // 2 + 1) + 16 * i)
            if q >= 2:
                act.wait_ge(w_used, q - 1 + 2 * i)
            act.activation(whi[q % 2][:, :], wraw[q % 2][:, :], ACT.Copy).then_inc(w_hi, 1)

        dve_step, steps = sem("dve_step"), [0]

        def stepped(k=1):
            steps[0] += k
            nc.vector.wait_ge(dve_step, steps[0])

        class Norm:

            def __init__(self, turn, nth, nth_stat, g, x_ready, same=None):
                self.x0, self.s0, self.p0 = TT * nth, TT * nth_stat, 2 * TT * turn
                self.g, self.x_ready, self.same = g, x_ready, same
                self.ss, self.ms, self.rt, self.r = ((stat(TT) for _ in range(4)) if same is None else
                                                     (None, None, None, same.r))
                self.T = Turn(turn, lambda t, k: xn[t % 2][:, k * P:(k + 1) * P],
                              lambda eng, t: eng.wait_ge(sem("norm_xn"), self.x0 + t + 1))

            def act(self):
                if self.same is not None:
                    self.T.act()
                    return
                for t in range(TT):
                    self.x_ready(nc.scalar, t)
                    if t:
                        nc.scalar.wait_ge(sem("norm_ss"), self.s0 + t)
                    nc.scalar.activation(junk[:, :], x_sb[:, t, :], ACT.Square,
                                         accum_out=self.ss[:, t:t + 1]).then_inc(sem("norm_ss"), 1)
                for t in range(TT):
                    nc.scalar.wait_ge(sem("norm_ms"), self.s0 + t + 1)
                    nc.scalar.activation(self.rt[:, t:t + 1], self.ms[:, t:t + 1], ACT.Sqrt).then_inc(sem("norm_rt"), 1)
                self.T.act()

            def dve(self):
                v = nc.vector
                for t in range(TT if self.same is None else 0):
                    v.wait_ge(sem("norm_ss"), self.s0 + t + 1)
                    v.tensor_scalar(self.ms[:, t:t + 1], self.ss[:, t:t + 1], 1.0 / D, EPS, ALU.mult,
                                    ALU.add).then_inc(sem("norm_ms"), 1)
                gain_ready(v, self.g)
                for t in range(TT):
                    if self.same is None:
                        v.wait_ge(sem("norm_rt"), self.s0 + t + 1)
                        v.reciprocal(self.r[:, t:t + 1], self.rt[:, t:t + 1]).then_inc(dve_step, 1)
                        stepped()
                    if t >= 2:
                        v.wait_ge(sem("turn_ps"), self.p0 + 2 * (t - 1))
                    v.scalar_tensor_tensor(out=xn[t % 2][:, :], in0=x_sb[:, t, :], scalar=self.r[:, t:t + 1],
                                           in1=gain[self.g % 2][:, :], op0=ALU.mult,
                                           op1=ALU.mult).then_inc(sem("norm_xn"), 1)
                    if t:
                        self.T.dve(t - 1)
                self.T.dve(TT - 1)

            def pe(self, before=None):
                self.T.pe(before)

        class Turn:

            def __init__(self, nth, src, ready):
                self.n0, self.src, self.ready = 2 * TT * nth, src, ready

            def pe(self, before=None):
                for t in range(TT):
                    self.ready(nc.tensor, t)
                    if before:
                        before(nc.tensor, t)
                    for half in range(2):
                        for k in range(4):
                            last = nc.tensor.transpose(PS[:, 2 * t + half, k * P:(k + 1) * P],
                                                       self.src(t, 4 * half + k), ident)
                        last.then_inc(sem("turn_ps"), 1)

            def act(self):
                for t in range(TT):
                    for half in range(2):
                        nc.scalar.wait_ge(sem("turn_ps"), self.n0 + 2 * t + half + 1)
                        nc.scalar.activation(hT_hi[:, 4 * half:4 * half + 4, t * P:(t + 1) * P],
                                             PS[:, 2 * t + half, :].rearrange("p (k c) -> p k c", k=4),
                                             ACT.Copy).then_inc(sem("turn_hi"), 1)

            def dve(self, t):
                for half in range(2):
                    nc.vector.wait_ge(sem("turn_hi"), self.n0 + 2 * t + half + 1)
                    o = (slice(None), slice(4 * half, 4 * half + 4), slice(t * P, (t + 1) * P))
                    nc.vector.tensor_tensor(hT_lo[o], PS[:, 2 * t + half, :].rearrange("p (k c) -> p k c", k=4),
                                            hT_hi[o].bitcast(F32), ALU.subtract).then_inc(sem("turn_lo"), 1)

            def done(self, eng):
                eng.wait_ge(sem("turn_lo"), self.n0 + 2 * TT)

        def gain_ready(eng, g):
            eng.wait_ge(sem(f"gain{g % 2}_in"), 16 * (g // 2 + 1))

        def gain_load(g, free):
            if free is not None:
                free(nc.sync)
            nc.sync.dma_start(gain[g % 2][:, :], gains[g:g + 1, :].partition_broadcast(P)).then_inc(sem(f"gain{g % 2}_in"), 16)

        class Mix:

            def __init__(self, nth, stage, nslots, g):
                self.n0, self.m0 = TT * nth, (TT - 1) * nth
                self.b, self.ns, self.g = BASE[stage], nslots, g
                self.ss, self.ms, self.rt, self.r = (stat(TT) for _ in range(4))

            def mix_ready(self, eng, t):
                if t < TT - 1:
                    eng.wait_ge(sem("mix_sum"), self.m0 + t + 1)
                else:
                    eng.wait_ge(w_used, self.b + self.ns)

            def pe_slot(self, n, first, final, lhi, llo):
                q = n % 2
                for t in range(TT):
                    for kk in range(2):
                        a, b = first and kk == 0, final and kk == 1
                        for half in range(2):
                            nc.tensor.matmul(PS[:, 2 * t + half, :], lhi(kk, t), whi[q][:, kk * D + half * 512:][:, 0:512],
                                             start=a, stop=False)
                        for half in range(2):
                            nc.tensor.matmul(PS[:, 2 * t + half, :], lhi(kk, t), wlo[q][:, kk * D + half * 512:][:, 0:512],
                                             start=False, stop=False)
                        for half in range(2):
                            last = nc.tensor.matmul(PS[:, 2 * t + half, :], llo(kk, t),
                                                    whi[q][:, kk * D + half * 512:][:, 0:512], start=False, stop=b)
                    if final and t < TT - 1:
                        last.then_inc(sem("mix_sum"), 1)
                last.then_inc(w_used, 1)

            def act(self):
                for t in range(TT):
                    self.mix_ready(nc.scalar, t)
                    if t:
                        nc.scalar.wait_ge(sem("mix_ss"), self.n0 + t)
                    nc.scalar.activation(junk[:, :].rearrange("p (a b) -> p a b", a=2), PS[:, 2 * t:2 * t + 2, :],
                                         ACT.Square, accum_out=self.ss[:, t:t + 1]).then_inc(sem("mix_ss"), 1)
                for t in range(TT):
                    nc.scalar.wait_ge(sem("mix_ms"), self.n0 + t + 1)
                    nc.scalar.activation(self.rt[:, t:t + 1], self.ms[:, t:t + 1], ACT.Sqrt).then_inc(sem("mix_rt"), 1)

            def dve(self):
                v = nc.vector
                for t in range(TT):
                    v.wait_ge(sem("mix_ss"), self.n0 + t + 1)
                    v.tensor_scalar(self.ms[:, t:t + 1], self.ss[:, t:t + 1], 1.0 / D, EPS, ALU.mult,
                                    ALU.add).then_inc(sem("mix_ms"), 1)
                gain_ready(v, self.g)
                for t in range(TT):
                    v.wait_ge(sem("mix_rt"), self.n0 + t + 1)
                    v.reciprocal(self.r[:, t:t + 1], self.rt[:, t:t + 1]).then_inc(dve_step, 1)
                    stepped()
                    v.scalar_tensor_tensor(out=xn[t % 2][:, :].rearrange("p (a b) -> p a b", a=2),
                                           in0=PS[:, 2 * t:2 * t + 2, :], scalar=self.r[:, t:t + 1],
                                           in1=gain[self.g % 2][:, :].rearrange("p (a b) -> p a b", a=2), op0=ALU.mult,
                                           op1=ALU.mult).then_inc(dve_step, 1)
                    stepped()
                    v.tensor_tensor(x_sb[:, t, :], x_sb[:, t, :], xn[t % 2][:, :], ALU.add).then_inc(sem("mix_x"), 1)

            def x_ready(self, eng, t):
                eng.wait_ge(sem("mix_x"), self.n0 + t + 1)

        def x_loaded(eng, t):
            eng.wait_ge(sem("x_in"), 16)

        N0 = Norm(0, 0, 0, 0, x_loaded)
        GOUT = Mix(0, "gout", 4, 1)
        NF0 = Norm(2, 1, 1, 2, GOUT.x_ready)
        FOUT0 = Mix(1, "fout0", FT // 2, 3)
        NKV = Norm(3, 2, 2, 4, FOUT0.x_ready)
        NQ = Norm(4, 3, 0, 5, FOUT0.x_ready, NKV)
        FO = Mix(2, "fo", 4, 6)
        NF1 = Norm(6, 4, 3, 7, FO.x_ready)
        FOUT1 = Mix(3, "fout1", FT // 2, 8)
        N2 = Norm(7, 5, 4, 9, FOUT1.x_ready)

        def feat_slot(q, wait_slot, rhs=None):
            for h in range(2):
                for k in range(KT):
                    w = (slice(None), slice(k * 256 + h * P, k * 256 + (h + 1) * P))
                    o = PS[:, 2 * q + h, :]
                    nc.tensor.matmul(o, whi[q][w], hT_hi[:, k, :], start=(k == 0), stop=False)
                    nc.tensor.matmul(o, whi[q][w], hT_lo[:, k, :], start=False, stop=False)
                    last = nc.tensor.matmul(o, wlo[q][w], hT_hi[:, k, :], start=False, stop=(k == KT - 1))
            last.then_inc(w_used, 1)

        def tok_slot(n, k0, nk, cols, bank0, first, final, hi=None, lo=None):
            hi, lo = hi or hT_hi, lo or hT_lo
            q = n % 2
            for t in range(TT):
                for kk in range(nk):
                    w = (slice(None), slice(kk * cols, (kk + 1) * cols))
                    ts = slice(t * P, (t + 1) * P)
                    o = PS[:, bank0 + t, 0:cols]
                    nc.tensor.matmul(o, hi[:, k0 + kk, ts], whi[q][w], start=(first and kk == 0), stop=False)
                    nc.tensor.matmul(o, hi[:, k0 + kk, ts], wlo[q][w], start=False, stop=False)
                    last = nc.tensor.matmul(o, lo[:, k0 + kk, ts], whi[q][w], start=False,
                                            stop=(final and kk == nk - 1))
            last.then_inc(w_used, 1)

        qkvT = at("qkvT", AT_ARENA, [P, 3 * GH, SEQ])
        zs = at("zs", AT_ARENA + 48 * KB, [P, TT, D])
        LATE = AT_ARENA + 64 * KB
        cvb = [at(f"cvb{i}", LATE + 2112 * i, [P, 3 + SEQ]) for i in range(4)]
        cva = [at(f"cva{i}", LATE + 8448 + 2048 * i, [P, SEQ]) for i in range(2)]
        wsraw = at("wsraw", LATE + 12544, [P, 2 * P])
        wshi = at("wshi", AT_WS, [P, 2 * P], F32R)
        wslo = at("wslo", AT_WS + KB, [P, 2 * P], F32R)
        cw = stat(4 * 3 * GH).rearrange("p (a b) -> p a b", a=4)
        vc = stat(160)
        alog, dtb, bfg, onorm = vc[:, 0:8], vc[:, 8:16], vc[:, 16:32], vc[:, 32:160]

        def pe_qkv_step(i, first):
            for p in range(2):
                nc.tensor.wait_ge(w_lo, BASE["qkv"] + p + 1 + 2 * i)
                if not first:
                    nc.tensor.wait_ge(sem("qkv_raw"), 4 * i + 2 * p - 2)
                feat_slot(p, None)

        def act_qkv_step(i, first):
            for p in range(2):
                nc.scalar.wait_ge(w_used, BASE["qkv"] + p + 1 + 2 * i)
                for h in range(2):
                    if not first:
                        nc.scalar.wait_ge(sem("qkv_conv"), 4 * i + 2 * p + h - 3)
                    nc.scalar.activation(cvb[2 * p + h][:, 3:3 + SEQ], PS[:, 2 * p + h, :],
                                         ACT.Copy).then_inc(sem("qkv_raw"), 1)
                act_split(2 + 2 * i + p, 2 + p, i)
                for h in range(2):
                    nc.scalar.wait_ge(sem("qkv_conv"), 4 * i + 2 * p + h + 1)
                    nc.scalar.activation(qkvT[:, bass.ds(4 * i + 2 * p + h, 1), :].rearrange("p a b -> p (a b)"),
                                         cva[h][:, :], ACT.Silu).then_inc(sem("qkv_silu"), 1)

        def dve_qkv_step(i, first):
            v = nc.vector
            for p in range(2):
                for h in range(2):
                    j = 4 * i + 2 * p + h
                    v.wait_ge(sem("qkv_raw"), j + 1)
                    if not (first and p == 0):
                        v.wait_ge(sem("qkv_silu"), j - 1)
                    src = cvb[2 * p + h]
                    v.tensor_scalar(cva[h][:, :], src[:, 0:SEQ], cw[:, 0, bass.ds(j, 1)], None,
                                    ALU.mult).then_inc(sem("qkv_tap"), 1)
                    for tap in range(1, 4):
                        v.wait_ge(sem("qkv_tap"), 3 * j + tap)
                        v.scalar_tensor_tensor(out=cva[h][:, :], in0=src[:, tap:tap + SEQ],
                                               scalar=cw[:, tap, bass.ds(j, 1)], in1=cva[h][:, :], op0=ALU.mult,
                                               op1=ALU.add).then_inc(sem("qkv_conv" if tap == 3 else "qkv_tap"), 1)

        def pe_z():
            b = BASE["z"]
            for cb in range(2):
                if cb:
                    nc.tensor.wait_ge(sem("qkv_raw"), 3 * GH)
                for m in range(2):
                    nc.tensor.wait_ge(w_lo, b + 2 * cb + m + 1)
                    tok_slot(b + 2 * cb + m, 4 * m, 4, 512, 4 - 4 * cb, m == 0, m == 1)
            nc.tensor.wait_ge(sem("z_silu"), 1)
            small_product(0, 4, "ba_logits")

        def small_product(which, bank, done):
            nc.tensor.wait_ge(sem("ws_lo"), 1)
            for t in range(TT):
                for k in range(KT):
                    w = (slice(None), slice(which * P + k * 16, which * P + (k + 1) * 16))
                    ts = slice(t * P, (t + 1) * P)
                    o = PS[:, bank, t * 16:(t + 1) * 16]
                    nc.tensor.matmul(o, hT_hi[:, k, ts], wshi[w], start=(k == 0), stop=False)
                    nc.tensor.matmul(o, hT_hi[:, k, ts], wslo[w], start=False, stop=False)
                    last = nc.tensor.matmul(o, hT_lo[:, k, ts], wshi[w], start=False, stop=(k == KT - 1))
            last.then_inc(sem(done), 1)

        def act_z():
            b = BASE["z"]
            for cb in range(2):
                act_split(b + 2 * cb + 2)
                nc.scalar.wait_ge(w_used, b + 2 * cb + 2)
                nc.scalar.activation(zs[:, :, cb * 512:(cb + 1) * 512], PS[:, 4 - 4 * cb:8 - 4 * cb, :],
                                     ACT.Silu).then_inc(sem("z_silu"), 1)
                act_split(b + 2 * cb + 3)

        def s32():
            return stat(TT * GH).rearrange("p (t h) -> p t h", t=TT)

        eb, eb1, beta, xa, xm, nab, ee, ln1, spl, g = (s32() for _ in range(10))
        nea = stat(GH)
        ex = stat(3 * 32)
        eG, eR, eL = (ex[:, 32 * i:32 * i + 32].rearrange("p (t h) -> p t h", t=TT) for i in range(3))
        n2s = stat(64)
        rqk_t = stat(64)
        rqk = stat(64)
        rqkv = rqk.rearrange("p (t j) -> p t j", t=TT)
        beG, rqeG, rqs = s32(), s32(), s32()
        gb = PS[:, 4, 0:64].rearrange("p (t j) -> p t j", t=TT)

        def bt(ap, shape):
            return ap.unsqueeze(len(ap.shape)).to_broadcast(shape)

        def rows(ap, n):
            return ap.unsqueeze(1).to_broadcast([P, n, ap.shape[1]])

        gate_a = sem("gate_a")

        def act_gates():
            a = nc.scalar
            a.wait_ge(sem("vec_in"), 32)
            a.activation(nea[:, :], alog, ACT.Exp).then_inc(gate_a, 1)
            a.wait_ge(sem("ba_logits"), 1)
            a.activation(eb[:, :, :], gb[:, :, 0:8], ACT.Exp, scale=-1.0).then_inc(gate_a, 1)
            a.wait_ge(sem("gate_nab"), 1)
            a.activation(ee[:, :, :], nab[:, :, :], ACT.Exp).then_inc(gate_a, 1)
            a.wait_ge(gate_a, 3)
            a.activation(ln1[:, :, :], ee[:, :, :], ACT.Ln, bias=1.0).then_inc(gate_a, 1)
            a.wait_ge(sem("gate_cum"), 1)
            a.activation(ex[:, :], PS[:, 5, 0:96], ACT.Exp).then_inc(gate_a, 1)
            for j in range(2 * GH):
                if j >= 2:
                    a.wait_ge(sem("qk_ss"), j - 1)
                a.wait_ge(sem("qkv_silu"), 3 * GH)
                a.activation(cva[j % 2][:, :], qkvT[:, j, :], ACT.Square).then_inc(sem("qk_sq"), 1)
            a.wait_ge(sem("qk_ms"), 1)
            a.activation(rqk_t[:, :], n2s[:, :], ACT.Sqrt).then_inc(sem("qk_rt"), 1)

        def dve_gates():
            v = nc.vector
            v.wait_ge(gate_a, 2)
            v.tensor_scalar(eb1[:, :, :], eb[:, :, :], 1.0, None, ALU.add).then_inc(dve_step, 1)
            stepped()
            v.reciprocal(beta[:, :, :], eb1[:, :, :]).then_inc(dve_step, 1)
            v.tensor_tensor(xa[:, :, :], gb[:, :, 8:16], rows(dtb, TT), ALU.add).then_inc(dve_step, 1)
            stepped(2)
            v.tensor_scalar(xm[:, :, :], xa[:, :, :], 0.0, None, ALU.max).then_inc(dve_step, 1)
            stepped()
            v.scalar_tensor_tensor(out=nab[:, :, :], in0=xm[:, :, :], scalar=-2.0, in1=xa[:, :, :], op0=ALU.mult,
                                   op1=ALU.add).then_inc(sem("gate_nab"), 1)
            v.wait_ge(gate_a, 4)
            v.tensor_tensor(spl[:, :, :], xm[:, :, :], ln1[:, :, :], ALU.add).then_inc(dve_step, 1)
            stepped()
            v.scalar_tensor_tensor(out=g[:, :, :], in0=spl[:, :, :], scalar=-1.0, in1=rows(nea, TT), op0=ALU.mult,
                                   op1=ALU.mult).then_inc(sem("gate_g"), 1)
            v.wait_ge(sem("qk_ss"), 2 * GH)
            v.tensor_scalar(n2s[:, :], PS[:, 6, 0:64], EPS, None, ALU.add).then_inc(sem("qk_ms"), 1)
            v.wait_ge(sem("qk_rt"), 1)
            v.reciprocal(rqk[:, :], rqk_t[:, :]).then_inc(dve_step, 1)
            stepped()
            v.tensor_scalar(rqs[:, :, :], rqkv[:, :, 0:8], GD ** -0.5, None, ALU.mult).then_inc(dve_step, 1)
            v.wait_ge(gate_a, 5)
            v.tensor_tensor(beG[:, :, :], beta[:, :, :], eG[:, :, :], ALU.mult).then_inc(dve_step, 1)
            stepped()
            v.tensor_tensor(rqeG[:, :, :], rqs[:, :, :], eG[:, :, :], ALU.mult).then_inc(dve_step, 1)
            stepped(2)

        def pe_gates():
            t = nc.tensor
            t.wait_ge(sem("gate_g"), 1)
            g2 = g.rearrange("p t h -> p (t h)")
            t.matmul(PS[:, 5, 0:32], const("upto")[:, 0:P], g2, start=True, stop=True)
            t.matmul(PS[:, 5, 32:64], const("strict"), g2, start=True, stop=True)
            t.matmul(PS[:, 5, 64:96], ones, g2, start=True, stop=True).then_inc(sem("gate_cum"), 1)
            for j in range(2 * GH):
                t.wait_ge(sem("qk_sq"), j + 1)
                for c in range(TT):
                    last = t.matmul(PS[:, 6, c * 16 + j:c * 16 + j + 1], cva[j % 2][:, c * P:(c + 1) * P], ones[:, 0:1],
                                    start=True, stop=True)
                last.then_inc(sem("qk_ss"), 1)

        SC = [AT_HHI + 4 * KB * i for i in range(8)] + [AT_XN, AT_XN + 4 * KB, AT_JUNK] + [LATE + 4 * KB * i for i in range(4)]
        names = ["kn", "bv", "mgP", "E", "A", "Aqk", "AT", "AqkT", "LT0", "LT1", "knT", "X", "XT", "r", "msk"]
        B = {n: at("g_" + n, SC[i], [P, GH, P]) for i, n in enumerate(names)}
        B["S"] = at("g_S", AT_GAIN, [P, GH, P])
        B["LT"] = [B["LT0"], B["LT1"]]
        msk = B["msk"]
        oss, oms, ort, orr = (stat(GH) for _ in range(4))

        def hs(hf):
            return slice(4 * hf, 4 * hf + 4)

        def bank(b):
            return PS[:, b, :].rearrange("p (h c) -> p h c", h=4)

        HB = [P, 4, P]

        def gw(eng, name, c, hf):
            eng.wait_ge(sem("g_" + name), 2 * c + hf + 1)

        def gl(eng, name, c, l, hf):
            eng.wait_ge(sem("g_" + name), 2 * (LEVELS * c + l - 1) + hf + 1)

        def gx(eng, name, c, l, hf):
            eng.wait_ge(sem("g_" + name), 2 * ((LEVELS - 1) * c + l - 1) + hf + 1)

        def g1(eng, name, c, hf):
            if c:
                eng.wait_ge(sem("g_" + name), 2 * (c - 1) + hf + 1)

        def group(name, b, hf, lhsT, rhs, transpose=False):
            for j in range(4):
                h = 4 * hf + j
                o = PS[:, b + hf, j * P:(j + 1) * P]
                if transpose:
                    last = nc.tensor.transpose(o, lhsT(h), ident)
                else:
                    last = nc.tensor.matmul(o, lhsT(h), rhs(h), start=True, stop=True)
            last.then_inc(sem("g_" + name), 1)

        def pe_chunk(c):
            t = nc.tensor
            ct = slice(c * P, (c + 1) * P)
            for hf in range(2):
                if c:
                    gw(t, "vn", c - 1, hf)
                    gl(t, "Pe", c - 1, LEVELS, hf)
                group("TK", 0, hf, lambda h: qkvT[:, GH + h, ct], None, True)
            for hf in range(2):
                if c:
                    g1(t, "oq", c - 1, hf)
                group("TV", 2, hf, lambda h: qkvT[:, 2 * GH + h, ct], None, True)
            for hf in range(2):
                gw(t, "mg", c, hf)
                if c:
                    gw(t, "o2", c - 1, hf)
                t.matmul(PS[:, 4 + hf, :], const("upto")[:, 0:P], B["mgP"][:, hs(hf), :], start=True,
                         stop=True).then_inc(sem("g_D"), 1)
            for hf in range(2):
                gw(t, "kn", c, hf)
                if c:
                    gw(t, "S", c - 1, hf)
                group("TKN", 6, hf, lambda h: B["kn"][:, h, :], None, True)
            for hf in range(2):
                gw(t, "knT", c, hf)
                group("KK", 0, hf, lambda h: B["knT"][:, h, :], lambda h: B["knT"][:, h, :])
                gw(t, "bv", c, hf)
                group("QK", 2, hf, lambda h: qkvT[:, h, ct], lambda h: B["knT"][:, h, :])
            for hf in range(2):
                gw(t, "A", c, hf)
                gw(t, "E", c, hf)
                group("TA", 4, hf, lambda h: B["A"][:, h, :], None, True)
                gw(t, "Aqk", c, hf)
                group("TQ", 6, hf, lambda h: B["Aqk"][:, h, :], None, True)
            for l in range(1, LEVELS + 1):
                for hf in range(2):
                    gl(t, "LT", c, l, hf)
                    if l == 1:
                        gw(t, "X0", c, hf)
                        gw(t, "XT0", c, hf)
                    else:
                        gx(t, "X", c, l - 1, hf)
                        gl(t, "XT", c, l - 1, hf)
                    group("Pm", 0, hf, lambda h: B["LT"][l % 2][:, h, :], lambda h: B["X"][:, h, :])
                for hf in range(2):
                    gl(t, "Pe", c, l, hf)
                    if l < LEVELS:
                        group("Xm", 2, hf, lambda h: B["XT"][:, h, :], lambda h: B["mgP"][:, h, :])
                    group("XTm", 4, hf, lambda h: B["mgP"][:, h, :], lambda h: B["XT"][:, h, :])
            if c:
                for hf in range(2):
                    gw(t, "AqkT", c, hf)
                    gw(t, "S", c - 1, hf)
                    group("KS", 6, hf, lambda h: B["knT"][:, h, :], lambda h: B["S"][:, h, :])
            for hf in range(2):
                g1(t, "r", c, hf)
                gl(t, "XT", c, LEVELS, hf)
                rhs = B["r"] if c else B["bv"]
                group("VN", 0, hf, lambda h: B["XT"][:, h, :], lambda h: rhs[:, h, :])
                if c:
                    group("QS", 2, hf, lambda h: qkvT[:, h, ct], lambda h: B["S"][:, h, :])
            for hf in range(2):
                gw(t, "vn", c, hf)
                gw(t, "AqkT", c, hf)
                group("O2", 4, hf, lambda h: B["AqkT"][:, h, :], lambda h: B["E"][:, h, :])
                if c < TT - 1:
                    gw(t, "kd", c, hf)
                    g1(t, "ks", c, hf)
                    group("SU", 6, hf, lambda h: B["kn"][:, h, :], lambda h: B["E"][:, h, :])

        def act_chunk(c):
            a = nc.scalar
            for hf in range(2):
                gw(a, "D", c, hf)
                if c:
                    gw(a, "SU", c - 1, hf)
                a.activation(B["E"][:, hs(hf), :], bank(4 + hf), ACT.Exp).then_inc(sem("g_E"), 1)
            for hf in range(2):
                gw(a, "TKN", c, hf)
                a.activation(B["knT"][:, hs(hf), :], bank(6 + hf), ACT.Copy).then_inc(sem("g_knT"), 1)
            for hf in range(2):
                gw(a, "TA", c, hf)
                if c:
                    gl(a, "LT", c - 1, LEVELS, hf)
                a.activation(B["AT"][:, hs(hf), :], bank(4 + hf), ACT.Copy).then_inc(sem("g_AT"), 1)
                gw(a, "TQ", c, hf)
                a.activation(B["AqkT"][:, hs(hf), :], bank(6 + hf), ACT.Copy).then_inc(sem("g_AqkT"), 1)
            for l in range(1, LEVELS + 1):
                for hf in range(2):
                    gl(a, "Pm", c, l, hf)
                    a.activation(B["mgP"][:, hs(hf), :], bank(hf), ACT.Copy).then_inc(sem("g_Pe"), 1)
            for hf in range(2):
                gw(a, "VN", c, hf)
                a.activation(B["E"][:, hs(hf), :], bank(hf), ACT.Copy).then_inc(sem("g_vn"), 1)
            g1(a, "o", c, 1) if c else gw(a, "o2", c, 1)
            a.activation(B["A"][:, :, :], B["Aqk"][:, :, :], ACT.Square).then_inc(sem("g_osq"), 1)
            a.wait_ge(sem("g_oms"), c + 1)
            a.activation(ort[:, :], oms[:, :], ACT.Sqrt).then_inc(sem("g_ort"), 1)

        def pool_chunk(c):
            p = nc.gpsimd
            if c == 0:
                p.wait_ge(sem("msk_in"), 16)
                p.wait_ge(sem("gate_g"), 1)
                p.wait_ge(gate_a, 5)
            for hf in range(2):
                if c:
                    gl(p, "XTm", c - 1, LEVELS, hf)
                p.tensor_tensor(B["mgP"][:, hs(hf), :], bt(g[:, c, hs(hf)], HB), rows(const("strict"), 4),
                                ALU.mult).then_inc(sem("g_mg"), 1)
            for hf in range(2):
                gw(p, "E", c, hf)
                p.tensor_tensor(B["E"][:, hs(hf), :], B["E"][:, hs(hf), :], rows(const("tril"), 4),
                                ALU.mult).then_inc(sem("g_M"), 1)
            for l in range(1, LEVELS + 1):
                for hf in range(2):
                    gw(p, "AT", c, hf)
                    if l > 2:
                        gl(p, "Pm", c, l - 2, hf)
                    p.tensor_tensor(B["LT"][l % 2][:, hs(hf), :], B["AT"][:, hs(hf), :], rows(msk[:, l + 1, :], 4),
                                    ALU.mult).then_inc(sem("g_LT"), 1)
                if l == 2:
                    for hf in range(2):
                        gw(p, "TKN", c, hf)
                        p.tensor_tensor(B["kn"][:, hs(hf), :], B["kn"][:, hs(hf), :], bt(eR[:, c, hs(hf)], HB),
                                        ALU.mult).then_inc(sem("g_kd"), 1)
            zc = zs[:, c, :].rearrange("p (h d) -> p h d", h=GH)
            p.wait_ge(sem("z_silu"), 2)
            p.tensor_tensor(zc, zc, rows(onorm, GH), ALU.mult).then_inc(sem("g_gz"), 1)

        def dve_chunk(c):
            v = nc.vector
            for hf in range(2):
                gw(v, "TK", c, hf)
                if c:
                    gw(v, "SU", c - 1, hf)
                v.tensor_tensor(B["kn"][:, hs(hf), :], bank(hf), bt(rqkv[:, c, 8 + 4 * hf:12 + 4 * hf], HB),
                                ALU.mult).then_inc(sem("g_kn"), 1)
            for hf in range(2):
                gw(v, "TV", c, hf)
                v.tensor_tensor(B["bv"][:, hs(hf), :], bank(2 + hf), bt(beta[:, c, hs(hf)], HB),
                                ALU.mult).then_inc(sem("g_bv"), 1)
            for hf in range(2):
                gw(v, "KK", c, hf)
                gw(v, "M", c, hf)
                v.tensor_tensor(B["A"][:, hs(hf), :], bank(hf), B["E"][:, hs(hf), :], ALU.mult).then_inc(dve_step, 1)
                stepped()
                v.tensor_tensor(B["A"][:, hs(hf), :], B["A"][:, hs(hf), :], bt(beta[:, c, hs(hf)], HB),
                                ALU.mult).then_inc(sem("g_A"), 1)
                gw(v, "QK", c, hf)
                v.tensor_tensor(B["Aqk"][:, hs(hf), :], bank(2 + hf), B["E"][:, hs(hf), :],
                                ALU.mult).then_inc(sem("g_Aqk"), 1)
            v.wait_ge(sem("msk_in"), 16)
            for hf in range(2):
                gw(v, "A", c, hf)
                v.tensor_tensor(B["X"][:, hs(hf), :], B["A"][:, hs(hf), :], rows(msk[:, 0, :], 4),
                                ALU.mult).then_inc(dve_step, 1)
                gw(v, "AT", c, hf)
                v.tensor_tensor(B["XT"][:, hs(hf), :], B["AT"][:, hs(hf), :], rows(msk[:, 1, :], 4),
                                ALU.mult).then_inc(dve_step, 1)
                stepped(2)
                v.tensor_tensor(B["X"][:, hs(hf), :], rows(ident, 4), B["X"][:, hs(hf), :],
                                ALU.subtract).then_inc(sem("g_X0"), 1)
                v.tensor_tensor(B["XT"][:, hs(hf), :], rows(ident, 4), B["XT"][:, hs(hf), :],
                                ALU.subtract).then_inc(sem("g_XT0"), 1)
                gw(v, "X0", c, hf)
                gw(v, "XT0", c, hf)
            for l in range(1, LEVELS + 1):
                for hf in range(2):
                    if l < LEVELS:
                        gx(v, "Xm", c, l, hf)
                        v.tensor_tensor(B["X"][:, hs(hf), :], B["X"][:, hs(hf), :], bank(2 + hf),
                                        ALU.subtract).then_inc(sem("g_X"), 1)
                    gl(v, "XTm", c, l, hf)
                    v.tensor_tensor(B["XT"][:, hs(hf), :], B["XT"][:, hs(hf), :], bank(4 + hf),
                                    ALU.subtract).then_inc(sem("g_XT"), 1)
                for hf in range(2):
                    if l < LEVELS:
                        gx(v, "X", c, l, hf)
                    gl(v, "XT", c, l, hf)
            for hf in range(2):
                if c:
                    g1(v, "KS", c, hf)
                    v.tensor_tensor(B["r"][:, hs(hf), :], bank(6 + hf), bt(beG[:, c, hs(hf)], HB),
                                    ALU.mult).then_inc(sem("g_ks"), 1)
                    g1(v, "ks", c, hf)
                    v.tensor_tensor(B["r"][:, hs(hf), :], B["bv"][:, hs(hf), :], B["r"][:, hs(hf), :],
                                    ALU.subtract).then_inc(sem("g_r"), 1)
            for hf in range(2):
                if c:
                    g1(v, "QS", c, hf)
                    v.tensor_tensor(B["A"][:, hs(hf), :], bank(2 + hf), bt(rqeG[:, c, hs(hf)], HB),
                                    ALU.mult).then_inc(sem("g_oq"), 1)
                gw(v, "O2", c, hf)
                v.tensor_tensor(B["Aqk"][:, hs(hf), :], bank(4 + hf), bt(rqs[:, c, hs(hf)], HB),
                                ALU.mult).then_inc(sem("g_o2"), 1)
                gw(v, "o2", c, hf)
                if c:
                    g1(v, "oq", c, hf)
                    v.tensor_tensor(B["Aqk"][:, hs(hf), :], B["Aqk"][:, hs(hf), :], B["A"][:, hs(hf), :],
                                    ALU.add).then_inc(sem("g_o"), 1)
            if c < TT - 1:
                for hf in range(2):
                    gw(v, "SU", c, hf)
                    if c:
                        v.tensor_tensor(B["S"][:, hs(hf), :], B["S"][:, hs(hf), :], bt(eL[:, c, hs(hf)], HB),
                                        ALU.mult).then_inc(dve_step, 1)
                        stepped()
                        v.tensor_tensor(B["S"][:, hs(hf), :], B["S"][:, hs(hf), :], bank(6 + hf),
                                        ALU.add).then_inc(sem("g_S"), 1)
                    else:
                        v.tensor_copy(B["S"][:, hs(hf), :], bank(6 + hf)).then_inc(sem("g_S"), 1)
            v.wait_ge(sem("g_osq"), c + 1)
            v.tensor_reduce(oss[:, :], B["A"][:, :, :], AX_X, ALU.add).then_inc(dve_step, 1)
            stepped()
            v.tensor_scalar(oms[:, :], oss[:, :], 1.0 / GD, EPS, ALU.mult, ALU.add).then_inc(sem("g_oms"), 1)
            v.wait_ge(sem("g_ort"), c + 1)
            v.reciprocal(orr[:, :], ort[:, :]).then_inc(dve_step, 1)
            stepped()
            v.tensor_tensor(B["Aqk"][:, :, :], B["Aqk"][:, :, :], bt(orr[:, :], [P, GH, P]),
                            ALU.mult).then_inc(dve_step, 1)
            stepped()
            v.wait_ge(sem("g_gz"), c + 1)
            zc = zs[:, c, :].rearrange("p (h d) -> p h d", h=GH)
            v.tensor_tensor(zc, zc, B["Aqk"][:, :, :], ALU.mult).then_inc(sem("g_og"), 1)

        GT = Turn(1, lambda t, k: zs[:, t, k * P:(k + 1) * P], lambda eng, t: eng.wait_ge(sem("g_og"), TT))

        act_sb = at("act_sb", AT_ARENA, [P, FT, SEQ])
        ahi = [at(f"ahi{i}", AT_ARENA + 44 * KB + 4 * KB * i, [P, 2, SEQ], F32R) for i in range(2)]
        alo = [at(f"alo{i}", AT_ARENA + 52 * KB + 4 * KB * i, [P, 2, SEQ], F32R) for i in range(2)]
        sil = [at(f"sil{i}", AT_ARENA + 60 * KB + 2 * KB * i, [P, SEQ]) for i in range(2)]
        NP = FT // 2

        class Ffn:
            def __init__(self, l, norm, mix):
                self.l, self.norm, self.mix = l, norm, mix
                self.b, self.c = BASE[f"fin{l}"], BASE[f"fout{l}"]
                self.p0, self.h0 = FT * l, NP * l

            def pe(self):
                t = nc.tensor
                self.norm.T.done(t)

                def step(i, first):
                    for p in range(2):
                        t.wait_ge(w_lo, self.b + p + 1 + 2 * i)
                        if not first:
                            t.wait_ge(sem("ffn_prod"), self.p0 + 2 * i + p - 1)
                        feat_slot((self.b + p) % 2, None)

                step(0, True)
                with t.Fori(1, NP) as i:
                    step(i, False)

                def out(m, static, i=0):
                    t.wait_ge(w_lo, self.c + static + 1 + 2 * i)
                    t.wait_ge(sem("ffn_lo"), self.h0 + static + 1 + 2 * i)
                    q = static % 2
                    self.mix.pe_slot(self.c + static, m == 0, m == NP - 1,
                                     lambda kk, tt: ahi[q][:, kk, tt * P:(tt + 1) * P],
                                     lambda kk, tt: alo[q][:, kk, tt * P:(tt + 1) * P])

                out(0, 0)
                out(1, 1)
                with t.Fori(1, (NP - 1) // 2) as i:
                    out(-1, 0, i)
                    out(-1, 1, i)
                out(NP - 1, NP - 1)

            def hi_of(self, static, i=0):
                if static >= 2:
                    nc.scalar.wait_ge(w_used, self.c + static - 1 + 2 * i)
                nc.scalar.wait_ge(sem("ffn_prod"), self.p0 + FT)
                nc.scalar.activation(ahi[static % 2][:, :, :], act_sb[:, bass.ds(2 * static + 4 * i, 2), :],
                                     ACT.Copy).then_inc(sem("ffn_hi"), 1)

            def act(self):
                a = nc.scalar

                def step(i, first, cut=False):
                    for p in range(2):
                        a.wait_ge(w_used, self.b + p + 1 + 2 * i)
                        if not first:
                            a.wait_ge(sem("ffn_prod"), self.p0 + 2 * i + p - 1)
                        a.activation(sil[p][:, :], PS[:, 2 * ((self.b + p) % 2), :], ACT.Silu).then_inc(sem("ffn_silu"), 1)
                        act_split(None, self.b + p + 2, i)

                step(0, True)
                with a.Fori(1, NP) as i:
                    step(i, False)
                self.hi_of(0)
                self.hi_of(1)
                with a.Fori(0, (NP - 3) // 2) as i:
                    for p in range(2):
                        act_split(None, self.c + 2 + p, i)
                        self.hi_of(2 + p, i)
                act_split(self.c + NP - 1)
                self.hi_of(NP - 1)
                act_split(self.c + NP)
                self.mix.act()
                act_split(self.c + NP + 1)

            def dve(self):
                v = nc.vector

                def step(i):
                    for p in range(2):
                        v.wait_ge(sem("ffn_silu"), self.p0 + 2 * i + p + 1)
                        v.tensor_tensor(act_sb[:, bass.ds(2 * i + p, 1), :].rearrange("p a b -> p (a b)"), sil[p][:, :],
                                        PS[:, 2 * ((self.b + p) % 2) + 1, :], ALU.mult).then_inc(sem("ffn_prod"), 1)

                with v.Fori(0, NP) as i:
                    step(i)

                def low(static, i=0):
                    v.wait_ge(sem("ffn_hi"), self.h0 + static + 1 + 2 * i)
                    v.tensor_tensor(alo[static % 2][:, :, :], act_sb[:, bass.ds(2 * static + 4 * i, 2), :],
                                    ahi[static % 2][:, :, :].bitcast(F32), ALU.subtract).then_inc(sem("ffn_lo"), 1)

                v.wait_ge(sem("ffn_prod"), self.p0 + FT)
                with v.Fori(0, (NP - 1) // 2) as i:
                    low(0, i)
                    low(1, i)
                low(NP - 1)
                self.mix.dve()

        F0 = Ffn(0, NF0, FOUT0)
        F1 = Ffn(1, NF1, FOUT1)

        class Attention:

            def __init__(self, before, heads, q, k, v, mask, out, pbuf, ptbuf, eye=None, after=None, ready=None):
                self.H, self.q, self.k, self.v, self.mask, self.out = heads, q, k, v, mask, out
                self.pbuf, self.ptbuf, self.eye, self.after, self.ready = pbuf, ptbuf, eye, after, ready
                self.units = [(i, h) for i in range(TT) for h in range(heads)]
                self.nm, self.rs, self.ri = stat(4), stat(TT * heads), stat(TT * heads)
                self.nb = heads * 64 // 512
                self.u0 = sum(len(a.units) for a in before)
                self.t0 = TT * len(before)
                self.o0 = sum(TT * a.nb for a in before)

            def obank(self, i):
                return 4 + (i % 2) * self.nb

            def pe_scores(self, u):
                t = nc.tensor
                i, h = self.units[u]
                if self.u0 + u >= 2:
                    t.wait_ge(sem("at_exp"), self.u0 + u - 1)
                if self.ready and h == 0 and i:
                    self.ready(i)
                eye = ident if self.eye is None else self.eye[:, :]
                full, m = self.mask(i)
                b, q = u % 2, self.q(h, i)
                n, d = (i + 1) * P, i * P
                if full:
                    t.matmul(PS[:, b, 0:n].rearrange("p (j c) -> p j c", c=P), q, self.k(h, 0, i + 1), start=True, stop=False)
                    t.matmul(PS[:, b, 0:n], eye, m, start=False, stop=True).then_inc(sem("at_score"), 1)
                else:
                    if i:
                        t.matmul(PS[:, b, 0:d].rearrange("p (j c) -> p j c", c=P), q, self.k(h, 0, i), start=True, stop=True)
                    t.matmul(PS[:, b, d:n], q, self.k(h, i, i + 1), start=True, stop=False)
                    t.matmul(PS[:, b, d:n], eye, m, start=False, stop=True).then_inc(sem("at_score"), 1)

            def pe_turn(self, u):
                t = nc.tensor
                i, h = self.units[u]
                t.wait_ge(sem("at_exp"), self.u0 + u + 1)
                if self.u0 + u >= 2:
                    t.wait_ge(sem("at_pt"), self.u0 + u - 1)
                for j in range(i + 1):
                    last = t.transpose(PS[:, 2 + u % 2, j * P:(j + 1) * P], self.pbuf[u % 2][:, j * P:(j + 1) * P], ident)
                last.then_inc(sem("at_turned"), 1)

            def pe_values(self, u):
                t = nc.tensor
                i, h = self.units[u]
                t.wait_ge(sem("at_pt"), self.u0 + u + 1)
                if h == 0 and self.o0 + i >= 2:
                    t.wait_ge(sem("at_out"), self.o0 + self.nb * (i - 1))
                b, c = self.obank(i) + h // 8, (h % 8) * 64
                for j in range(i + 1):
                    last = t.matmul(PS[:, b, c:c + 64], self.ptbuf[u % 2][:, j * P:(j + 1) * P], self.v(h, j),
                                    start=(j == 0), stop=(j == i))
                last.then_inc(sem("at_pv"), 1)

            def pe(self):
                n = len(self.units)
                for u in range(n + 2):
                    if u < n:
                        self.pe_scores(u)
                    if 1 <= u <= n:
                        self.pe_turn(u - 1)
                    if u >= 2:
                        self.pe_values(u - 2)

            def act(self):
                a = nc.scalar
                for u, (i, h) in enumerate(self.units):
                    a.wait_ge(sem("at_max"), self.u0 + u + 1)
                    if self.u0 + u >= 2:
                        a.wait_ge(sem("at_turned"), self.u0 + u - 1)
                    n = (i + 1) * P
                    a.activation(self.pbuf[u % 2][:, 0:n], PS[:, u % 2, 0:n], ACT.Exp, bias=self.nm[:, u % 4:u % 4 + 1],
                                 accum_out=self.rs[:, u:u + 1]).then_inc(sem("at_exp"), 1)

            def dve_pt(self, u):
                v = nc.vector
                i, h = self.units[u]
                v.wait_ge(sem("at_turned"), self.u0 + u + 1)
                if self.u0 + u >= 2:
                    v.wait_ge(sem("at_pv"), self.u0 + u - 1)
                n = (i + 1) * P
                v.tensor_copy(self.ptbuf[u % 2][:, 0:n], PS[:, 2 + u % 2, 0:n]).then_inc(sem("at_pt"), 1)

            def dve_out(self, i):
                v, H = nc.vector, self.H
                v.wait_ge(sem("at_exp"), self.u0 + (i + 1) * H)
                c = slice(i * H, (i + 1) * H)
                v.reciprocal(self.ri[:, c], self.rs[:, c]).then_inc(dve_step, 1)
                stepped()
                v.wait_ge(sem("at_pv"), self.u0 + (i + 1) * H)
                for b in range(self.nb):
                    r = self.ri[:, i * H + 8 * b:i * H + 8 * b + 8]
                    v.tensor_tensor(self.out(i, b),
                                    PS[:, self.obank(i) + b, :].rearrange("p (a b c) -> p a b c", a=4, b=2),
                                    bt(r.rearrange("p (a b) -> p a b", a=4), [P, 4, 2, 64]),
                                    ALU.mult).then_inc(sem("at_out"), 1)
                if self.after:
                    self.after(i)

            def dve_max(self, u):
                v = nc.vector
                i, h = self.units[u]
                v.wait_ge(sem("at_score"), self.u0 + u + 1)
                v.tensor_reduce(self.nm[:, u % 4:u % 4 + 1], PS[:, u % 2, 0:(i + 1) * P], AX_X, ALU.max,
                                negate=True).then_inc(sem("at_max"), 1)

            def dve(self, hook=None):
                n = len(self.units)
                for u in range(n + 3):
                    if u < n:
                        self.dve_max(u)
                    if 1 <= u <= n:
                        self.dve_pt(u - 1)
                    if u >= 3 and self.units[u - 3][1] == self.H - 1:
                        self.dve_out(self.units[u - 3][0])
                    if hook and u < n:
                        hook(u)

        KA = at("KA", AT_ARENA, [P, FH, SEQ])
        QA = at("QA", AT_ARENA + 32 * KB, [P, FH, SEQ])
        FV = at("FV", AT_ARENA + 64 * KB, [P, TT, D])
        crow = [at(f"crow{i}", AT_ARENA + 80 * KB + 2 * KB * i, [16, SEQ]) for i in range(2)]
        fp = [at(f"fp{i}", AT_ARENA + 80 * KB + 2 * KB * i, [P, SEQ]) for i in range(2)]
        fpt = [at(f"fpt{i}", AT_ARENA + 84 * KB + 2 * KB * i, [P, SEQ]) for i in range(2)]
        fl, fm, fna, fe, fln, lf = (stat(TT * FH).rearrange("p (t h) -> p t h", t=TT) for _ in range(6))
        FOX = Attention([], FH, lambda h, i: QA[0:66, h, i * P:(i + 1) * P],
                        lambda h, a, b: KA[0:66, h, a * P:b * P].rearrange("p (j c) -> p j c", c=P), lambda h, j: FV[:, j, h * FD:(h + 1) * FD],
                        lambda i: (False, const("negcausal")),
                        lambda i, b: QA[:, 4 * b:4 * b + 4, i * P:(i + 1) * P].rearrange("p a (b c) -> p a b c", b=2),
                        fp, fpt)
        FT_ = Turn(5, lambda t, k: QA[:, k, t * P:(t + 1) * P], lambda eng, t: eng.wait_ge(sem("at_out"), 2 * TT))

        def pe_heads(stage):
            b = BASE[stage]
            h0 = 8 if stage == "fq" else 0
            for m in range(4):
                nc.tensor.wait_ge(w_lo, b + m + 1)
                if m >= 2:
                    nc.tensor.wait_ge(sem("heads_a"), h0 + 2 * (m - 1))
                    nc.tensor.wait_ge(sem("heads_v"), h0 + 2 * (m - 1))
                feat_slot((b + m) % 2, None)

        def act_heads(stage, dst, scale):
            b = BASE[stage]
            for m in range(4):
                act_split(b + m + 2)
                for r in range(2):
                    nc.scalar.activation(dst[0:64, 4 * m + r, :], PS[64 * r:64 * r + 64, 2 * ((b + m) % 2), :], ACT.Copy,
                                         scale=scale).then_inc(sem("heads_a"), 1)

        def dve_heads(stage, dst, scale):
            b = BASE[stage]
            for m in range(4):
                nc.vector.wait_ge(w_used, b + m + 1)
                for r in range(2):
                    nc.vector.tensor_scalar(dst[0:64, 4 * m + 2 + r, :], PS[64 * r:64 * r + 64, 2 * ((b + m) % 2) + 1, :],
                                            scale, None, ALU.mult).then_inc(sem("heads_v"), 1)

        def foxproj_free(eng, t):
            eng.wait_ge(sem("fv"), 2)
            eng.wait_ge(sem("c_rows"), 2)

        def pe_foxproj():
            t = nc.tensor
            NKV.pe()
            NKV.T.done(t)
            pe_heads("fk")
            b = BASE["fv"]
            for cb in range(2):
                if cb:
                    t.wait_ge(sem("heads_a"), 8)
                    t.wait_ge(sem("heads_v"), 8)
                for m in range(2):
                    t.wait_ge(w_lo, b + 2 * cb + m + 1)
                    tok_slot(b + 2 * cb + m, 4 * m, 4, 512, 4 - 4 * cb, m == 0, m == 1)
            t.wait_ge(sem("fv"), 1)
            small_product(1, 4, "f_logits")
            t.wait_ge(sem("lf"), 1)
            for j in range(TT):
                last = t.matmul(PS[0:16, 5, j * P:SEQ], lf[:, j, :], const("upto")[:, 0:SEQ - j * P], start=(j == 0),
                                stop=(j == TT - 1), skip_group_check=True)
            last.then_inc(sem("c_sum"), 1)
            NQ.pe(foxproj_free)
            NQ.T.done(t)
            pe_heads("fq")

        def act_foxproj():
            a = nc.scalar
            NKV.act()
            act_heads("fk", KA, 1.0)
            b = BASE["fv"]
            for cb in range(2):
                act_split(b + 2 * cb + 2)
                a.wait_ge(w_used, b + 2 * cb + 2)
                a.activation(FV[:, :, cb * 512:(cb + 1) * 512], PS[:, 4 - 4 * cb:8 - 4 * cb, :],
                             ACT.Copy).then_inc(sem("fv"), 1)
                act_split(b + 2 * cb + 3)
            a.wait_ge(sem("fna"), 1)
            a.activation(fe[:, :, :], fna[:, :, :], ACT.Exp).then_inc(gate_a, 1)
            a.wait_ge(gate_a, 6)
            a.activation(fln[:, :, :], fe[:, :, :], ACT.Ln, bias=1.0).then_inc(gate_a, 1)
            a.wait_ge(sem("c_sum"), 1)
            a.activation(crow[0][:, :], PS[0:16, 5, :], ACT.Copy).then_inc(sem("c_rows"), 1)
            a.activation(crow[1][:, :], PS[0:16, 5, :], ACT.Copy, scale=-1.0).then_inc(sem("c_rows"), 1)
            NQ.act()
            act_heads("fq", QA, FD ** -0.5)

        def dve_foxproj():
            v = nc.vector
            NKV.dve()
            dve_heads("fk", KA, 1.0)
            v.memset(KA[64:66, :, :], 1.0).then_inc(sem("rows1"), 1)
            v.memset(QA[64:66, :, :], 1.0).then_inc(sem("rows1"), 1)
            v.wait_ge(sem("f_logits"), 1)
            v.tensor_tensor(fl[:, :, :], PS[:, 4, 0:64].rearrange("p (t h) -> p t h", t=TT), rows(bfg, TT),
                            ALU.add).then_inc(dve_step, 1)
            stepped()
            v.tensor_scalar(fm[:, :, :], fl[:, :, :], 0.0, None, ALU.min).then_inc(dve_step, 1)
            stepped()
            v.scalar_tensor_tensor(out=fna[:, :, :], in0=fm[:, :, :], scalar=2.0, in1=fl[:, :, :], op0=ALU.mult,
                                   op1=ALU.subtract).then_inc(sem("fna"), 1)
            v.wait_ge(gate_a, 7)
            v.tensor_tensor(lf[:, :, :], fm[:, :, :], fln[:, :, :], ALU.subtract).then_inc(sem("lf"), 1)
            NQ.dve()
            dve_heads("fq", QA, FD ** -0.5)

        def pe_fox():
            nc.tensor.wait_ge(sem("heads_a"), 16)
            nc.tensor.wait_ge(sem("heads_v"), 16)
            nc.tensor.wait_ge(sem("crows_in"), 32)
            FOX.pe()
            FT_.pe()
            FT_.done(nc.tensor)

        def pe_rows(mix, stage):
            for m in range(4):
                nc.tensor.wait_ge(w_lo, BASE[stage] + m + 1)
                mix.pe_slot(BASE[stage] + m, m == 0, m == 3, lambda kk, tt: hT_hi[:, 2 * m + kk, tt * P:(tt + 1) * P],
                            lambda kk, tt: hT_lo[:, 2 * m + kk, tt * P:(tt + 1) * P])

        def act_rows(mix, stage):
            for m in range(3):
                act_split(BASE[stage] + m + 2)
            mix.act()
            act_split(BASE[stage] + 5)

        STEPS = ["cq", "ckv", "qi", "Tcq", "Tckv", "qa", "uq0", "uq1", "ukv0", "ukv1", "ka", "va", "Tqi", "ga", "Tqa",
                 "gb", "Tki", "Tqb0", "Tqb1", "Tkb0", "Tkb1", "Tka"]
        PREPS = ["cq", "ckv", "lcq", "lckv", "qi", "qa", "qb0", "qb1", "kb", "ka"]
        BLK = ["cq", "ckv", "qi", "qa", "ka", "va", "ga", "gb"]
        COLS = {n: c1 - c0 for n, (c0, c1) in zip(BLK, IN2_BLOCKS)}
        SLOT_OF = {n: (BASE["in2"] if j < 4 else BASE["in2b"] - 8) + 2 * j for j, n in enumerate(BLK)}
        HEADS4 = [P, TT, AH, AD]

        qa, ka, qi, va = (at(n, AT_ARENA + 8 * KB * i, [P, TT, AH, AD]) for i, n in enumerate(("qa", "ka", "qi", "va")))
        cqb = at("cqb", AT_ARENA + 24 * KB, [P, TT, COLS["cq"]])
        ckvb = at("ckvb", AT_ARENA + 32 * KB, [P, TT, COLS["ckv"]])
        gz = at("gz", AT_ARENA + 32 * KB, [P, TT, D])
        tmp_a = at("tmp_a", AT_ARENA + 37 * KB, [P, 2048])
        tmp_b = at("tmp_b", AT_XN, [P, 3072])
        vlat = at("vlat", AT_ARENA + 45 * KB, [P, QL + KVL])
        qb = at("qb", AT_ARENA + 48 * KB, [P, TT, BH, P])
        kb = at("kb", AT_ARENA + 64 * KB, [P, TT, BH, P])
        vb = at("vb", AT_ARENA + 80 * KB, [P, TT, BH, BV])
        vh = at("vh", AT_ARENA + 88 * KB, [P, 2 * AD + 2 * BQ])
        krb = at("krb", AT_ARENA + 88 * KB + 1536, [P, TT, BR])
        kir = at("kir", AT_WS, [P, TT, P])
        lat_hi = at("lat_hi", AT_GAIN, [P, 5, SEQ], F32R)
        lat_lo = at("lat_lo", AT_GAIN + 10 * KB, [P, 5, SEQ], F32R)
        pbuf = [at(f"pbuf{i}", AT_GAIN + 2 * KB * i, [P, SEQ]) for i in range(2)]
        ptbuf = [at(f"ptbuf{i}", AT_GAIN + 4 * KB + 2 * KB * i, [P, SEQ]) for i in range(2)]
        obuf = [at(f"obuf{i}", AT_XN + 2 * KB * i, [P, 512]) for i in range(2)]
        identr = at("identr", AT_XN + 4 * KB, [P, P], F32R)
        chunkr = at("chunkr", AT_XN + 4 * KB + 512, [P, P], F32R)
        score = [at(f"score{i}", AT_HLO + 2 * KB * i, [P, SEQ]) for i in range(3)]
        topm = [at(f"topm{i}", AT_HLO + 6 * KB + 2 * KB * i, [P, SEQ], F32R) for i in range(3)]
        rbuf = [at(f"rbuf{i}", AT_HLO + 12 * KB + 2 * KB * i, [P, SEQ]) for i in range(2)]
        wi = stat(TT * AH).rearrange("p (t h) -> p t h", t=TT)
        rms_s, rms_m, rms_t, rms_r = (stat(TT * BH) for _ in range(4))
        top8 = stat(8)
        evacs = {n: (2 if n in ("ukv0", "ukv1") else 1) for n in STEPS}

        def evac_done(eng, name):
            eng.wait_ge(sem("st_evac"), sum(evacs[n] for n in STEPS[:STEPS.index(name) + 1]))

        def prep_done(eng, name):
            eng.wait_ge(sem("prep"), PREPS.index(name) + 1)

        TURNS = [n for n in STEPS if n[0] == "T"]

        def group_of(name):
            return 4 * (STEPS.index(name) % 2)

        def pe_step(name):
            t, g = nc.tensor, group_of(name)
            s = STEPS.index(name)
            if s >= 2:
                evac_done(t, STEPS[s - 2])
                if STEPS[s - 2] in ("Tcq", "Tckv"):
                    prep_done(t, "l" + STEPS[s - 2][1:])
            if name in BLK:
                n = SLOT_OF[name]
                for m in range(2):
                    t.wait_ge(w_lo, n + m + 1)
                    tok_slot(n + m, 4 * m, 4, COLS[name], g, m == 0, m == 1)
            elif name in ("uq0", "uq1"):
                n = BASE["uq"] + int(name[2])
                prep_done(t, "lcq")
                t.wait_ge(w_lo, n + 1)
                tok_slot(n, 0, QL // P, 384, g, True, True, lat_hi, lat_lo)
            elif name in ("ukv0", "ukv1"):
                half, q = int(name[3]), BASE["ukv"] % 2
                prep_done(t, "lckv")
                t.wait_ge(w_lo, BASE["ukv"] + 1)
                for tt in range(TT):
                    for kk in range(2):
                        w = (slice(None), slice(kk * D + 512 * half, kk * D + 512 * half + 512))
                        ts = slice(tt * P, (tt + 1) * P)
                        o = PS[:, g + tt, :]
                        t.matmul(o, lat_hi[:, 3 + kk, ts], whi[q][w], start=(kk == 0), stop=False)
                        t.matmul(o, lat_hi[:, 3 + kk, ts], wlo[q][w], start=False, stop=False)
                        last = t.matmul(o, lat_lo[:, 3 + kk, ts], whi[q][w], start=False, stop=(kk == 1))
                last.then_inc(w_used if half else sem("kv_half"), 1)
            else:
                prep_done(t, {"Tki": "qi"}.get(name, name[1:].rstrip("01") if name[1] == "k" else name[1:]))
                if name in ("Tcq", "Tckv"):
                    src, first, nk = (cqb, 72, 3) if name == "Tcq" else (ckvb, 0, 2)
                    for k in range(nk):
                        for tt in range(TT):
                            last = t.transpose(PS[:, g + k, tt * P:(tt + 1) * P],
                                               src[:, tt, first + k * P:first + (k + 1) * P], ident)
                elif name == "Tki":
                    for tt in range(TT):
                        last = t.transpose(PS[:, g, tt * P:(tt + 1) * P], kir[:, tt, :], ident)
                elif name in ("Tqi", "Tqa", "Tka"):
                    src = {"Tqi": qi, "Tqa": qa, "Tka": ka}[name].rearrange("p t h c -> p t (h c)")
                    for tt in range(TT):
                        for k in range(4):
                            last = t.transpose(PS[:, g + tt, k * P:(k + 1) * P], src[:, tt, k * P:(k + 1) * P], ident)
                else:
                    src, q = {"q": qb, "k": kb}[name[1]], int(name[3])
                    for tt in range(TT):
                        for j in range(4):
                            last = t.transpose(PS[0:BQ, g + tt, j * P:(j + 1) * P], src[:, tt, 4 * q + j, 0:BQ], ident)
                last.then_inc(sem("turned"), 1)

        def act_step(name):
            a, g = nc.scalar, group_of(name)
            bank4 = PS[:, g:g + 4, :]

            def evac(o, i, func=ACT.Copy, scale=1.0):
                a.activation(o, i, func, scale=scale).then_inc(sem("st_evac"), 1)

            if name in BLK:
                n = SLOT_OF[name]
                act_split(n + 2)
                a.wait_ge(w_used, n + 2)
                i = PS[:, g:g + 4, 0:COLS[name]]
                if name in ("va", "ga"):
                    prep_done(a, "qi" if name == "va" else "qb1")
                if name in ("ga", "gb"):
                    c = 512 * (name == "gb")
                    evac(gz[:, :, c:c + 512], i, ACT.Silu)
                elif name in ("cq", "ckv"):
                    evac({"cq": cqb, "ckv": ckvb}[name][:, :, :], i)
                else:
                    evac({"qi": qi, "qa": qa, "ka": ka, "va": va}[name].rearrange("p t h c -> p t (h c)"), i)
                act_split(n + 3)
            elif name in ("uq0", "uq1"):
                n, q = BASE["uq"] + int(name[2]), int(name[2])
                act_split(n + 2)
                evac(qb[:, :, 4 * q:4 * q + 4, 0:BQ], PS[:, g:g + 4, 0:384].rearrange("p t (h c) -> p t h c", h=4))
            elif name in ("ukv0", "ukv1"):
                q = int(name[3])
                if q:
                    act_split(BASE["ukv"] + 2)
                else:
                    a.wait_ge(sem("kv_half"), 1)
                i = bank4.rearrange("p t (h c) -> p t h c", h=4)
                evac(kb[:, :, 4 * q:4 * q + 4, 0:BN], i[:, :, :, 0:BN])
                evac(vb[:, :, 4 * q:4 * q + 4, :], i[:, :, :, BN:P])
            else:
                a.wait_ge(sem("turned"), TURNS.index(name) + 1)
                if name in ("Tcq", "Tckv"):
                    k0, nk = (0, 3) if name == "Tcq" else (3, 2)
                    evac(lat_hi[:, k0:k0 + nk, :], PS[:, g:g + nk, :])
                elif name == "Tki":
                    evac(kir.rearrange("p t c -> p (t c)"), PS[:, g, :])
                elif name in ("Tqi", "Tqa", "Tka"):
                    evac({"Tqi": qi, "Tqa": qa, "Tka": ka}[name].rearrange("p t h c -> p t (h c)"), bank4,
                         scale=AD ** -0.5 if name == "Tqa" else 1.0)
                else:
                    q = int(name[3])
                    evac({"q": qb, "k": kb}[name[1]][0:BQ, :, 4 * q:4 * q + 4, :].rearrange("p t h c -> p t (h c)"),
                         PS[0:BQ, g:g + 4, :], scale=BQ ** -0.5 if name[1] == "q" else 1.0)

        RMS = ["cq", "ckv", "qa", "qb0", "qb1", "kb", "ka"]

        def act_rt(name, n):
            nc.scalar.wait_ge(sem("rms_ms"), RMS.index(name) + 1)
            nc.scalar.activation(rms_t[:, 0:n], rms_m[:, 0:n], ACT.Sqrt).then_inc(sem("rms_rt"), 1)

        def dve_rms(name, x, tmp, gain_row, last=None):
            v = nc.vector
            _, nt, nh, w = x.shape
            n = nt * nh
            sq = tmp[:, 0:n * w].rearrange("p (t h c) -> p t h c", t=nt, h=nh)
            v.tensor_tensor(sq, x, x, ALU.mult).then_inc(dve_step, 1)
            stepped()
            v.tensor_reduce(rms_s[:, 0:n].rearrange("p (t h) -> p t h", t=nt), sq, AX_X, ALU.add).then_inc(dve_step, 1)
            stepped()
            v.tensor_scalar(rms_m[:, 0:n], rms_s[:, 0:n], 1.0 / w, EPS, ALU.mult, ALU.add).then_inc(sem("rms_ms"), 1)
            v.wait_ge(sem("rms_rt"), RMS.index(name) + 1)
            v.reciprocal(rms_r[:, 0:n], rms_t[:, 0:n]).then_inc(dve_step, 1)
            stepped()
            r = rms_r[:, 0:n].rearrange("p (t h) -> p t h", t=nt).unsqueeze(3).to_broadcast([P, nt, nh, w])
            v.tensor_tensor(x, x, r, ALU.mult).then_inc(dve_step, 1)
            stepped()
            o = v.tensor_tensor(x, x, gain_row.unsqueeze(1).unsqueeze(1).to_broadcast([P, nt, nh, w]), ALU.mult)
            o.then_inc(sem("prep") if last else dve_step, 1)
            if not last:
                stepped()

        def dve_rope(x, half, table, tmp, last):
            v = nc.vector
            _, nt, nh, _ = x.shape
            shape = [P, nt, nh, half]
            n = nt * nh * half
            cos, sin = (const(s + table).rearrange("p (t c) -> p t c", t=TT).unsqueeze(2).to_broadcast(shape)
                        for s in ("cos", "sin"))
            x1, x2 = x[:, :, :, 0:half], x[:, :, :, half:2 * half]
            a, b = (tmp[:, n * i:n * i + n].rearrange("p (t h c) -> p t h c", t=nt, h=nh) for i in range(2))
            v.tensor_tensor(a, x1, sin, ALU.mult).then_inc(dve_step, 1)
            v.tensor_tensor(b, x2, sin, ALU.mult).then_inc(dve_step, 1)
            v.tensor_tensor(x1, x1, cos, ALU.mult).then_inc(dve_step, 1)
            v.tensor_tensor(x2, x2, cos, ALU.mult).then_inc(dve_step, 1)
            stepped(4)
            v.tensor_tensor(x1, x1, b, ALU.subtract).then_inc(dve_step, 1)
            v.tensor_tensor(x2, x2, a, ALU.add).then_inc(sem("prep") if last else dve_step, 1)
            stepped(1 if last else 2)

        def dve_prep(name):
            v = nc.vector
            if PREPS.index(name):
                prep_done(v, PREPS[PREPS.index(name) - 1])
            if name == "cq":
                evac_done(v, "cq")
                v.wait_ge(sem("vec2_in"), 48)
                dve_rms("cq", cqb[:, :, 72:72 + QL].unsqueeze(2), tmp_a, vlat[:, 0:QL], True)
            elif name == "ckv":
                evac_done(v, "ckv")
                dve_rms("ckv", ckvb[:, :, 0:KVL].unsqueeze(2), tmp_a, vlat[:, QL:], True)
            elif name in ("lcq", "lckv"):
                k0, nk = (0, 3) if name == "lcq" else (3, 2)
                g = group_of("T" + name[1:])
                evac_done(v, "T" + name[1:])
                v.tensor_tensor(lat_lo[:, k0:k0 + nk, :], PS[:, g:g + nk, :], lat_hi[:, k0:k0 + nk, :].bitcast(F32),
                                ALU.subtract).then_inc(sem("prep"), 1)
            elif name == "qi":
                v.tensor_copy(wi, cqb[:, :, 64:72]).then_inc(dve_step, 1)
                v.tensor_copy(krb[:, :, :], ckvb[:, :, KVL:KVL + BR]).then_inc(dve_step, 1)
                v.tensor_copy(kir[:, :, 0:64], cqb[:, :, 0:64]).then_inc(dve_step, 1)
                stepped(3)
                dve_rope(kir[:, :, 0:64].unsqueeze(2), 16, "b", tmp_a, False)
                v.tensor_copy(kir[:, :, 64:128], kir[:, :, 0:64]).then_inc(dve_step, 1)
                stepped()
                evac_done(v, "qi")
                dve_rope(qi[:, :, :, :], 16, "b", tmp_a, True)
            elif name in ("qa", "ka"):
                x, tmp, c = {"qa": (qa, tmp_a, 0), "ka": (ka, tmp_b, AD)}[name]
                evac_done(v, name)
                dve_rms(name, x[:, :, :, :], tmp, vh[:, c:c + AD])
                dve_rope(x[:, :, :, :], 32, "a", tmp, True)
            elif name in ("qb0", "qb1"):
                q = int(name[2])
                evac_done(v, "uq" + name[2])
                x = qb[:, :, 4 * q:4 * q + 4, 0:BQ]
                dve_rms(name, x, tmp_a, vh[:, 2 * AD:2 * AD + BQ])
                dve_rope(x[:, :, :, BN:BQ], 16, "b", tmp_a, True)
            else:
                evac_done(v, "ukv1")
                v.tensor_copy(kb[:, :, :, BN:BQ], krb[:, :, :].unsqueeze(2).to_broadcast([P, TT, BH, BR])).then_inc(dve_step, 1)
                stepped()
                dve_rms("kb", kb[:, :, :, 0:BQ], tmp_b, vh[:, 2 * AD + BQ:])
                dve_rope(kb[:, :, :, BN:BQ], 16, "b", tmp_b, True)

        IDX = [(i, h) for i in range(1, TT) for h in range(AH)]

        def pe_index():
            t = nc.tensor
            evac_done(t, STEPS[-1])
            for u, (i, h) in enumerate(IDX):
                if u >= 4:
                    t.wait_ge(sem("idx_relu"), u - 3)
                r = slice(64 * (h % 2), 64 * (h % 2) + 64)
                t.matmul(PS[:, 4 + u % 4, 0:(i + 1) * P], qi.rearrange("p t h c -> p t (h c)")[r, i, (h // 2) * P:(h // 2 + 1) * P],
                         kir.rearrange("p t c -> p (t c)")[r, 0:(i + 1) * P], start=True, stop=True).then_inc(sem("idx_dot"), 1)

        def act_index():
            a = nc.scalar
            for u, (i, h) in enumerate(IDX):
                a.wait_ge(sem("idx_dot"), u + 1)
                if u >= 2:
                    a.wait_ge(sem("idx_sum"), u - 1)
                n = (i + 1) * P
                a.activation(rbuf[u % 2][:, 0:n], PS[:, 4 + u % 4, 0:n], ACT.Relu).then_inc(sem("idx_relu"), 1)

        def dve_index():
            v = nc.vector
            v.wait_ge(w_used, BASE["out2"])
            v.tensor_copy(identr[:, :], ident).then_inc(sem("mask"), 1)
            v.tensor_copy(chunkr[:, :], const("negchunk")).then_inc(sem("mask"), 1)
            for u, (i, h) in enumerate(IDX):
                v.wait_ge(sem("idx_relu"), u + 1)
                n = (i + 1) * P
                s, w = score[i - 1][:, 0:n], wi[:, i, h:h + 1]
                if h == 0:
                    v.tensor_scalar(s, rbuf[u % 2][:, 0:n], w, None, ALU.mult).then_inc(sem("idx_sum"), 1)
                else:
                    v.wait_ge(sem("idx_sum"), u)
                    v.scalar_tensor_tensor(out=s, in0=rbuf[u % 2][:, 0:n], scalar=w, in1=s, op0=ALU.mult,
                                           op1=ALU.add).then_inc(sem("idx_sum"), 1)
                if h == AH - 1:
                    v.wait_ge(sem("idx_sum"), u + 1)
                    v.tensor_scalar(s, s, (AH * AD) ** -0.5, None, ALU.mult).then_inc(dve_step, 1)
                    stepped()
                    v.memset(score[i - 1][0:64, n - 64:n], NEG).then_inc(dve_step, 1)
                    stepped()

        ROUNDS = TOPK // 8

        def top_find(r):
            i = r // ROUNDS
            nc.vector.max(top8[:, :], score[i][:, 0:(i + 2) * P]).then_inc(dve_step, 1)

        def top_mark(r):
            v, i = nc.vector, r // ROUNDS
            s = score[i][:, 0:(i + 2) * P]
            stepped()
            v.match_replace(s, top8[:, :], s, MAX_NEG).then_inc(dve_step, 1)
            stepped()
            if r % ROUNDS == ROUNDS - 1:
                v.tensor_scalar(topm[i][:, 0:(i + 2) * P], s, MAX_NEG, NEG, ALU.not_equal, ALU.mult).then_inc(sem("mask"), 1)

        def mask_a(i):
            return (True, topm[i - 1][:, 0:(i + 1) * P]) if i else (False, chunkr[:, :])

        def after_out(side, count):
            def after(i):
                nc.vector.wait_ge(sem("at_out"), count + i + 1)
                c = 512 * side
                nc.vector.tensor_tensor(gz[:, i, c:c + 512], gz[:, i, c:c + 512], obuf[i % 2][:, :], ALU.mult).then_inc(sem("gated"), 1)
            return after

        def out_view(i, b):
            return obuf[i % 2][:, :].rearrange("p (a b c) -> p a b c", a=4, b=2)

        qaT, kaT = (x.rearrange("p t h c -> p t (h c)") for x in (qa, ka))

        def half_of(h):
            return slice(64 * (h % 2), 64 * (h % 2) + 64), slice((h // 2) * P, (h // 2 + 1) * P)

        MLA = Attention([FOX], BH, lambda h, i: qb[0:BQ, i, h, :], lambda h, a, b: kb[0:BQ, a:b, h, :],
                        lambda h, j: vb[:, j, h, :], lambda i: (False, chunkr[:, :]), out_view, pbuf, ptbuf,
                        eye=identr, after=after_out(1, 8))
        SPA = Attention([FOX, MLA], AH, lambda h, i: qaT[half_of(h)[0], i, half_of(h)[1]],
                        lambda h, a, b: kaT[half_of(h)[0], a:b, half_of(h)[1]],
                        lambda h, j: va[:, j, h, :], mask_a, out_view, pbuf, ptbuf, eye=identr, after=after_out(0, 12),
                        ready=lambda i: nc.tensor.wait_ge(sem("mask"), 2 + i))
        T2 = Turn(8, lambda t, k: gz[:, t, k * P:(k + 1) * P], lambda eng, t: eng.wait_ge(sem("gated"), 2 * TT))
        OUT = Mix(4, "out2", 4, None)

        def top_hook(u):
            for r in range(3 * u // 2, 3 * (u + 1) // 2):
                top_find(r)
                top_mark(r)

        def pe_second():
            N2.pe()
            N2.T.done(nc.tensor)
            for name in STEPS:
                pe_step(name)
            pe_index()
            nc.tensor.wait_ge(sem("mask"), 2)
            MLA.pe()
            SPA.pe()
            T2.pe()
            T2.done(nc.tensor)
            pe_rows(OUT, "out2")

        def act_second():
            N2.act()
            rt_after = {"cq": ("cq", TT), "ckv": ("ckv", TT), "uq0": ("qa", 32), "uq1": ("qb0", 16), "ukv1": ("qb1", 16),
                        "ka": ("kb", 32), "va": ("ka", 32)}
            for name in STEPS:
                act_step(name)
                if name in rt_after:
                    act_rt(*rt_after[name])
            act_index()
            MLA.act()
            SPA.act()
            T2.act()
            for n in range(2):
                act_split(BASE["out2"] + 2 + n)

        def dve_second():
            v = nc.vector
            N2.dve()
            for name in PREPS:
                dve_prep(name)
            dve_index()
            MLA.dve(top_hook)
            SPA.dve()
            for t in range(TT):
                T2.dve(t)
            for t in range(TT):
                OUT.mix_ready(v, t)
                x2 = x_sb[:, t, :].rearrange("p (a b) -> p a b", a=2)
                v.tensor_tensor(x2, x2, PS[:, 2 * t:2 * t + 2, :], ALU.add).then_inc(sem("out_x"), 1)

        def sp_second(load):
            s = nc.sync
            s.wait_ge(sem("at_out"), 2 * TT)
            s.wait_ge(sem("mix_x"), 4 * TT)
            s.dma_start(vlat[:, :], vecs[0:1, 288:928].partition_broadcast(P)).then_inc(sem("vec2_in"), 16)
            s.dma_start(vh[:, 0:2 * AD], vecs[0:1, 160:288].partition_broadcast(P)).then_inc(sem("vec2_in"), 16)
            s.dma_start(vh[:, 2 * AD:], vecs[0:1, 928:1120].partition_broadcast(P)).then_inc(sem("vec2_in"), 16)
            load(BASE["in2"] + 2, NSLOT)
            for t in range(TT):
                s.wait_ge(sem("out_x"), t + 1)
                s.dma_start(out[0, t * P:(t + 1) * P, :], x_sb[:, t, :]).then_inc(sem("out_done"), 16)
            s.wait_ge(sem("out_done"), 16 * TT)

        block = ctx.enter_context(nc.Block())

        @block.tensor
        def _(t):
            t.wait_ge(sem("const_in"), 16)
            N0.pe()
            N0.T.done(t)
            pe_qkv_step(0, True)
            with t.Fori(1, 6) as i:
                pe_qkv_step(i, False)
            pe_z()
            pe_gates()
            for c in range(TT):
                pe_chunk(c)
            t.wait_ge(sem("g_o2"), 2 * TT)
            GT.pe()
            GT.done(t)
            pe_rows(GOUT, "gout")
            NF0.pe()
            F0.pe()
            pe_foxproj()
            pe_fox()
            pe_rows(FO, "fo")
            NF1.pe()
            F1.pe()
            pe_second()

        @block.scalar
        def _(a):
            a.wait_ge(sem("const_in"), 16)
            act_split(0)
            act_split(1)
            a.wait_ge(sem("ws_in"), 32)
            a.activation(wshi[:, :], wsraw[:, :], ACT.Copy).then_inc(sem("ws_hi"), 1)
            N0.act()
            act_qkv_step(0, True)
            with a.Fori(1, 6) as i:
                act_qkv_step(i, False)
            act_z()
            act_gates()
            for c in range(TT):
                act_chunk(c)
            GT.act()
            act_rows(GOUT, "gout")
            NF0.act()
            F0.act()
            act_foxproj()
            FOX.act()
            FT_.act()
            act_rows(FO, "fo")
            NF1.act()
            F1.act()
            act_second()

        @block.vector
        def _(v):
            for i in range(4):
                v.memset(cvb[i][:, 0:3], 0.0).then_inc(dve_step, 1)
            stepped(4)
            N0.dve()
            v.wait_ge(sem("vec_in"), 32)
            dve_qkv_step(0, True)
            with v.Fori(1, 6) as i:
                dve_qkv_step(i, False)
            dve_gates()
            for c in range(TT):
                dve_chunk(c)
            for t in range(TT):
                GT.dve(t)
            GOUT.dve()
            NF0.dve()
            F0.dve()
            dve_foxproj()
            FOX.dve()
            for t in range(TT):
                FT_.dve(t)
            FO.dve()
            NF1.dve()
            F1.dve()
            dve_second()

        def pool_low(n0, n1):
            p = nc.gpsimd

            def low(n, q):
                p.wait_ge(w_hi, n + 1)
                p.tensor_tensor(wlo[q][:, :], wraw[q][:, :], whi[q][:, :].bitcast(F32),
                                ALU.subtract).then_inc(w_lo, 1)

            if n0 % 2:
                low(n0, 1)
                n0 += 1
            if n1 - n0 >= 2:
                with p.Fori(0, (n1 - n0) // 2) as i:
                    low(n0 + 2 * i, 0)
                    low(n0 + 2 * i + 1, 1)
            if (n1 - n0) % 2:
                low(n1 - 1, 0)

        @block.gpsimd
        def _(p):
            pool_low(0, 2)
            p.wait_ge(sem("ws_hi"), 1)
            p.tensor_tensor(wslo[:, :], wsraw[:, :], wshi[:, :].bitcast(F32), ALU.subtract).then_inc(sem("ws_lo"), 1)
            pool_low(2, BASE["gout"] + 2)
            for c in range(TT):
                pool_chunk(c)
            pool_low(BASE["gout"] + 2, NSLOT)

        @block.sync
        def _(s):
            def load(n0, n1):

                def one(n, q, i=0):
                    if n >= 2:
                        s.wait_ge(w_lo, n - 1 + 2 * i)
                    s.dma_start(wraw[q][:, :], wpack[bass.ds(n + 2 * i, 1), :, :].rearrange("a p c -> (a p) c")).then_inc(w_loaded[q], 16)

                if n0 < 2:
                    one(0, 0)
                    one(1, 1)
                    n0 = 2
                if n0 % 2:
                    one(n0, 1)
                    n0 += 1
                if n1 - n0 >= 2:
                    with s.Fori(0, (n1 - n0) // 2) as i:
                        one(n0, 0, i)
                        one(n0 + 1, 1, i)
                if (n1 - n0) % 2:
                    one(n1 - 1, 0)

            s.dma_start(csb[:, :], consts).then_inc(sem("const_in"), 16)
            s.dma_start(x_sb[:, :, :], x_in[0].rearrange("(t p) d -> p t d", p=P)).then_inc(sem("x_in"), 16)
            gain_load(0, None)
            s.dma_start(wraw[0][:, :], wpack[0]).then_inc(w_loaded[0], 16)
            s.dma_start(wraw[1][:, :], wpack[1]).then_inc(w_loaded[1], 16)
            s.dma_start(wsraw[:, 0:P], wba).then_inc(sem("ws_in"), 16)
            s.dma_start(wsraw[:, P:2 * P], wf).then_inc(sem("ws_in"), 16)
            s.dma_start(cw, convw).then_inc(sem("vec_in"), 16)
            s.dma_start(vc[:, :], vecs[0:1, 0:160].partition_broadcast(P)).then_inc(sem("vec_in"), 16)
            gain_load(1, None)
            load(2, BASE["gout"] + 2)
            s.wait_ge(sem("qk_ss"), 2 * GH)
            s.dma_start(msk[:, :, :], masks).then_inc(sem("msk_in"), 16)
            load(BASE["gout"] + 2, BASE["gout"] + 4)
            gain_load(2, lambda e: e.wait_ge(sem("g_og"), TT))
            load(BASE["gout"] + 4, BASE["fout0"])
            gain_load(3, lambda e: GOUT.x_ready(e, TT - 1))
            load(BASE["fout0"], BASE["fk"] + 2)
            gain_load(4, lambda e: NF0.T.done(e))
            gain_load(5, lambda e: FOUT0.x_ready(e, TT - 1))
            load(BASE["fk"] + 2, BASE["fo"])
            s.wait_ge(sem("c_rows"), 2)
            s.wait_ge(sem("rows1"), 2)
            s.dma_start(KA[64:65, :, :], crow[1][:, :]).then_inc(sem("crows_in"), 16)
            s.dma_start(QA[65:66, :, :], crow[0][:, :]).then_inc(sem("crows_in"), 16)
            load(BASE["fo"], BASE["fo"] + 4)
            gain_load(6, lambda e: NKV.T.done(e))
            gain_load(7, lambda e: NQ.T.done(e))
            load(BASE["fo"] + 4, BASE["fout1"])
            gain_load(8, lambda e: FO.x_ready(e, TT - 1))
            gain_load(9, lambda e: NF1.T.done(e))
            load(BASE["fout1"], BASE["in2"] + 2)
            sp_second(load)


def constants():
    i = np.arange(P)
    row, col = i[:, None], i[None, :]
    f = np.float32
    upto = np.ones((P, SEQ), f)
    upto[:, :P] = row <= col
    parts = {"ident": row == col, "upto": upto, "strict": row > col, "tril": row >= col,
             "negcausal": np.where(row >= col, 0.0, NEG), "negchunk": np.where((row // 64) >= (col // 64), 0.0, NEG)}
    pos = np.arange(SEQ).astype(f)
    for name, d in (("a", 64), ("b", 32)):
        freqs = np.power(f(10000.0), -np.arange(d // 2, dtype=f) * f(2.0) / f(d)).astype(f)
        ang = (pos[:, None] * freqs[None, :]).astype(f).reshape(TT, P, d // 2).transpose(1, 0, 2).reshape(P, -1)
        parts["cos" + name], parts["sin" + name] = np.cos(ang), np.sin(ang)
    table = np.concatenate([np.asarray(parts[n], f) for n, _ in CONSTS], axis=1)
    masks = []
    for l in range(LEVELS + 1):
        s = 1 << l
        m = ((row // (2 * s)) == (col // (2 * s))) & ((row // s) % 2 == 1) & ((col // s) % 2 == 0)
        if l == 0:
            masks.append(m)
        masks.append(m.T)
    return np.ascontiguousarray(table), np.ascontiguousarray(np.stack(masks, 1).astype(f))


def pack(inputs):
    n = {k: np.asarray(v) for k, v in inputs.items()}
    slots = []

    def add(a):
        a = a.reshape(P, -1)
        if a.shape[1] < SLOT:
            a = np.concatenate([a, np.zeros((P, SLOT - a.shape[1]), a.dtype)], axis=1)
        slots.append(a)

    def tiles(w, k0, nk, c0, c1):
        return w[k0 * P:(k0 + nk) * P, c0:c1].reshape(nk, P, c1 - c0).transpose(1, 0, 2)

    def by_features(w, c0, c1):
        for c in range(c0, c1, 256):
            add(tiles(w, 0, KT, c, c + 256))

    def by_tokens(w, blocks, nk=4):
        for c0, c1 in blocks:
            for k0 in range(0, KT, nk):
                add(tiles(w, k0, nk, c0, c1))

    def by_rows(w):
        for k0 in range(0, w.shape[0] // P, 2):
            add(tiles(w, k0, 2, 0, D))

    gin, kv = n["gdn_w_in"][0], n["w_kv"]
    by_features(gin, 0, 3072)
    by_tokens(gin, [(3072, 3584), (3584, 4096)])
    by_rows(n["gdn_w_out"][0])
    for l in range(2):
        if l == 1:
            by_features(kv, 0, D)
            by_tokens(kv, [(D, D + 512), (D + 512, 2 * D)])
            by_features(n["fox_w_q"][0], 0, D)
            by_rows(n["fox_w_o"][0])
        w = n["w_ffn_in"][l]
        for j in range(FT):
            g, u = tiles(w, 0, KT, j * P, (j + 1) * P), tiles(w, 0, KT, DFF + j * P, DFF + (j + 1) * P)
            add(np.concatenate([g, u], axis=2))
        by_rows(n["w_ffn_out"][l])
    by_tokens(n["w_in_2"][0], IN2_BLOCKS[:4])
    for h in range(2):
        add(tiles(n["w_uq_2"][0], 0, QL // P, 384 * h, 384 * (h + 1)))
    add(tiles(n["w_ukv_2"][0], 0, KVL // P, 0, D))
    by_tokens(n["w_in_2"][0], IN2_BLOCKS[4:])
    by_rows(n["w_out_2"][0])
    small = [tiles(w, 0, KT, c, c + 16).reshape(P, -1) for w, c in ((gin, 4096), (kv, 2 * D))]
    gains = np.stack([n["pre_mix_norm"][0], n["post_mix_norm"][0], n["pre_ffn_norm"][0], n["post_ffn_norm"][0],
                      n["kv_norm"], n["pre_mix_norm"][1], n["post_mix_norm"][1], n["pre_ffn_norm"][1],
                      n["post_ffn_norm"][1], n["norm_gain_2"][0]])
    convw = n["gdn_conv"][0].reshape(4, 3 * GH, P).transpose(2, 0, 1)
    vecs = np.concatenate([n["gdn_a_log"][0], n["gdn_dt_bias"][0], n["b_forget"], n["gdn_out_norm"][0],
                           n["a_q_norm_2"][0], n["a_k_norm_2"][0], n["b_q_latent_norm_2"][0],
                           n["b_kv_latent_norm_2"][0], n["b_q_norm_2"][0], n["b_k_norm_2"][0]])[None]
    assert len(slots) == NSLOT
    return {"wpack": np.stack(slots), "wba": small[0], "wf": small[1], "gains": gains,
            "convw": convw, "vecs": vecs}


def kernel(**inputs):
    import concourse.bacc as bacc
    from concourse.bass_utils import run_bass_kernel_spmd

    arrays = {"x": np.asarray(inputs["x"]), **pack(inputs)}
    arrays["consts"], arrays["masks"] = constants()
    arrays = {k: np.ascontiguousarray(v) for k, v in arrays.items()}
    nc = bacc.Bacc("TRN2", target_bir_lowering=False, num_devices=1, dynamic_dma_scratch_size=1024)
    aps = [nc.dram_tensor(k, a.shape, mybir.dt.from_np(a.dtype), kind="ExternalInput").ap() for k, a in arrays.items()]
    aps.append(nc.dram_tensor("out", (1, SEQ, D), F32, kind="ExternalOutput").ap())
    program(nc, *aps)
    return run_bass_kernel_spmd(nc, [arrays], core_ids=[0]).results[0]["out"]
```

```python
import math
from contextlib import ExitStack

import numpy as np

import concourse.bass as bass
from concourse import mybir

F32 = mybir.dt.float32
F32R = mybir.dt.float32r
ALU = mybir.AluOpType
ACT = mybir.ActivationFunctionType
AX_X = mybir.AxisListType.X

P = 128
D = 1024
SEQ = 512
TT = SEQ // P
KT = D // P
SLOT = 2048
GH, GD = 8, 128
FH, FD = 16, 64
DFF = int(math.ceil(8 * D / 3 / 256) * 256)
FT = DFF // P
AH, AD = 8, 64
TOPK = min(256, SEQ // 4)
BH, BN, BR, BV = 8, 64, 32, 64
BQ = BN + BR
QL, KVL = 384, 256
EPS = 1e-6
NEG = -1e30
MAX_NEG = -3.4028234663852886e38
LEVELS = 6

STAGES = [("qkv", 12), ("z", 4), ("gout", 4), ("fin0", FT), ("fout0", FT // 2), ("fk", 4), ("fv", 4),
          ("fq", 4), ("fo", 4), ("fin1", FT), ("fout1", FT // 2), ("in2", 8), ("uq", 2), ("ukv", 1),
          ("in2b", 8), ("out2", 4)]
BASE = {}
NSLOT = 0
for _name, _count in STAGES:
    BASE[_name] = NSLOT
    NSLOT += _count

CONSTS = [("ident", 128), ("upto", 512), ("strict", 128), ("tril", 128), ("negcausal", 128), ("negchunk", 128),
          ("cosa", 128), ("sina", 128), ("cosb", 64), ("sinb", 64)]
CAT = {}
NCONST = 0
for _name, _count in CONSTS:
    CAT[_name] = (NCONST, _count)
    NCONST += _count

IN2_BLOCKS = [(2048, 2560), (2560, 3016), (3016, 3304), (0, 512), (512, 1024), (1024, 1536), (1536, 2048), (3304, 3816)]

WIDTH = {BASE["in2"] + 2 * _j + _m: 4 * (IN2_BLOCKS[_j][1] - IN2_BLOCKS[_j][0]) for _j in range(4) for _m in range(2)}
WIDTH.update({BASE["uq"] + _m: QL // P * 384 for _m in range(2)})

KB = 1024
AT_X = 0
AT_WRAW, AT_WHI, AT_WLO = 16 * KB, 32 * KB, 48 * KB
AT_CONST, AT_WS, AT_SMALL = 64 * KB, 70 * KB, 72 * KB
AT_HHI, AT_HLO = 80 * KB, 96 * KB
AT_GAIN = 112 * KB
AT_XN = 120 * KB
AT_JUNK = 128 * KB
AT_ARENA = 132 * KB


def program(nc, x_in, wpack, wba, wf, gains, convw, vecs, consts, masks, out):
    ctx = ExitStack()
    with ctx:
        base = (nc.sbuf_base + 63) // 64 * 64

        def at(name, offset, shape, dt=F32):
            return nc.alloc_sbuf_tensor_at(name, shape, dt, offset=base + offset)

        sems = {}

        def sem(name):
            if name not in sems:
                sems[name] = ctx.enter_context(nc.semaphore(name))
            return sems[name]

        x_sb = at("x_sb", AT_X, [P, TT, D])
        wraw = [at(f"wraw{i}", AT_WRAW + 8 * KB * i, [P, SLOT]) for i in range(2)]
        whi = [at(f"whi{i}", AT_WHI + 8 * KB * i, [P, SLOT], F32R) for i in range(2)]
        wlo = [at(f"wlo{i}", AT_WLO + 8 * KB * i, [P, SLOT], F32R) for i in range(2)]
        csb = at("csb", AT_CONST, [P, NCONST])
        hT_hi = at("hT_hi", AT_HHI, [P, KT, SEQ], F32R)
        hT_lo = at("hT_lo", AT_HLO, [P, KT, SEQ], F32R)
        gain = [at(f"gain{i}", AT_GAIN + 4 * KB * i, [P, D]) for i in range(2)]
        xn = [at(f"xn{i}", AT_XN + 4 * KB * i, [P, D]) for i in range(2)]
        junk = at("junk", AT_JUNK, [P, D])
        small = at("small", AT_SMALL, [P, 2 * KB])
        PS = ctx.enter_context(nc.psum_tensor("PS", [P, 8, 512], F32))

        def const(name):
            a, n = CAT[name]
            return csb[:, a:a + n]

        ident = const("ident")
        ones = const("upto")[:, 128:256]
        small_at = [0]

        def stat(n):
            a = small_at[0]
            small_at[0] += n
            assert small_at[0] <= 2 * KB
            return small[:, a:a + n]

        w_hi, w_lo, w_used = sem("w_hi"), sem("w_lo"), sem("w_used")
        w_loaded = [sem("w_loaded0"), sem("w_loaded1")]

        def act_split(n, static=None, i=0):
            q = n if static is None else static
            act = nc.scalar
            act.wait_ge(w_loaded[q % 2], 16 * (q // 2 + 1) + 16 * i)
            if q >= 2:
                act.wait_ge(w_used, q - 1 + 2 * i)
            w = slice(0, WIDTH.get(q, SLOT) if static is None else SLOT)
            act.activation(whi[q % 2][:, w], wraw[q % 2][:, w], ACT.Copy).then_inc(w_hi, 1)

        dve_step, steps = sem("dve_step"), [0]

        def stepped(k=1):
            steps[0] += k
            nc.vector.wait_ge(dve_step, steps[0])

        mixed = at("mixed", AT_ARENA + 84 * KB, [P, D])
        squares = []

        def square(src, dst, total, signal):
            if squares:
                nc.scalar.wait_ge(sem(squares[-1]), squares.count(squares[-1]))
            nc.scalar.activation(dst, src, ACT.Square, accum_out=total).then_inc(sem(signal), 1)
            squares.append(signal)

        class Norm:

            def __init__(self, turn, nth, nth_stat, g, x_ready, same=None):
                self.x0, self.s0, self.p0 = TT * nth, TT * nth_stat, 2 * TT * turn
                self.g, self.x_ready, self.same = g, x_ready, same
                self.ss, self.ms, self.rt, self.r = ((stat(TT) for _ in range(4)) if same is None else
                                                     (None, None, None, same.r))
                self.T = Turn(turn, lambda t, k: xn[t % 2][:, k * P:(k + 1) * P],
                              lambda eng, t: eng.wait_ge(sem("norm_xn"), self.x0 + t + 1))

            def act_sq(self, t):
                self.x_ready(nc.scalar, t)
                square(x_sb[:, t, :], junk[:, :], self.ss[:, t:t + 1], "norm_ss")

            def act_rt(self, t):
                nc.scalar.wait_ge(sem("norm_ms"), self.s0 + t + 1)
                nc.scalar.activation(self.rt[:, t:t + 1], self.ms[:, t:t + 1], ACT.Sqrt).then_inc(sem("norm_rt"), 1)

            def dve_xn(self, t):
                v = nc.vector
                if self.same is None:
                    v.wait_ge(sem("norm_ss"), self.s0 + t + 1)
                    v.tensor_scalar(self.ms[:, t:t + 1], self.ss[:, t:t + 1], 1.0 / D, EPS, ALU.mult,
                                    ALU.add).then_inc(sem("norm_ms"), 1)
                    v.wait_ge(sem("norm_rt"), self.s0 + t + 1)
                    v.reciprocal(self.r[:, t:t + 1], self.rt[:, t:t + 1]).then_inc(dve_step, 1)
                    stepped()
                if t == 0:
                    gain_ready(v, self.g)
                if t >= 2:
                    v.wait_ge(sem("turn_ps"), self.p0 + 2 * (t - 1))
                v.scalar_tensor_tensor(out=xn[t % 2][:, :], in0=x_sb[:, t, :], scalar=self.r[:, t:t + 1],
                                       in1=gain[self.g % 2][:, :], op0=ALU.mult,
                                       op1=ALU.mult).then_inc(sem("norm_xn"), 1)

            def act_first(self):
                for t in range(TT):
                    self.act_sq(t)
                    self.act_rt(t)
                    if t:
                        if t <= 2:
                            act_split(t - 1)
                        self.T.act_tile(t - 1)
                self.T.act_tile(TT - 1)
                nc.scalar.wait_ge(sem("ws_in"), 32)
                nc.scalar.activation(wshi[:, :], wsraw[:, :], ACT.Copy).then_inc(sem("ws_hi"), 1)

            def dve(self):
                for t in range(TT + 1):
                    if t < TT:
                        self.dve_xn(t)
                    if t:
                        self.T.dve(t - 1)

            def pe_head(self, n, before=None, between=None):
                t, T = nc.tensor, self.T
                for c in range(0, TT, 2):
                    T.pe_tile(c, before)
                    T.pe_tile(c + 1, before)
                    T.tile_done(t, c + 1)
                    for m in range(2):
                        t.wait_ge(w_lo, n + m + 1)
                        feat_tile(n + m, c)
                    if between and c == 0:
                        between()

        class Turn:

            def __init__(self, nth, src, ready):
                self.n0, self.src, self.ready = 2 * TT * nth, src, ready

            def pe_tile(self, t, before=None):
                self.ready(nc.tensor, t)
                if before:
                    before(nc.tensor, t)
                for half in range(2):
                    for k in range(4):
                        last = nc.tensor.transpose(PS[:, 2 * t + half, k * P:(k + 1) * P],
                                                   self.src(t, 4 * half + k), ident)
                    last.then_inc(sem("turn_ps"), 1)

            def pe(self):
                for t in range(TT):
                    self.pe_tile(t)

            def act_tile(self, t):
                for half in range(2):
                    nc.scalar.wait_ge(sem("turn_ps"), self.n0 + 2 * t + half + 1)
                    nc.scalar.activation(hT_hi[:, 4 * half:4 * half + 4, t * P:(t + 1) * P],
                                         PS[:, 2 * t + half, :].rearrange("p (k c) -> p k c", k=4),
                                         ACT.Copy).then_inc(sem("turn_hi"), 1)

            def act(self):
                for t in range(TT):
                    self.act_tile(t)

            def dve(self, t):
                for half in range(2):
                    nc.vector.wait_ge(sem("turn_hi"), self.n0 + 2 * t + half + 1)
                    o = (slice(None), slice(4 * half, 4 * half + 4), slice(t * P, (t + 1) * P))
                    nc.vector.tensor_tensor(hT_lo[o], PS[:, 2 * t + half, :].rearrange("p (k c) -> p k c", k=4),
                                            hT_hi[o].bitcast(F32), ALU.subtract).then_inc(sem("turn_lo"), 1)

            def tile_done(self, eng, t):
                eng.wait_ge(sem("turn_lo"), self.n0 + 2 * t + 2)

            def done(self, eng):
                eng.wait_ge(sem("turn_lo"), self.n0 + 2 * TT)

        def gain_ready(eng, g):
            eng.wait_ge(sem(f"gain{g % 2}_in"), 16 * (g // 2 + 1))

        def gain_load(g, free):
            if free is not None:
                free(nc.sync)
            nc.sync.dma_start(gain[g % 2][:, :], gains[g:g + 1, :].partition_broadcast(P)).then_inc(sem(f"gain{g % 2}_in"), 16)

        class Mix:

            def __init__(self, nth, stage, nslots, g):
                self.n0, self.m0 = TT * nth, (TT - 1) * nth
                self.b, self.ns, self.g = BASE[stage], nslots, g
                self.ss, self.ms, self.rt, self.r = (stat(TT) for _ in range(4))

            def mix_ready(self, eng, t):
                if t < TT - 1:
                    eng.wait_ge(sem("mix_sum"), self.m0 + t + 1)
                else:
                    eng.wait_ge(w_used, self.b + self.ns)

            def pe_slot(self, n, first, final, lhi, llo, ready=None, tiles=range(TT)):
                q = n % 2
                for t in tiles:
                    if ready:
                        ready(t)
                    for kk in range(2):
                        a, b = first and kk == 0, final and kk == 1
                        for half in range(2):
                            nc.tensor.matmul(PS[:, 2 * t + half, :], lhi(kk, t), whi[q][:, kk * D + half * 512:][:, 0:512],
                                             start=a, stop=False)
                        for half in range(2):
                            nc.tensor.matmul(PS[:, 2 * t + half, :], lhi(kk, t), wlo[q][:, kk * D + half * 512:][:, 0:512],
                                             start=False, stop=False)
                        for half in range(2):
                            last = nc.tensor.matmul(PS[:, 2 * t + half, :], llo(kk, t),
                                                    whi[q][:, kk * D + half * 512:][:, 0:512], start=False, stop=b)
                    if final and t < TT - 1:
                        last.then_inc(sem("mix_sum"), 1)
                    if t == tiles[-1] and TT - 1 in tiles:
                        last.then_inc(w_used, 1)

            def pe_last(self, slot):
                for m, t in ((0, 0), (0, 1), (1, 0), (0, 2), (1, 1), (0, 3), (1, 2), (1, 3)):
                    slot(m, [t])

            def act_sq(self, t):
                self.mix_ready(nc.scalar, t)
                square(PS[:, 2 * t:2 * t + 2, :], junk[:, :].rearrange("p (a b) -> p a b", a=2), self.ss[:, t:t + 1], "mix_ss")

            def act_rt(self, t):
                nc.scalar.wait_ge(sem("mix_ms"), self.n0 + t + 1)
                nc.scalar.activation(self.rt[:, t:t + 1], self.ms[:, t:t + 1], ACT.Sqrt).then_inc(sem("mix_rt"), 1)

            def dve_x(self, t):
                v = nc.vector
                v.wait_ge(sem("mix_ss"), self.n0 + t + 1)
                v.tensor_scalar(self.ms[:, t:t + 1], self.ss[:, t:t + 1], 1.0 / D, EPS, ALU.mult,
                                ALU.add).then_inc(sem("mix_ms"), 1)
                v.wait_ge(sem("mix_rt"), self.n0 + t + 1)
                v.reciprocal(self.r[:, t:t + 1], self.rt[:, t:t + 1]).then_inc(dve_step, 1)
                stepped()
                if t == 0:
                    gain_ready(v, self.g)
                v.scalar_tensor_tensor(out=mixed[:, :].rearrange("p (a b) -> p a b", a=2),
                                       in0=PS[:, 2 * t:2 * t + 2, :], scalar=self.r[:, t:t + 1],
                                       in1=gain[self.g % 2][:, :].rearrange("p (a b) -> p a b", a=2), op0=ALU.mult,
                                       op1=ALU.mult).then_inc(dve_step, 1)
                stepped()
                v.tensor_tensor(x_sb[:, t, :], x_sb[:, t, :], mixed[:, :], ALU.add).then_inc(sem("mix_x"), 1)
                v.wait_ge(sem("mix_x"), self.n0 + t + 1)

            def x_ready(self, eng, t):
                eng.wait_ge(sem("mix_x"), self.n0 + t + 1)

        CHAIN = ["M0", "N0", "M1", "R", "N1", "S", "T0", "T1", "M2", "M3", "N2", "N3", "T2", "T3"]

        def act_chain(mix, norm, split):
            for kind, *t in CHAIN:
                if kind in "RS":
                    act_split(split - (kind == "R"))
                elif kind == "T":
                    norm.T.act_tile(int(t[0]))
                else:
                    m = mix if kind == "M" else norm
                    m.act_sq(int(t[0]))
                    m.act_rt(int(t[0]))

        def dve_chain(mix, norm):
            step = {"M": mix.dve_x, "N": norm.dve_xn, "T": norm.T.dve}
            for kind, *t in CHAIN:
                if kind not in "RS":
                    step[kind](int(t[0]))

        def x_loaded(eng, t):
            eng.wait_ge(sem(f"x_in{t}"), 16)

        N0 = Norm(0, 0, 0, 0, x_loaded)
        GOUT = Mix(0, "gout", 4, 1)
        NF0 = Norm(2, 1, 1, 2, GOUT.x_ready)
        FOUT0 = Mix(1, "fout0", FT // 2, 3)
        NKV = Norm(3, 2, 2, 4, FOUT0.x_ready)
        NQ = Norm(4, 3, 0, 5, FOUT0.x_ready, NKV)
        FO = Mix(2, "fo", 4, 6)
        NF1 = Norm(6, 4, 3, 7, FO.x_ready)
        FOUT1 = Mix(3, "fout1", FT // 2, 8)
        N2 = Norm(7, 5, 4, 9, FOUT1.x_ready)

        def feat_slot(q):
            for h in range(2):
                for k in range(KT):
                    w = (slice(None), slice(k * 256 + h * P, k * 256 + (h + 1) * P))
                    o = PS[:, 2 * q + h, :]
                    nc.tensor.matmul(o, whi[q][w], hT_hi[:, k, :], start=(k == 0), stop=False)
                    nc.tensor.matmul(o, whi[q][w], hT_lo[:, k, :], start=False, stop=False)
                    last = nc.tensor.matmul(o, wlo[q][w], hT_hi[:, k, :], start=False, stop=(k == KT - 1))
            last.then_inc(w_used, 1)

        def feat_tile(n, t):
            q, ts = n % 2, slice(t * P, (t + 2) * P)
            for h in range(2):
                for k in range(KT):
                    w = (slice(None), slice(k * 256 + h * P, k * 256 + (h + 1) * P))
                    o = PS[:, 2 * q + h, ts]
                    nc.tensor.matmul(o, whi[q][w], hT_hi[:, k, ts], start=(k == 0), stop=False)
                    nc.tensor.matmul(o, whi[q][w], hT_lo[:, k, ts], start=False, stop=False)
                    last = nc.tensor.matmul(o, wlo[q][w], hT_hi[:, k, ts], start=False, stop=(k == KT - 1))
            if t == TT - 2:
                last.then_inc(w_used, 1)

        def tok_slot(n, k0, nk, cols, bank0, first, final, hi=None, lo=None, tiles=range(TT)):
            hi, lo = hi or hT_hi, lo or hT_lo
            q = n % 2
            for t in tiles:
                for kk in range(nk):
                    w = (slice(None), slice(kk * cols, (kk + 1) * cols))
                    ts = slice(t * P, (t + 1) * P)
                    o = PS[:, bank0 + t, 0:cols]
                    nc.tensor.matmul(o, hi[:, k0 + kk, ts], whi[q][w], start=(first and kk == 0), stop=False)
                    nc.tensor.matmul(o, hi[:, k0 + kk, ts], wlo[q][w], start=False, stop=False)
                    last = nc.tensor.matmul(o, lo[:, k0 + kk, ts], whi[q][w], start=False,
                                            stop=(final and kk == nk - 1))
            if tiles[-1] == TT - 1:
                last.then_inc(w_used, 1)

        qkvT = at("qkvT", AT_ARENA, [P, 3 * GH, SEQ])
        zs = at("zs", AT_ARENA + 48 * KB, [P, TT, D])
        LATE = AT_ARENA + 64 * KB
        cvb = [at(f"cvb{i}", LATE + 2112 * i, [P, 3 + SEQ]) for i in range(4)]
        cva = [at(f"cva{i}", LATE + 8448 + 2048 * i, [P, SEQ]) for i in range(2)]
        wsraw = at("wsraw", LATE + 12544, [P, 2 * P])
        wshi = at("wshi", AT_WS, [P, 2 * P], F32R)
        wslo = at("wslo", AT_WS + KB, [P, 2 * P], F32R)
        cw = stat(4 * 3 * GH).rearrange("p (a b) -> p a b", a=4)
        vc = stat(160)
        alog, dtb, bfg, onorm = vc[:, 0:8], vc[:, 8:16], vc[:, 16:32], vc[:, 32:160]

        def pe_qkv_step(i):
            for p in range(2):
                nc.tensor.wait_ge(w_lo, BASE["qkv"] + p + 1 + 2 * i)
                nc.tensor.wait_ge(sem("qkv_raw"), 4 * i + 2 * p - 2)
                feat_slot(p)

        def act_qkv_step(i, first):
            for p in range(2):
                nc.scalar.wait_ge(w_used, BASE["qkv"] + p + 1 + 2 * i)
                for h in range(2):
                    if not first:
                        nc.scalar.wait_ge(sem("qkv_conv"), 4 * i + 2 * p + h - 3)
                    nc.scalar.activation(cvb[2 * p + h][:, 3:3 + SEQ], PS[:, 2 * p + h, :],
                                         ACT.Copy).then_inc(sem("qkv_raw"), 1)
                act_split(2 + 2 * i + p, 2 + p, i)
                for h in range(2):
                    nc.scalar.wait_ge(sem("qkv_conv"), 4 * i + 2 * p + h + 1)
                    nc.scalar.activation(qkvT[:, bass.ds(4 * i + 2 * p + h, 1), :].rearrange("p a b -> p (a b)"),
                                         cva[h][:, :], ACT.Silu).then_inc(sem("qkv_silu"), 1)

        def dve_qkv_step(i, first):
            v = nc.vector
            for p in range(2):
                for h in range(2):
                    j = 4 * i + 2 * p + h
                    v.wait_ge(sem("qkv_raw"), j + 1)
                    if not (first and p == 0):
                        v.wait_ge(sem("qkv_silu"), j - 1)
                    src = cvb[2 * p + h]
                    v.tensor_scalar(cva[h][:, :], src[:, 0:SEQ], cw[:, 0, bass.ds(j, 1)], None,
                                    ALU.mult).then_inc(sem("qkv_tap"), 1)
                    for tap in range(1, 4):
                        v.wait_ge(sem("qkv_tap"), 3 * j + tap)
                        v.scalar_tensor_tensor(out=cva[h][:, :], in0=src[:, tap:tap + SEQ],
                                               scalar=cw[:, tap, bass.ds(j, 1)], in1=cva[h][:, :], op0=ALU.mult,
                                               op1=ALU.add).then_inc(sem("qkv_conv" if tap == 3 else "qkv_tap"), 1)

        logitT = at("logitT", AT_ARENA + 88 * KB, [16, SEQ])

        def small_product(which, bank, done):
            nc.tensor.wait_ge(sem("ws_lo"), 1)
            o = PS[0:16, bank, :]
            for k in range(KT):
                w = (slice(None), slice(which * P + k * 16, which * P + (k + 1) * 16))
                nc.tensor.matmul(o, wshi[w], hT_hi[:, k, :], start=(k == 0), stop=False)
                nc.tensor.matmul(o, wshi[w], hT_lo[:, k, :], start=False, stop=False)
                last = nc.tensor.matmul(o, wslo[w], hT_hi[:, k, :], start=False, stop=(k == KT - 1))
            last.then_inc(sem(done), 1)

        def turn_logits(bank, nth, c=0):
            nc.tensor.wait_ge(sem("logitT"), nth)
            for t in range(TT):
                last = nc.tensor.transpose(PS[:, bank, c + t * 16:c + (t + 1) * 16], logitT[:, t * P:(t + 1) * P], ident[0:16, 0:16])
            last.then_inc(sem("logits"), 1)

        sqb = [b[:, 0:SEQ] for b in cva] + [b[:, 0:SEQ] for b in cvb]

        pick = stat(31)

        def pe_sums(j0, j1):
            for j in range(j0, j1):
                nc.tensor.wait_ge(sem("qk_sq"), j + 1)
                nc.tensor.matmul(PS[0:16, 6, :], pick[:, 15 - j:31 - j], sqb[j % 6], start=(j == 0),
                                 stop=(j == 15)).then_inc(sem("qk_ss"), 1)

        def pe_z():
            b, t = BASE["z"], nc.tensor
            for m in range(2):
                t.wait_ge(w_lo, b + m + 1)
                tok_slot(b + m, 4 * m, 4, 512, 4, m == 0, m == 1)
            t.wait_ge(sem("qkv_raw"), 3 * GH)
            t.wait_ge(w_lo, b + 3)
            tok_slot(b + 2, 0, 4, 512, 0, True, False)
            t.wait_ge(sem("z_silu"), 1)
            t.wait_ge(sem("pick"), 1)
            small_product(0, 4, "ba_logits")
            t.wait_ge(w_lo, b + 4)
            for c in range(TT):
                tok_slot(b + 3, 4, 4, 512, 0, False, True, tiles=[c])
                if c == 0:
                    turn_logits(7, 1)
                if c < TT - 1:
                    pe_sums(4 * c, 4 * c + 4)

        def act_squares(j0, j1):
            a = nc.scalar
            for j in range(j0, j1):
                if j >= 6:
                    a.wait_ge(sem("qk_ss"), j - 5)
                a.activation(sqb[j % 6], qkvT[:, j, :], ACT.Square).then_inc(sem("qk_sq"), 1)

        def act_z():
            b, a = BASE["z"], nc.scalar
            act_split(b + 2)
            a.wait_ge(w_used, b + 2)
            a.activation(zs[:, :, 0:512], PS[:, 4:8, :], ACT.Silu).then_inc(sem("z_silu"), 1)
            act_split(b + 3)
            act_split(b + 4)
            a.wait_ge(sem("ba_logits"), 1)
            a.activation(logitT[:, :], PS[0:16, 4, :], ACT.Copy).then_inc(sem("logitT"), 1)
            a.wait_ge(sem("vec_in"), 32)
            a.activation(nea[:, :], alog, ACT.Exp).then_inc(gate_a, 1)
            a.wait_ge(sem("qkv_silu"), 3 * GH)
            act_squares(0, 6)
            a.wait_ge(sem("logits"), 1)
            a.activation(eb[:, :, :], gb[:, :, 0:8], ACT.Exp, scale=-1.0).then_inc(gate_a, 1)
            a.wait_ge(sem("gate_nab"), 1)
            a.activation(ee[:, :, :], nab[:, :, :], ACT.Exp).then_inc(gate_a, 1)
            a.wait_ge(gate_a, 3)
            a.activation(ln1[:, :, :], ee[:, :, :], ACT.Ln, bias=1.0).then_inc(gate_a, 1)
            act_squares(6, 16)
            a.wait_ge(sem("qk_ss"), 2 * GH)
            a.activation(logitT[:, :], PS[0:16, 6, :], ACT.Copy).then_inc(sem("logitT"), 1)
            a.wait_ge(sem("gate_cum"), 1)
            a.activation(ex[:, :], PS[:, 5, 0:96], ACT.Exp).then_inc(gate_a, 1)
            a.activation(zs[:, :, 512:1024], PS[:, 0:4, :], ACT.Copy).then_inc(sem("z_raw"), 1)
            a.wait_ge(sem("qk_ms"), 1)
            a.activation(rqk_t[:, :], n2s[:, :], ACT.Sqrt).then_inc(sem("qk_rt"), 1)
            act_split(b + 5)

        def s32():
            return stat(TT * GH).rearrange("p (t h) -> p t h", t=TT)

        eb, eb1, beta, xa, xm, nab, ee, ln1, spl, g = (s32() for _ in range(10))
        nea = stat(GH)
        ex = stat(3 * 32)
        eG, eR, eL = (ex[:, 32 * i:32 * i + 32].rearrange("p (t h) -> p t h", t=TT) for i in range(3))
        n2s = stat(64)
        rqk_t = stat(64)
        rqk = stat(64)
        rqkv = rqk.rearrange("p (t j) -> p t j", t=TT)
        beG, rqeG, rqs = s32(), s32(), s32()
        gb = PS[:, 7, 0:64].rearrange("p (t j) -> p t j", t=TT)

        def bt(ap, shape):
            return ap.unsqueeze(len(ap.shape)).to_broadcast(shape)

        def rows(ap, n):
            return ap.unsqueeze(1).to_broadcast([P, n, ap.shape[1]])

        gate_a = sem("gate_a")

        def dve_gates():
            v = nc.vector
            v.wait_ge(gate_a, 2)
            v.tensor_scalar(eb1[:, :, :], eb[:, :, :], 1.0, None, ALU.add).then_inc(dve_step, 1)
            stepped()
            v.reciprocal(beta[:, :, :], eb1[:, :, :]).then_inc(dve_step, 1)
            v.tensor_tensor(xa[:, :, :], gb[:, :, 8:16], rows(dtb, TT), ALU.add).then_inc(dve_step, 1)
            stepped(2)
            v.tensor_scalar(xm[:, :, :], xa[:, :, :], 0.0, None, ALU.max).then_inc(dve_step, 1)
            stepped()
            v.scalar_tensor_tensor(out=nab[:, :, :], in0=xm[:, :, :], scalar=-2.0, in1=xa[:, :, :], op0=ALU.mult,
                                   op1=ALU.add).then_inc(sem("gate_nab"), 1)
            v.wait_ge(gate_a, 4)
            v.tensor_tensor(spl[:, :, :], xm[:, :, :], ln1[:, :, :], ALU.add).then_inc(dve_step, 1)
            stepped()
            v.scalar_tensor_tensor(out=g[:, :, :], in0=spl[:, :, :], scalar=-1.0, in1=rows(nea, TT), op0=ALU.mult,
                                   op1=ALU.mult).then_inc(sem("gate_g"), 1)
            v.wait_ge(sem("logits"), 2)
            v.tensor_scalar(n2s[:, :], PS[:, 7, 64:128], EPS, None, ALU.add).then_inc(sem("qk_ms"), 1)
            v.wait_ge(sem("qk_rt"), 1)
            v.reciprocal(rqk[:, :], rqk_t[:, :]).then_inc(dve_step, 1)
            stepped()
            v.tensor_scalar(rqs[:, :, :], rqkv[:, :, 0:8], GD ** -0.5, None, ALU.mult).then_inc(dve_step, 1)
            v.wait_ge(gate_a, 5)
            v.tensor_tensor(beG[:, :, :], beta[:, :, :], eG[:, :, :], ALU.mult).then_inc(dve_step, 1)
            stepped()
            v.tensor_tensor(rqeG[:, :, :], rqs[:, :, :], eG[:, :, :], ALU.mult).then_inc(dve_step, 1)
            stepped(2)

        def pe_gates():
            t = nc.tensor
            t.wait_ge(sem("gate_g"), 1)
            g2 = g.rearrange("p t h -> p (t h)")
            t.matmul(PS[:, 5, 0:32], const("upto")[:, 0:P], g2, start=True, stop=True)
            t.matmul(PS[:, 5, 32:64], const("strict"), g2, start=True, stop=True)
            t.matmul(PS[:, 5, 64:96], ones, g2, start=True, stop=True).then_inc(sem("gate_cum"), 1)
            pe_sums(12, 16)
            turn_logits(7, 2, 64)
            t.wait_ge(sem("z_raw"), 1)

        SC = [AT_HHI + 4 * KB * i for i in range(8)] + [AT_XN, AT_XN + 4 * KB, AT_JUNK] + [LATE + 4 * KB * i for i in range(4)]
        names = ["kn", "bv", "mgP", "E", "A", "Aqk", "AT", "AqkT", "LT0", "LT1", "knT", "X", "XT", "r", "msk"]
        B = {n: at("g_" + n, SC[i], [P, GH, P]) for i, n in enumerate(names)}
        B["S"] = at("g_S", AT_GAIN, [P, GH, P])
        B["LT"] = [B["LT0"], B["LT1"]]
        msk = B["msk"]
        oss, oms, ort, orr = (stat(GH) for _ in range(4))

        def hs(hf):
            return slice(4 * hf, 4 * hf + 4)

        def bank(b):
            return PS[:, b, :].rearrange("p (h c) -> p h c", h=4)

        HB = [P, 4, P]

        def gw(eng, name, c, hf):
            eng.wait_ge(sem("g_" + name), 2 * c + hf + 1)

        def gl(eng, name, c, l, hf):
            eng.wait_ge(sem("g_" + name), 2 * (LEVELS * c + l - 1) + hf + 1)

        def gx(eng, name, c, l, hf):
            eng.wait_ge(sem("g_" + name), 2 * ((LEVELS - 1) * c + l - 1) + hf + 1)

        def g1(eng, name, c, hf):
            if c:
                eng.wait_ge(sem("g_" + name), 2 * (c - 1) + hf + 1)

        def group(name, b, hf, lhsT, rhs, transpose=False):
            for j in range(4):
                h = 4 * hf + j
                o = PS[:, b + hf, j * P:(j + 1) * P]
                if transpose:
                    last = nc.tensor.transpose(o, lhsT(h), ident)
                else:
                    last = nc.tensor.matmul(o, lhsT(h), rhs(h), start=True, stop=True)
            last.then_inc(sem("g_" + name), 1)

        def pe_chunk(c):
            t = nc.tensor
            ct = slice(c * P, (c + 1) * P)
            for hf in range(2):
                if c:
                    gw(t, "vn", c - 1, hf)
                    gl(t, "Pe", c - 1, LEVELS, hf)
                group("TK", 0, hf, lambda h: qkvT[:, GH + h, ct], None, True)
            for hf in range(2):
                if c:
                    g1(t, "oq", c - 1, hf)
                group("TV", 2, hf, lambda h: qkvT[:, 2 * GH + h, ct], None, True)
            for hf in range(2):
                gw(t, "mg", c, hf)
                if c:
                    gw(t, "o2", c - 1, hf)
                t.matmul(PS[:, 4 + hf, :], const("upto")[:, 0:P], B["mgP"][:, hs(hf), :], start=True,
                         stop=True).then_inc(sem("g_D"), 1)
            for hf in range(2):
                gw(t, "kn", c, hf)
                if c:
                    gw(t, "S", c - 1, hf)
                group("TKN", 6, hf, lambda h: B["kn"][:, h, :], None, True)
            for hf in range(2):
                gw(t, "knT", c, hf)
                group("KK", 0, hf, lambda h: B["knT"][:, h, :], lambda h: B["knT"][:, h, :])
                gw(t, "bv", c, hf)
                group("QK", 2, hf, lambda h: qkvT[:, h, ct], lambda h: B["knT"][:, h, :])
            for hf in range(2):
                gw(t, "A", c, hf)
                gw(t, "E", c, hf)
                group("TA", 4, hf, lambda h: B["A"][:, h, :], None, True)
                gw(t, "Aqk", c, hf)
                group("TQ", 6, hf, lambda h: B["Aqk"][:, h, :], None, True)
            for l in range(1, LEVELS + 1):
                for hf in range(2):
                    gl(t, "LT", c, l, hf)
                    if l == 1:
                        gw(t, "X0", c, hf)
                        gw(t, "XT0", c, hf)
                    else:
                        gx(t, "X", c, l - 1, hf)
                        gl(t, "XT", c, l - 1, hf)
                    group("Pm", 0, hf, lambda h: B["LT"][l % 2][:, h, :], lambda h: B["X"][:, h, :])
                for hf in range(2):
                    gl(t, "Pe", c, l, hf)
                    if l < LEVELS:
                        group("Xm", 2, hf, lambda h: B["XT"][:, h, :], lambda h: B["mgP"][:, h, :])
                    group("XTm", 4, hf, lambda h: B["mgP"][:, h, :], lambda h: B["XT"][:, h, :])
            if c:
                for hf in range(2):
                    gw(t, "AqkT", c, hf)
                    gw(t, "S", c - 1, hf)
                    group("KS", 6, hf, lambda h: B["knT"][:, h, :], lambda h: B["S"][:, h, :])
            for hf in range(2):
                g1(t, "r", c, hf)
                gl(t, "XT", c, LEVELS, hf)
                rhs = B["r"] if c else B["bv"]
                group("VN", 0, hf, lambda h: B["XT"][:, h, :], lambda h: rhs[:, h, :])
                if c:
                    group("QS", 2, hf, lambda h: qkvT[:, h, ct], lambda h: B["S"][:, h, :])
            for hf in range(2):
                gw(t, "vn", c, hf)
                gw(t, "AqkT", c, hf)
                group("O2", 4, hf, lambda h: B["AqkT"][:, h, :], lambda h: B["E"][:, h, :])
                if c < TT - 1:
                    gw(t, "kd", c, hf)
                    g1(t, "ks", c, hf)
                    group("SU", 6, hf, lambda h: B["kn"][:, h, :], lambda h: B["E"][:, h, :])

        def act_chunk(c):
            a = nc.scalar
            for hf in range(2):
                gw(a, "D", c, hf)
                if c:
                    gw(a, "SU", c - 1, hf)
                a.activation(B["E"][:, hs(hf), :], bank(4 + hf), ACT.Exp).then_inc(sem("g_E"), 1)
            for hf in range(2):
                gw(a, "TKN", c, hf)
                a.activation(B["knT"][:, hs(hf), :], bank(6 + hf), ACT.Copy).then_inc(sem("g_knT"), 1)
            for hf in range(2):
                gw(a, "TA", c, hf)
                if c:
                    gl(a, "LT", c - 1, LEVELS, hf)
                a.activation(B["AT"][:, hs(hf), :], bank(4 + hf), ACT.Copy).then_inc(sem("g_AT"), 1)
                gw(a, "TQ", c, hf)
                a.activation(B["AqkT"][:, hs(hf), :], bank(6 + hf), ACT.Copy).then_inc(sem("g_AqkT"), 1)
            if c:
                act_squared(c - 1)
            else:
                a.wait_ge(sem("z_raw"), 1)
                a.activation(zs[:, :, 512:1024], zs[:, :, 512:1024], ACT.Silu).then_inc(sem("z_silu"), 1)
            for l in range(1, LEVELS + 1):
                for hf in range(2):
                    gl(a, "Pm", c, l, hf)
                    a.activation(B["mgP"][:, hs(hf), :], bank(hf), ACT.Copy).then_inc(sem("g_Pe"), 1)
                if c and l == 2:
                    act_root(c - 1)
            for hf in range(2):
                gw(a, "VN", c, hf)
                a.activation(B["E"][:, hs(hf), :], bank(hf), ACT.Copy).then_inc(sem("g_vn"), 1)

        def output(c):
            return qkvT[:, 0:GH, c * P:(c + 1) * P]

        def squared(c):
            return qkvT[:, GH:2 * GH, c * P:(c + 1) * P]

        def act_squared(c):
            a = nc.scalar
            g1(a, "o", c, 1) if c else gw(a, "o2", c, 1)
            a.activation(squared(c), output(c), ACT.Square).then_inc(sem("g_osq"), 1)

        def act_root(c):
            nc.scalar.wait_ge(sem("g_oms"), c + 1)
            nc.scalar.activation(ort[:, :], oms[:, :], ACT.Sqrt).then_inc(sem("g_ort"), 1)

        def dve_mean(c):
            v = nc.vector
            v.wait_ge(sem("g_osq"), c + 1)
            v.tensor_reduce(oss[:, :], squared(c), AX_X, ALU.add).then_inc(dve_step, 1)
            stepped()
            v.tensor_scalar(oms[:, :], oss[:, :], 1.0 / GD, EPS, ALU.mult, ALU.add).then_inc(sem("g_oms"), 1)

        def dve_gated(c):
            v = nc.vector
            v.wait_ge(sem("g_ort"), c + 1)
            v.reciprocal(orr[:, :], ort[:, :]).then_inc(dve_step, 1)
            stepped()
            v.tensor_tensor(output(c), output(c), bt(orr[:, :], [P, GH, P]), ALU.mult).then_inc(dve_step, 1)
            stepped()
            v.wait_ge(sem("g_gz"), c + 1)
            zc = zs[:, c, :].rearrange("p (h d) -> p h d", h=GH)
            v.tensor_tensor(zc, zc, output(c), ALU.mult).then_inc(sem("g_og"), 1)

        def pool_decays(c):
            p = nc.gpsimd
            if c == 0:
                p.wait_ge(sem("gate_g"), 1)
                p.wait_ge(w_used, BASE["gout"])
            for hf in range(2):
                if c:
                    gl(p, "XTm", c - 1, LEVELS, hf)
                p.tensor_tensor(B["mgP"][:, hs(hf), :], bt(g[:, c, hs(hf)], HB), rows(const("strict"), 4),
                                ALU.mult).then_inc(sem("g_mg"), 1)

        def pool_chunk(c):
            p = nc.gpsimd
            if c == 0:
                p.wait_ge(sem("msk_in"), 16)
                p.wait_ge(gate_a, 5)
            else:
                pool_decays(c)
            for hf in range(2):
                gw(p, "E", c, hf)
                p.tensor_tensor(B["E"][:, hs(hf), :], B["E"][:, hs(hf), :], rows(const("tril"), 4),
                                ALU.mult).then_inc(sem("g_M"), 1)
            for l in range(1, LEVELS + 1):
                for hf in range(2):
                    gw(p, "AT", c, hf)
                    if l > 2:
                        gl(p, "Pm", c, l - 2, hf)
                    p.tensor_tensor(B["LT"][l % 2][:, hs(hf), :], B["AT"][:, hs(hf), :], rows(msk[:, l + 1, :], 4),
                                    ALU.mult).then_inc(sem("g_LT"), 1)
                if l == 2:
                    for hf in range(2):
                        gw(p, "TKN", c, hf)
                        p.tensor_tensor(B["kn"][:, hs(hf), :], B["kn"][:, hs(hf), :], bt(eR[:, c, hs(hf)], HB),
                                        ALU.mult).then_inc(sem("g_kd"), 1)
            zc = zs[:, c, :].rearrange("p (h d) -> p h d", h=GH)
            p.wait_ge(sem("z_silu"), 2)
            p.tensor_tensor(zc, zc, rows(onorm, GH), ALU.mult).then_inc(sem("g_gz"), 1)

        def dve_chunk(c):
            v = nc.vector
            for hf in range(2):
                gw(v, "TK", c, hf)
                if c:
                    gw(v, "SU", c - 1, hf)
                v.tensor_tensor(B["kn"][:, hs(hf), :], bank(hf), bt(rqkv[:, c, 8 + 4 * hf:12 + 4 * hf], HB),
                                ALU.mult).then_inc(sem("g_kn"), 1)
            for hf in range(2):
                gw(v, "TV", c, hf)
                v.tensor_tensor(B["bv"][:, hs(hf), :], bank(2 + hf), bt(beta[:, c, hs(hf)], HB),
                                ALU.mult).then_inc(sem("g_bv"), 1)
            for hf in range(2):
                gw(v, "KK", c, hf)
                gw(v, "M", c, hf)
                v.tensor_tensor(B["A"][:, hs(hf), :], bank(hf), B["E"][:, hs(hf), :], ALU.mult).then_inc(dve_step, 1)
                stepped()
                v.tensor_tensor(B["A"][:, hs(hf), :], B["A"][:, hs(hf), :], bt(beta[:, c, hs(hf)], HB),
                                ALU.mult).then_inc(sem("g_A"), 1)
                gw(v, "QK", c, hf)
                v.tensor_tensor(B["Aqk"][:, hs(hf), :], bank(2 + hf), B["E"][:, hs(hf), :],
                                ALU.mult).then_inc(sem("g_Aqk"), 1)
            v.wait_ge(sem("msk_in"), 16)
            for hf in range(2):
                gw(v, "A", c, hf)
                v.tensor_tensor(B["X"][:, hs(hf), :], B["A"][:, hs(hf), :], rows(msk[:, 0, :], 4),
                                ALU.mult).then_inc(dve_step, 1)
                gw(v, "AT", c, hf)
                v.tensor_tensor(B["XT"][:, hs(hf), :], B["AT"][:, hs(hf), :], rows(msk[:, 1, :], 4),
                                ALU.mult).then_inc(dve_step, 1)
                stepped(2)
                v.tensor_tensor(B["X"][:, hs(hf), :], rows(ident, 4), B["X"][:, hs(hf), :],
                                ALU.subtract).then_inc(sem("g_X0"), 1)
                v.tensor_tensor(B["XT"][:, hs(hf), :], rows(ident, 4), B["XT"][:, hs(hf), :],
                                ALU.subtract).then_inc(sem("g_XT0"), 1)
                gw(v, "X0", c, hf)
                gw(v, "XT0", c, hf)
            for l in range(1, LEVELS + 1):
                for hf in range(2):
                    if l < LEVELS:
                        gx(v, "Xm", c, l, hf)
                        v.tensor_tensor(B["X"][:, hs(hf), :], B["X"][:, hs(hf), :], bank(2 + hf),
                                        ALU.subtract).then_inc(sem("g_X"), 1)
                    gl(v, "XTm", c, l, hf)
                    v.tensor_tensor(B["XT"][:, hs(hf), :], B["XT"][:, hs(hf), :], bank(4 + hf),
                                    ALU.subtract).then_inc(sem("g_XT"), 1)
                for hf in range(2):
                    if l < LEVELS:
                        gx(v, "X", c, l, hf)
                    gl(v, "XT", c, l, hf)
                if c and l == 1:
                    dve_mean(c - 1)
                if c and l == 3:
                    dve_gated(c - 1)
            for hf in range(2):
                if c:
                    g1(v, "KS", c, hf)
                    v.tensor_tensor(B["r"][:, hs(hf), :], bank(6 + hf), bt(beG[:, c, hs(hf)], HB),
                                    ALU.mult).then_inc(sem("g_ks"), 1)
                    g1(v, "ks", c, hf)
                    v.tensor_tensor(B["r"][:, hs(hf), :], B["bv"][:, hs(hf), :], B["r"][:, hs(hf), :],
                                    ALU.subtract).then_inc(sem("g_r"), 1)
            for hf in range(2):
                if c:
                    g1(v, "QS", c, hf)
                    v.tensor_tensor(B["A"][:, hs(hf), :], bank(2 + hf), bt(rqeG[:, c, hs(hf)], HB),
                                    ALU.mult).then_inc(sem("g_oq"), 1)
                gw(v, "O2", c, hf)
                v.tensor_tensor(output(c)[:, hs(hf), :], bank(4 + hf), bt(rqs[:, c, hs(hf)], HB),
                                ALU.mult).then_inc(sem("g_o2"), 1)
                gw(v, "o2", c, hf)
                if c:
                    g1(v, "oq", c, hf)
                    v.tensor_tensor(output(c)[:, hs(hf), :], output(c)[:, hs(hf), :], B["A"][:, hs(hf), :],
                                    ALU.add).then_inc(sem("g_o"), 1)
            if c < TT - 1:
                for hf in range(2):
                    gw(v, "SU", c, hf)
                    if c:
                        v.tensor_tensor(B["S"][:, hs(hf), :], B["S"][:, hs(hf), :], bt(eL[:, c, hs(hf)], HB),
                                        ALU.mult).then_inc(dve_step, 1)
                        stepped()
                        v.tensor_tensor(B["S"][:, hs(hf), :], B["S"][:, hs(hf), :], bank(6 + hf),
                                        ALU.add).then_inc(sem("g_S"), 1)
                    else:
                        v.tensor_copy(B["S"][:, hs(hf), :], bank(6 + hf)).then_inc(sem("g_S"), 1)

        GT = Turn(1, lambda t, k: zs[:, t, k * P:(k + 1) * P], lambda eng, t: eng.wait_ge(sem("g_og"), t + 1))

        act_sb = at("act_sb", AT_ARENA, [P, FT, SEQ])
        ahi = [at(f"ahi{i}", AT_ARENA + 44 * KB + 4 * KB * i, [P, 2, SEQ], F32R) for i in range(2)]
        alo = [at(f"alo{i}", AT_ARENA + 52 * KB + 4 * KB * i, [P, 2, SEQ], F32R) for i in range(2)]
        sil = [at(f"sil{i}", AT_ARENA + 60 * KB + 2 * KB * i, [P, SEQ]) for i in range(2)]
        NP = FT // 2

        class Ffn:
            def __init__(self, l, norm, mix, after):
                self.norm, self.mix, self.next = norm, mix, after
                self.b, self.c = BASE[f"fin{l}"], BASE[f"fout{l}"]
                self.p0, self.h0 = FT * l, NP * l

            def pe(self):
                t = nc.tensor
                self.norm.pe_head(self.b)

                def step(i):
                    for p in range(2):
                        t.wait_ge(w_lo, self.b + p + 1 + 2 * i)
                        t.wait_ge(sem("ffn_prod"), self.p0 + 2 * i + p - 1)
                        feat_slot((self.b + p) % 2)

                with t.Fori(1, NP) as i:
                    step(i)

                def out(m, static, i=0, tiles=range(TT)):
                    t.wait_ge(w_lo, self.c + static + 1 + 2 * i)
                    t.wait_ge(sem("ffn_lo"), self.h0 + static + 1 + 2 * i)
                    q = static % 2
                    self.mix.pe_slot(self.c + static, m == 0, m == NP - 1,
                                     lambda kk, tt: ahi[q][:, kk, tt * P:(tt + 1) * P],
                                     lambda kk, tt: alo[q][:, kk, tt * P:(tt + 1) * P], free if m == 0 else None,
                                     tiles)

                def free(tt):
                    if tt == 0:
                        t.wait_ge(sem("ffn_prod"), self.p0 + FT)

                out(0, 0, tiles=(2, 3, 0, 1))
                out(1, 1)
                with t.Fori(1, (NP - 3) // 2) as i:
                    out(-1, 0, i)
                    out(-1, 1, i)
                out(-1, NP - 3)
                self.mix.pe_last(lambda m, tiles: out(NP - 2 + m, NP - 2 + m, 0, tiles))

            def hi_of(self, static, i=0):
                if static >= 2:
                    nc.scalar.wait_ge(w_used, self.c + static - 1 + 2 * i)
                if static < 2:
                    nc.scalar.wait_ge(sem("ffn_prod"), self.p0 + 2 * static + 2)
                else:
                    nc.scalar.wait_ge(sem("ffn_prod"), self.p0 + FT)
                nc.scalar.activation(ahi[static % 2][:, :, :], act_sb[:, bass.ds(2 * static + 4 * i, 2), :],
                                     ACT.Copy).then_inc(sem("ffn_hi"), 1)

            def act(self):
                a = nc.scalar

                def step(i, first, cut=False):
                    for p in range(2):
                        a.wait_ge(w_used, self.b + p + 1 + 2 * i)
                        if not first:
                            a.wait_ge(sem("ffn_prod"), self.p0 + 2 * i + p - 1)
                        a.activation(sil[p][:, :], PS[:, 2 * ((self.b + p) % 2), :], ACT.Silu).then_inc(sem("ffn_silu"), 1)
                        act_split(None, self.b + p + 2, i)

                step(0, True)
                with a.Fori(1, 4) as i:
                    step(i, False)
                self.hi_of(0)
                self.hi_of(1)
                with a.Fori(4, NP) as i:
                    step(i, False)
                with a.Fori(0, (NP - 3) // 2) as i:
                    for p in range(2):
                        act_split(None, self.c + 2 + p, i)
                        self.hi_of(2 + p, i)
                act_split(self.c + NP - 1)
                self.hi_of(NP - 1)
                act_chain(self.mix, self.next, self.c + NP + 1)

            def dve(self):
                v = nc.vector

                def step(i):
                    for p in range(2):
                        v.wait_ge(sem("ffn_silu"), self.p0 + 2 * i + p + 1)
                        v.tensor_tensor(act_sb[:, bass.ds(2 * i + p, 1), :].rearrange("p a b -> p (a b)"), sil[p][:, :],
                                        PS[:, 2 * ((self.b + p) % 2) + 1, :], ALU.mult).then_inc(sem("ffn_prod"), 1)

                def low(static, i=0):
                    v.wait_ge(sem("ffn_hi"), self.h0 + static + 1 + 2 * i)
                    v.tensor_tensor(alo[static % 2][:, :, :], act_sb[:, bass.ds(2 * static + 4 * i, 2), :],
                                    ahi[static % 2][:, :, :].bitcast(F32), ALU.subtract).then_inc(sem("ffn_lo"), 1)

                with v.Fori(0, 5) as i:
                    step(i)
                v.wait_ge(sem("ffn_prod"), self.p0 + 4)
                low(0)
                low(1)
                with v.Fori(5, NP) as i:
                    step(i)
                v.wait_ge(sem("ffn_prod"), self.p0 + FT)
                with v.Fori(1, (NP - 1) // 2) as i:
                    low(0, i)
                    low(1, i)
                low(NP - 1)
                dve_chain(self.mix, self.next)

        F0 = Ffn(0, NF0, FOUT0, NKV)
        F1 = Ffn(1, NF1, FOUT1, N2)

        class Attention:

            def __init__(self, before, heads, q, k, v, mask, out, pbuf, ptbuf, after=None, ready=None, copies="vector"):
                self.q, self.k, self.v, self.mask, self.out = q, k, v, mask, out
                self.pbuf, self.ptbuf, self.after, self.ready, self.copies = pbuf, ptbuf, after, ready, copies
                self.groups = [(i, b) for i in range(TT - 1, -1, -1) for b in range(heads // 8)]
                self.units = [(g, i, 8 * b + j) for g, (i, b) in enumerate(self.groups) for j in range(8)]
                self.nm, self.rs, self.ri = stat(4), stat(TT * heads), stat(TT * heads)
                self.u0 = sum(len(a.units) for a in before)
                self.g0 = sum(len(a.groups) for a in before)

            def obank(self, g):
                return 4 + (self.g0 + g) % 2

            def ring(self, u):
                n = (self.u0 + u) % 3
                return (0, 1, 6)[n], (2, 3, 7)[n], n

            def pe_scores(self, u):
                t = nc.tensor
                g, i, h = self.units[u]
                if self.u0 + u >= 3:
                    t.wait_ge(sem("at_exp"), self.u0 + u - 2)
                if self.ready and h % 8 == 0 and i:
                    self.ready(i)
                full, m = self.mask(i)
                b, q = self.ring(u)[0], self.q(h, i)
                n, d = (i + 1) * P, i * P
                if full:
                    t.matmul(PS[:, b, 0:n].rearrange("p (j c) -> p j c", c=P), q, self.k(h, 0, i + 1), start=True, stop=False)
                    t.matmul(PS[:, b, 0:n], identr[:, :], m, start=False, stop=True).then_inc(sem("at_score"), 1)
                else:
                    if i:
                        t.matmul(PS[:, b, 0:d].rearrange("p (j c) -> p j c", c=P), q, self.k(h, 0, i), start=True, stop=True)
                    t.matmul(PS[:, b, d:n], q, self.k(h, i, i + 1), start=True, stop=False)
                    t.matmul(PS[:, b, d:n], ident, m, start=False, stop=True).then_inc(sem("at_score"), 1)

            def pe_turn(self, u):
                t = nc.tensor
                _, i, h = self.units[u]
                t.wait_ge(sem("at_exp"), self.u0 + u + 1)
                if self.u0 + u >= 3:
                    t.wait_ge(sem("at_pt"), self.u0 + u - 2)
                _, b, m = self.ring(u)
                for j in range(i + 1):
                    last = t.transpose(PS[:, b, j * P:(j + 1) * P], self.pbuf[m][:, j * P:(j + 1) * P], ident)
                last.then_inc(sem("at_turned"), 1)

            def pe_values(self, u):
                t = nc.tensor
                g, i, h = self.units[u]
                t.wait_ge(sem("at_pt"), self.u0 + u + 1)
                if h % 8 == 0 and self.g0 + g >= 2:
                    t.wait_ge(sem("at_out"), self.g0 + g - 1)
                c = (h % 8) * 64
                for j in range(i + 1):
                    last = t.matmul(PS[:, self.obank(g), c:c + 64], self.ptbuf[self.ring(u)[2]][:, j * P:(j + 1) * P],
                                    self.v(h, j), start=(j == 0), stop=(j == i))
                last.then_inc(sem("at_pv"), 1)

            def exp(self, u):
                a = nc.scalar
                a.wait_ge(sem("at_max"), self.u0 + u + 1)
                if self.u0 + u >= 3:
                    a.wait_ge(sem("at_turned"), self.u0 + u - 2)
                n = (self.units[u][1] + 1) * P
                b, _, m = self.ring(u)
                a.activation(self.pbuf[m][:, 0:n], PS[:, b, 0:n], ACT.Exp, bias=self.nm[:, u % 4:u % 4 + 1],
                             accum_out=self.rs[:, u:u + 1]).then_inc(sem("at_exp"), 1)

            def copy_pt(self, e, u):
                e.wait_ge(sem("at_turned"), self.u0 + u + 1)
                if self.u0 + u >= 3:
                    e.wait_ge(sem("at_pv"), self.u0 + u - 2)
                n = (self.units[u][1] + 1) * P
                _, b, m = self.ring(u)
                o, i = self.ptbuf[m][:, 0:n], PS[:, b, 0:n]
                if e is nc.scalar:
                    nc.scalar.activation(o, i, ACT.Copy).then_inc(sem("at_pt"), 1)
                else:
                    nc.vector.tensor_copy(o, i).then_inc(sem("at_pt"), 1)

            def dve_out(self, g):
                v = nc.vector
                i, b = self.groups[g]
                v.wait_ge(sem("at_exp"), self.u0 + 8 * (g + 1))
                c = slice(8 * g, 8 * (g + 1))
                v.reciprocal(self.ri[:, c], self.rs[:, c]).then_inc(dve_step, 1)
                stepped()
                v.wait_ge(sem("at_pv"), self.u0 + 8 * (g + 1))
                v.tensor_tensor(self.out(i, b), PS[:, self.obank(g), :].rearrange("p (a b c) -> p a b c", a=4, b=2),
                                bt(self.ri[:, c].rearrange("p (a b) -> p a b", a=4), [P, 4, 2, 64]),
                                ALU.mult).then_inc(sem("at_out"), 1)
                if self.after:
                    v.wait_ge(sem("at_out"), self.g0 + g + 1)
                    self.after(i)

            def dve_max(self, u):
                v = nc.vector
                v.wait_ge(sem("at_score"), self.u0 + u + 1)
                v.tensor_reduce(self.nm[:, u % 4:u % 4 + 1], PS[:, self.ring(u)[0], 0:(self.units[u][1] + 1) * P], AX_X,
                                ALU.max, negate=True).then_inc(sem("at_max"), 1)

        def all_units(attentions):
            return [(a, u) for a in attentions for u in range(len(a.units))]

        def pe_attend(attentions):
            w = all_units(attentions)
            for n in range(len(w) + 3):
                if n < len(w):
                    w[n][0].pe_scores(w[n][1])
                if 2 <= n < len(w) + 2:
                    w[n - 2][0].pe_turn(w[n - 2][1])
                if n >= 3:
                    w[n - 3][0].pe_values(w[n - 3][1])

        def act_attend(attentions):
            w = all_units(attentions)
            for n in range(len(w) + 2):
                if n < len(w):
                    w[n][0].exp(w[n][1])
                if n >= 2 and w[n - 2][0].copies == "scalar":
                    w[n - 2][0].copy_pt(nc.scalar, w[n - 2][1])

        def dve_attend(attentions, hook=None):
            w = all_units(attentions)
            for n in range(len(w) + 4):
                if n < len(w):
                    w[n][0].dve_max(w[n][1])
                if 2 <= n < len(w) + 2 and w[n - 2][0].copies == "vector":
                    w[n - 2][0].copy_pt(nc.vector, w[n - 2][1])
                if n >= 4 and n % 8 == 3:
                    w[n - 4][0].dve_out(w[n - 4][1] // 8)
                if hook and n < len(w):
                    hook(n)

        KA = at("KA", AT_ARENA, [P, FH, SEQ])
        QA = at("QA", AT_ARENA + 32 * KB, [P, FH, SEQ])
        FV = at("FV", AT_ARENA + 64 * KB, [P, TT, D])
        crow = [at(f"crow{i}", AT_ARENA + 80 * KB + 2 * KB * i, [16, SEQ]) for i in range(2)]
        fp = [at(f"fp{i}", AT_ARENA + 80 * KB + 2 * KB * i, [P, SEQ]) for i in range(3)]
        fpt = [at(f"fpt{i}", AT_XN + 2 * KB * i, [P, SEQ]) for i in range(3)]
        identr = at("identr", AT_JUNK, [P, P], F32R)
        fl, fm, fna, fe, fln, lf = (stat(TT * FH).rearrange("p (t h) -> p t h", t=TT) for _ in range(6))
        FOX = Attention([], FH, lambda h, i: QA[0:66, h, i * P:(i + 1) * P],
                        lambda h, a, b: KA[0:66, h, a * P:b * P].rearrange("p (j c) -> p j c", c=P), lambda h, j: FV[:, j, h * FD:(h + 1) * FD],
                        lambda i: (False, const("negcausal")),
                        lambda i, b: QA[:, 4 * b:4 * b + 4, i * P:(i + 1) * P].rearrange("p a (b c) -> p a b c", b=2),
                        fp, fpt)
        FT_ = Turn(5, lambda t, k: QA[:, k, t * P:(t + 1) * P], lambda eng, t: eng.wait_ge(sem("at_out"), 2 * TT))

        def pe_heads(stage):
            b = BASE[stage]
            h0 = 8 if stage == "fq" else 0
            for m in range(2, 4):
                nc.tensor.wait_ge(w_lo, b + m + 1)
                nc.tensor.wait_ge(sem("heads_a"), h0 + 2 * (m - 1))
                nc.tensor.wait_ge(sem("heads_v"), h0 + 2 * (m - 1))
                feat_slot((b + m) % 2)

        def act_heads(stage, dst, scale):
            b = BASE[stage]
            for m in range(4):
                nc.scalar.wait_ge(w_used, b + m + 1)
                for r in range(2):
                    nc.scalar.activation(dst[0:64, 4 * m + r, :], PS[64 * r:64 * r + 64, 2 * ((b + m) % 2), :], ACT.Copy,
                                         scale=scale).then_inc(sem("heads_a"), 1)
                act_split(b + m + 2)

        def dve_heads(stage, dst, scale):
            b = BASE[stage]
            for m in range(4):
                nc.vector.wait_ge(w_used, b + m + 1)
                for r in range(2):
                    nc.vector.tensor_scalar(dst[0:64, 4 * m + 2 + r, :], PS[64 * r:64 * r + 64, 2 * ((b + m) % 2) + 1, :],
                                            scale, None, ALU.mult).then_inc(sem("heads_v"), 1)

        def foxproj_free(eng, t):
            eng.wait_ge(sem("fv"), 2)
            if t >= 2:
                eng.wait_ge(sem("c_rows"), 2)

        def pe_foxproj():
            t = nc.tensor
            NKV.pe_head(BASE["fk"])
            pe_heads("fk")
            b = BASE["fv"]
            for cb in range(2):
                if cb:
                    t.wait_ge(sem("heads_a"), 8)
                    t.wait_ge(sem("heads_v"), 8)
                for m in range(2):
                    t.wait_ge(w_lo, b + 2 * cb + m + 1)
                    tok_slot(b + 2 * cb + m, 4 * m, 4, 512, 4 - 4 * cb, m == 0, m == 1)
            t.wait_ge(sem("fv"), 1)
            small_product(1, 4, "f_logits")
            turn_logits(6, 3)

            def sum_gates():
                t.wait_ge(sem("lf"), 1)
                for j in range(TT):
                    last = t.matmul(PS[0:16, 5, j * P:SEQ], lf[:, j, :], const("upto")[:, 0:SEQ - j * P], start=(j == 0),
                                    stop=(j == TT - 1), skip_group_check=True)
                last.then_inc(sem("c_sum"), 1)

            NQ.pe_head(BASE["fq"], foxproj_free, sum_gates)
            pe_heads("fq")

        def act_foxproj():
            a = nc.scalar
            act_heads("fk", KA, 1.0)
            b = BASE["fv"]
            for cb in range(2):
                act_split(b + 2 * cb + 2)
                a.wait_ge(w_used, b + 2 * cb + 2)
                a.activation(FV[:, :, cb * 512:(cb + 1) * 512], PS[:, 4 - 4 * cb:8 - 4 * cb, :],
                             ACT.Copy).then_inc(sem("fv"), 1)
                act_split(b + 2 * cb + 3)
            a.wait_ge(sem("f_logits"), 1)
            a.activation(logitT[:, :], PS[0:16, 4, :], ACT.Copy).then_inc(sem("logitT"), 1)
            a.wait_ge(sem("fna"), 1)
            a.activation(fe[:, :, :], fna[:, :, :], ACT.Exp).then_inc(gate_a, 1)
            a.wait_ge(gate_a, 6)
            a.activation(fln[:, :, :], fe[:, :, :], ACT.Ln, bias=1.0).then_inc(gate_a, 1)
            NQ.T.act_tile(0)
            NQ.T.act_tile(1)
            a.wait_ge(sem("c_sum"), 1)
            a.activation(crow[0][:, :], PS[0:16, 5, :], ACT.Copy).then_inc(sem("c_rows"), 1)
            a.activation(crow[1][:, :], PS[0:16, 5, :], ACT.Copy, scale=-1.0).then_inc(sem("c_rows"), 1)
            NQ.T.act_tile(2)
            NQ.T.act_tile(3)
            act_heads("fq", QA, FD ** -0.5)

        def dve_foxproj():
            v = nc.vector
            dve_heads("fk", KA, 1.0)
            v.memset(KA[64:66, :, :], 1.0).then_inc(sem("rows1"), 1)
            v.memset(QA[64:66, :, :], 1.0).then_inc(sem("rows1"), 1)
            NQ.dve_xn(0)
            NQ.dve_xn(1)
            v.wait_ge(sem("logits"), 3)
            v.tensor_tensor(fl[:, :, :], PS[:, 6, 0:64].rearrange("p (t h) -> p t h", t=TT), rows(bfg, TT),
                            ALU.add).then_inc(dve_step, 1)
            stepped()
            v.tensor_scalar(fm[:, :, :], fl[:, :, :], 0.0, None, ALU.min).then_inc(dve_step, 1)
            stepped()
            v.scalar_tensor_tensor(out=fna[:, :, :], in0=fm[:, :, :], scalar=2.0, in1=fl[:, :, :], op0=ALU.mult,
                                   op1=ALU.subtract).then_inc(sem("fna"), 1)
            v.wait_ge(gate_a, 7)
            v.tensor_tensor(lf[:, :, :], fm[:, :, :], fln[:, :, :], ALU.subtract).then_inc(sem("lf"), 1)
            for t in (0, 1):
                NQ.T.dve(t)
            for t in (2, 3):
                NQ.dve_xn(t)
            for t in (2, 3):
                NQ.T.dve(t)
            dve_heads("fq", QA, FD ** -0.5)

        def pe_fox():
            nc.tensor.wait_ge(sem("heads_a"), 16)
            nc.tensor.wait_ge(sem("heads_v"), 16)
            nc.tensor.wait_ge(sem("crows_in"), 32)
            pe_attend([FOX])
            FT_.pe()

        def pe_rows(mix, stage, turn):
            def slot(m, tiles):
                nc.tensor.wait_ge(w_lo, BASE[stage] + m + 1)
                mix.pe_slot(BASE[stage] + m, m == 0, m == 3, lambda kk, tt: hT_hi[:, 2 * m + kk, tt * P:(tt + 1) * P],
                            lambda kk, tt: hT_lo[:, 2 * m + kk, tt * P:(tt + 1) * P],
                            (lambda tt: turn.tile_done(nc.tensor, tt)) if m == 0 else None, tiles)

            slot(0, range(TT))
            slot(1, range(TT))
            mix.pe_last(lambda m, tiles: slot(2 + m, tiles))

        def act_rows(mix, stage, norm):
            for m in range(2):
                act_split(BASE[stage] + m + 2)
            act_chain(mix, norm, BASE[stage] + 5)

        STEPS = ["qi", "cq", "ckv", "Tcq", "qa", "Tckv", "uq0", "uq1", "ukv0", "ukv1", "ka", "va", "Tqi", "ga", "Tqa",
                 "Tki", "gb", "Tqb0", "Tqb1", "Tkb0", "Tkb1", "Tka"]
        PREPS = ["cq", "ckv", "lcq", "qi", "lckv", "qa", "qb0", "qb1", "kb", "ka"]
        BLK = ["qi", "cq", "ckv", "qa", "ka", "va", "ga", "gb"]
        COLS = {n: c1 - c0 for n, (c0, c1) in zip(BLK, IN2_BLOCKS)}
        SLOT_OF = {n: (BASE["in2"] if j < 4 else BASE["in2b"] - 8) + 2 * j for j, n in enumerate(BLK)}

        qa, ka, qi, va = (at(n, AT_ARENA + 8 * KB * i, [P, TT, AH, AD]) for i, n in enumerate(("qa", "ka", "qi", "va")))
        cqb = at("cqb", AT_ARENA + 24 * KB, [P, TT, COLS["cq"]])
        ckvb = at("ckvb", AT_ARENA + 32 * KB, [P, TT, COLS["ckv"]])
        gz = at("gz", AT_ARENA + 32 * KB, [P, TT, D])
        tmp_a = at("tmp_a", AT_ARENA + 37 * KB, [P, 2048])
        tmp_b = at("tmp_b", AT_XN, [P, 3072])
        vlat = at("vlat", AT_ARENA + 45 * KB, [P, QL + KVL])
        qb = at("qb", AT_ARENA + 48 * KB, [P, TT, BH, P])
        kb = at("kb", AT_ARENA + 64 * KB, [P, TT, BH, P])
        vb = at("vb", AT_ARENA + 80 * KB, [P, TT, BH, BV])
        vh = at("vh", AT_ARENA + 88 * KB, [P, 2 * AD + 2 * BQ])
        krb = at("krb", AT_ARENA + 88 * KB + 1536, [P, TT, BR])
        kir = at("kir", AT_WS, [P, TT, P])
        lat_hi = at("lat_hi", AT_GAIN, [P, 5, SEQ], F32R)
        lat_lo = at("lat_lo", AT_GAIN + 10 * KB, [P, 5, SEQ], F32R)
        pbuf = [at(f"pbuf{i}", AT_HLO + 2 * KB * i, [P, SEQ]) for i in range(3)]
        ptbuf = [at(f"ptbuf{i}", AT_HLO + 6 * KB + 2 * KB * i, [P, SEQ]) for i in range(3)]
        obuf = [at(f"obuf{i}", AT_HLO + 12 * KB + 2 * KB * i, [P, 512]) for i in range(2)]
        score = [at(f"score{i}", AT_GAIN + 2 * KB * i, [P, SEQ]) for i in range(3)]
        topm = [at(f"topm{i}", AT_XN + 2 * KB * i, [P, SEQ], F32R) for i in range(3)]
        wi = stat(TT * AH).rearrange("p (t h) -> p t h", t=TT)
        rms_s, rms_m, rms_t, rms_r = (stat(TT * BH) for _ in range(4))
        top8 = stat(8)
        evacs = {n: (2 if n in ("ukv0", "ukv1") else 1) for n in STEPS}

        def evac_done(eng, name):
            eng.wait_ge(sem("st_evac"), sum(evacs[n] for n in STEPS[:STEPS.index(name) + 1]))

        def prep_done(eng, name):
            eng.wait_ge(sem("prep"), PREPS.index(name) + 1)

        TURNS = [n for n in STEPS if n[0] == "T"]

        def group_of(name):
            return 4 * (STEPS.index(name) % 2)

        def pe_step(name):
            t, g = nc.tensor, group_of(name)
            s = STEPS.index(name)
            if s >= 2:
                evac_done(t, STEPS[s - 2])
                if name == "Tqb0":
                    t.wait_ge(sem("idx_sum"), len(IDX))
                if STEPS[s - 2] in ("Tcq", "Tckv"):
                    prep_done(t, "l" + STEPS[s - 2][1:])
            if name in BLK:
                n = SLOT_OF[name]
                for m in range(2):
                    t.wait_ge(w_lo, n + m + 1)
                    tok_slot(n + m, 4 * m, 4, COLS[name], g, m == 0, m == 1)
            elif name in ("uq0", "uq1"):
                n = BASE["uq"] + int(name[2])
                prep_done(t, "lcq")
                t.wait_ge(w_lo, n + 1)
                tok_slot(n, 0, QL // P, 384, g, True, True, lat_hi, lat_lo)
            elif name in ("ukv0", "ukv1"):
                half, q = int(name[3]), BASE["ukv"] % 2
                prep_done(t, "lckv")
                t.wait_ge(w_lo, BASE["ukv"] + 1)
                for tt in range(TT):
                    for kk in range(2):
                        w = (slice(None), slice(kk * D + 512 * half, kk * D + 512 * half + 512))
                        ts = slice(tt * P, (tt + 1) * P)
                        o = PS[:, g + tt, :]
                        t.matmul(o, lat_hi[:, 3 + kk, ts], whi[q][w], start=(kk == 0), stop=False)
                        t.matmul(o, lat_hi[:, 3 + kk, ts], wlo[q][w], start=False, stop=False)
                        last = t.matmul(o, lat_lo[:, 3 + kk, ts], whi[q][w], start=False, stop=(kk == 1))
                last.then_inc(w_used if half else sem("kv_half"), 1)
            else:
                prep_done(t, {"Tki": "qi"}.get(name, name[1:].rstrip("01") if name[1] == "k" else name[1:]))
                if name in ("Tcq", "Tckv"):
                    src, first, nk = (cqb, 72, 3) if name == "Tcq" else (ckvb, 0, 2)
                    for k in range(nk):
                        for tt in range(TT):
                            last = t.transpose(PS[:, g + k, tt * P:(tt + 1) * P],
                                               src[:, tt, first + k * P:first + (k + 1) * P], ident)
                elif name == "Tki":
                    for tt in range(TT):
                        last = t.transpose(PS[:, g, tt * P:(tt + 1) * P], kir[:, tt, :], ident)
                elif name in ("Tqi", "Tqa", "Tka"):
                    src = {"Tqi": qi, "Tqa": qa, "Tka": ka}[name].rearrange("p t h c -> p t (h c)")
                    for tt in range(TT):
                        for k in range(4):
                            last = t.transpose(PS[:, g + tt, k * P:(k + 1) * P], src[:, tt, k * P:(k + 1) * P], ident)
                else:
                    src, q = {"q": qb, "k": kb}[name[1]], int(name[3])
                    for tt in range(TT):
                        for j in range(4):
                            last = t.transpose(PS[0:BQ, g + tt, j * P:(j + 1) * P], src[:, tt, 4 * q + j, 0:BQ], ident)
                last.then_inc(sem("turned"), 1)

        def act_step(name):
            a, g = nc.scalar, group_of(name)
            bank4 = PS[:, g:g + 4, :]

            def evac(o, i, func=ACT.Copy, scale=1.0):
                a.activation(o, i, func, scale=scale).then_inc(sem("st_evac"), 1)

            if name in BLK:
                n = SLOT_OF[name]
                act_split(n + 2)
                act_split(n + 3)
                i = PS[:, g:g + 4, 0:COLS[name]]
                if name in ("va", "ga"):
                    prep_done(a, "qi" if name == "va" else "qb1")
                if name in ("ga", "gb"):
                    c = 512 * (name == "gb")
                    evac(gz[:, :, c:c + 512], i, ACT.Silu)
                elif name in ("cq", "ckv"):
                    evac({"cq": cqb, "ckv": ckvb}[name][:, :, :], i)
                else:
                    evac({"qi": qi, "qa": qa, "ka": ka, "va": va}[name].rearrange("p t h c -> p t (h c)"), i)
            elif name in ("uq0", "uq1"):
                n, q = BASE["uq"] + int(name[2]), int(name[2])
                act_split(n + 2)
                evac(qb[:, :, 4 * q:4 * q + 4, 0:BQ], PS[:, g:g + 4, 0:384].rearrange("p t (h c) -> p t h c", h=4))
            elif name in ("ukv0", "ukv1"):
                q = int(name[3])
                if q:
                    act_split(BASE["ukv"] + 2)
                else:
                    a.wait_ge(sem("kv_half"), 1)
                i = bank4.rearrange("p t (h c) -> p t h c", h=4)
                evac(kb[:, :, 4 * q:4 * q + 4, 0:BN], i[:, :, :, 0:BN])
                evac(vb[:, :, 4 * q:4 * q + 4, :], i[:, :, :, BN:P])
            else:
                a.wait_ge(sem("turned"), TURNS.index(name) + 1)
                if name in ("Tcq", "Tckv"):
                    k0, nk = (0, 3) if name == "Tcq" else (3, 2)
                    evac(lat_hi[:, k0:k0 + nk, :], PS[:, g:g + nk, :])
                elif name == "Tki":
                    evac(kir.rearrange("p t c -> p (t c)"), PS[:, g, :])
                elif name in ("Tqi", "Tqa", "Tka"):
                    evac({"Tqi": qi, "Tqa": qa, "Tka": ka}[name].rearrange("p t h c -> p t (h c)"), bank4,
                         scale=AD ** -0.5 if name == "Tqa" else 1.0)
                else:
                    q = int(name[3])
                    evac({"q": qb, "k": kb}[name[1]][0:BQ, :, 4 * q:4 * q + 4, :].rearrange("p t h c -> p t (h c)"),
                         PS[0:BQ, g:g + 4, :], scale=BQ ** -0.5 if name[1] == "q" else 1.0)

        RMS = ["cq", "ckv", "qa", "qb0", "qb1", "kb", "ka"]

        def act_rt(name, n):
            nc.scalar.wait_ge(sem("rms_ms"), RMS.index(name) + 1)
            nc.scalar.activation(rms_t[:, 0:n], rms_m[:, 0:n], ACT.Sqrt).then_inc(sem("rms_rt"), 1)

        def dve_rms(name, x, tmp, gain_row, last=None):
            v = nc.vector
            _, nt, nh, w = x.shape
            n = nt * nh
            sq = tmp[:, 0:n * w].rearrange("p (t h c) -> p t h c", t=nt, h=nh)
            v.tensor_tensor(sq, x, x, ALU.mult).then_inc(dve_step, 1)
            stepped()
            v.tensor_reduce(rms_s[:, 0:n].rearrange("p (t h) -> p t h", t=nt), sq, AX_X, ALU.add).then_inc(dve_step, 1)
            stepped()
            v.tensor_scalar(rms_m[:, 0:n], rms_s[:, 0:n], 1.0 / w, EPS, ALU.mult, ALU.add).then_inc(sem("rms_ms"), 1)
            v.wait_ge(sem("rms_rt"), RMS.index(name) + 1)
            v.reciprocal(rms_r[:, 0:n], rms_t[:, 0:n]).then_inc(dve_step, 1)
            stepped()
            r = rms_r[:, 0:n].rearrange("p (t h) -> p t h", t=nt).unsqueeze(3).to_broadcast([P, nt, nh, w])
            v.tensor_tensor(x, x, r, ALU.mult).then_inc(dve_step, 1)
            stepped()
            o = v.tensor_tensor(x, x, gain_row.unsqueeze(1).unsqueeze(1).to_broadcast([P, nt, nh, w]), ALU.mult)
            o.then_inc(sem("prep") if last else dve_step, 1)
            if not last:
                stepped()

        def dve_rope(x, half, table, tmp, last):
            v = nc.vector
            _, nt, nh, _ = x.shape
            shape = [P, nt, nh, half]
            n = nt * nh * half
            cos, sin = (const(s + table).rearrange("p (t c) -> p t c", t=TT).unsqueeze(2).to_broadcast(shape)
                        for s in ("cos", "sin"))
            x1, x2 = x[:, :, :, 0:half], x[:, :, :, half:2 * half]
            a, b = (tmp[:, n * i:n * i + n].rearrange("p (t h c) -> p t h c", t=nt, h=nh) for i in range(2))
            v.tensor_tensor(a, x1, sin, ALU.mult).then_inc(dve_step, 1)
            v.tensor_tensor(b, x2, sin, ALU.mult).then_inc(dve_step, 1)
            v.tensor_tensor(x1, x1, cos, ALU.mult).then_inc(dve_step, 1)
            v.tensor_tensor(x2, x2, cos, ALU.mult).then_inc(dve_step, 1)
            stepped(4)
            v.tensor_tensor(x1, x1, b, ALU.subtract).then_inc(dve_step, 1)
            v.tensor_tensor(x2, x2, a, ALU.add).then_inc(sem("prep") if last else dve_step, 1)
            stepped(1 if last else 2)

        def dve_prep(name):
            v = nc.vector
            if PREPS.index(name):
                prep_done(v, PREPS[PREPS.index(name) - 1])
            if name == "cq":
                evac_done(v, "cq")
                v.wait_ge(sem("vec2_in"), 48)
                dve_rms("cq", cqb[:, :, 72:72 + QL].unsqueeze(2), tmp_a, vlat[:, 0:QL], True)
            elif name == "ckv":
                evac_done(v, "ckv")
                dve_rms("ckv", ckvb[:, :, 0:KVL].unsqueeze(2), tmp_a, vlat[:, QL:], True)
            elif name in ("lcq", "lckv"):
                k0, nk = (0, 3) if name == "lcq" else (3, 2)
                g = group_of("T" + name[1:])
                evac_done(v, "T" + name[1:])
                v.tensor_tensor(lat_lo[:, k0:k0 + nk, :], PS[:, g:g + nk, :], lat_hi[:, k0:k0 + nk, :].bitcast(F32),
                                ALU.subtract).then_inc(sem("prep"), 1)
            elif name == "qi":
                v.tensor_copy(wi, cqb[:, :, 64:72]).then_inc(dve_step, 1)
                v.tensor_copy(krb[:, :, :], ckvb[:, :, KVL:KVL + BR]).then_inc(dve_step, 1)
                v.tensor_copy(kir[:, :, 0:64], cqb[:, :, 0:64]).then_inc(dve_step, 1)
                stepped(3)
                dve_rope(kir[:, :, 0:64].unsqueeze(2), 16, "b", tmp_a, False)
                v.tensor_copy(kir[:, :, 64:128], kir[:, :, 0:64]).then_inc(dve_step, 1)
                stepped()
                evac_done(v, "qi")
                dve_rope(qi[:, :, :, :], 16, "b", tmp_a, True)
            elif name in ("qa", "ka"):
                x, tmp, c = {"qa": (qa, tmp_a, 0), "ka": (ka, tmp_b, AD)}[name]
                evac_done(v, name)
                dve_rms(name, x[:, :, :, :], tmp, vh[:, c:c + AD])
                dve_rope(x[:, :, :, :], 32, "a", tmp, True)
            elif name in ("qb0", "qb1"):
                q = int(name[2])
                evac_done(v, "uq" + name[2])
                x = qb[:, :, 4 * q:4 * q + 4, 0:BQ]
                dve_rms(name, x, tmp_a, vh[:, 2 * AD:2 * AD + BQ])
                dve_rope(x[:, :, :, BN:BQ], 16, "b", tmp_a, True)
            else:
                evac_done(v, "ukv1")
                v.tensor_copy(kb[:, :, :, BN:BQ], krb[:, :, :].unsqueeze(2).to_broadcast([P, TT, BH, BR])).then_inc(dve_step, 1)
                stepped()
                dve_rms("kb", kb[:, :, :, 0:BQ], tmp_b, vh[:, 2 * AD + BQ:])
                dve_rope(kb[:, :, :, BN:BQ], 16, "b", tmp_b, True)

        IDX = [(i, h) for i in range(1, TT) for h in range(AH)]

        def pe_index():
            t = nc.tensor
            evac_done(t, "Tki")
            for u, (i, h) in enumerate(IDX):
                if u >= 4:
                    t.wait_ge(sem("idx_sum"), u - 3)
                r = slice(64 * (h % 2), 64 * (h % 2) + 64)
                t.matmul(PS[:, 4 + u % 4, 0:(i + 1) * P], qi.rearrange("p t h c -> p t (h c)")[r, i, (h // 2) * P:(h // 2 + 1) * P],
                         kir.rearrange("p t c -> p (t c)")[r, 0:(i + 1) * P], start=True, stop=True).then_inc(sem("idx_dot"), 1)

        def act_index():
            a = nc.scalar
            for u, (i, h) in enumerate(IDX):
                a.wait_ge(sem("idx_dot"), u + 1)
                n = (i + 1) * P
                a.activation(PS[:, 4 + u % 4, 0:n], PS[:, 4 + u % 4, 0:n], ACT.Relu).then_inc(sem("idx_relu"), 1)

        def dve_index():
            v = nc.vector
            v.tensor_copy(identr[:, :], ident).then_inc(sem("mask"), 1)
            for u, (i, h) in enumerate(IDX):
                v.wait_ge(sem("idx_relu"), u + 1)
                n = (i + 1) * P
                s, w = score[i - 1][:, 0:n], wi[:, i, h:h + 1]
                if h == 0:
                    v.tensor_scalar(s, PS[:, 4 + u % 4, 0:n], w, None, ALU.mult).then_inc(sem("idx_sum"), 1)
                else:
                    v.wait_ge(sem("idx_sum"), u)
                    v.scalar_tensor_tensor(out=s, in0=PS[:, 4 + u % 4, 0:n], scalar=w, in1=s, op0=ALU.mult,
                                           op1=ALU.add).then_inc(sem("idx_sum"), 1)
                if h == AH - 1:
                    v.wait_ge(sem("idx_sum"), u + 1)
                    v.tensor_scalar(s, s, (AH * AD) ** -0.5, None, ALU.mult).then_inc(dve_step, 1)
                    stepped()
                    v.memset(score[i - 1][0:64, n - 64:n], NEG).then_inc(dve_step, 1)
                    stepped()

        ROUNDS = TOPK // 8
        EARLY = 24

        def top_find(r):
            i = 2 - r // ROUNDS
            nc.vector.max(top8[:, :], score[i][:, 0:(i + 2) * P]).then_inc(dve_step, 1)

        def top_mark(r):
            v, i = nc.vector, 2 - r // ROUNDS
            s = score[i][:, 0:(i + 2) * P]
            stepped()
            v.match_replace(s, top8[:, :], s, MAX_NEG).then_inc(dve_step, 1)
            stepped()
            if r % ROUNDS == ROUNDS - 1:
                v.tensor_scalar(topm[i][:, 0:(i + 2) * P], s, MAX_NEG, NEG, ALU.not_equal, ALU.mult).then_inc(sem("mask"), 1)

        def mask_a(i):
            return (True, topm[i - 1][:, 0:(i + 1) * P]) if i else (False, const("negchunk"))

        def after_out(side):
            def after(i):
                c = 512 * side
                nc.vector.tensor_tensor(gz[:, i, c:c + 512], gz[:, i, c:c + 512], obuf[i % 2][:, :], ALU.mult).then_inc(sem("gated"), 1)
            return after

        def out_view(i, b):
            return obuf[i % 2][:, :].rearrange("p (a b c) -> p a b c", a=4, b=2)

        qaT, kaT = (x.rearrange("p t h c -> p t (h c)") for x in (qa, ka))

        def half_of(h):
            return slice(64 * (h % 2), 64 * (h % 2) + 64), slice((h // 2) * P, (h // 2 + 1) * P)

        MLA = Attention([FOX], BH, lambda h, i: qb[0:BQ, i, h, :], lambda h, a, b: kb[0:BQ, a:b, h, :],
                        lambda h, j: vb[:, j, h, :], lambda i: (False, const("negchunk")), out_view, pbuf, ptbuf,
                        after=after_out(1), copies="scalar")
        SPA = Attention([FOX, MLA], AH, lambda h, i: qaT[half_of(h)[0], i, half_of(h)[1]],
                        lambda h, a, b: kaT[half_of(h)[0], a:b, half_of(h)[1]],
                        lambda h, j: va[:, j, h, :], mask_a, out_view, pbuf, ptbuf, after=after_out(0), copies="scalar",
                        ready=lambda i: nc.tensor.wait_ge(sem("mask"), 5 - i))
        T2 = Turn(8, lambda t, k: gz[:, t, k * P:(k + 1) * P], lambda eng, t: eng.wait_ge(sem("gated"), 2 * TT))
        OUT = Mix(4, "out2", 4, None)

        def top_round(r):
            if r < 3 * ROUNDS:
                top_find(r)
                top_mark(r)

        def pe_second():
            n = SLOT_OF[STEPS[0]]
            for t in range(0, TT, 2):
                N2.T.pe_tile(t)
                N2.T.pe_tile(t + 1)
                for c in (t, t + 1):
                    N2.T.tile_done(nc.tensor, c)
                    for m in range(2):
                        nc.tensor.wait_ge(w_lo, n + m + 1)
                        tok_slot(n + m, 4 * m, 4, COLS[STEPS[0]], 0, m == 0, m == 1, tiles=[c])
            for name in STEPS[1:]:
                if name == "gb":
                    pe_index()
                pe_step(name)
            evac_done(nc.tensor, STEPS[-1])
            pe_attend([MLA, SPA])
            T2.pe()
            pe_rows(OUT, "out2", T2)

        def act_second():
            rt_after = {"cq": ("cq", TT), "ckv": ("ckv", TT), "uq0": ("qa", 32), "uq1": ("qb0", 16), "ukv1": ("qb1", 16),
                        "ka": ("kb", 32), "va": ("ka", 32)}
            for name in STEPS:
                if name == "gb":
                    act_index()
                act_step(name)
                if name in rt_after:
                    act_rt(*rt_after[name])
            act_attend([MLA, SPA])
            T2.act()
            for n in range(2):
                act_split(BASE["out2"] + 2 + n)

        def dve_second():
            v = nc.vector
            for name in PREPS:
                dve_prep(name)
            dve_index()
            for n in range(EARLY):
                top_round(n)
            dve_attend([MLA, SPA], lambda n: top_round(EARLY + n))
            for t in range(TT):
                T2.dve(t)
            for t in range(TT):
                OUT.mix_ready(v, t)
                x2 = x_sb[:, t, :].rearrange("p (a b) -> p a b", a=2)
                v.tensor_tensor(x2, x2, PS[:, 2 * t:2 * t + 2, :], ALU.add).then_inc(sem("out_x"), 1)

        def sp_second(load):
            s = nc.sync
            s.wait_ge(sem("at_out"), 2 * TT)
            s.wait_ge(sem("mix_x"), 4 * TT)
            s.dma_start(vlat[:, :], vecs[0:1, 288:928].partition_broadcast(P)).then_inc(sem("vec2_in"), 16)
            s.dma_start(vh[:, 0:2 * AD], vecs[0:1, 160:288].partition_broadcast(P)).then_inc(sem("vec2_in"), 16)
            s.dma_start(vh[:, 2 * AD:], vecs[0:1, 928:1120].partition_broadcast(P)).then_inc(sem("vec2_in"), 16)
            load(BASE["in2"] + 2, NSLOT)
            for t in range(TT):
                s.wait_ge(sem("out_x"), t + 1)
                s.dma_start(out[0, t * P:(t + 1) * P, :], x_sb[:, t, :]).then_inc(sem("out_done"), 16)
            s.wait_ge(sem("out_done"), 16 * TT)

        block = ctx.enter_context(nc.Block())

        @block.tensor
        def _(t):
            t.wait_ge(sem("const_in"), 16)
            N0.pe_head(BASE["qkv"])
            with t.Fori(1, 6) as i:
                pe_qkv_step(i)
            pe_z()
            pe_gates()
            for c in range(TT):
                pe_chunk(c)
            t.wait_ge(sem("g_o2"), 2 * TT)
            GT.pe()
            pe_rows(GOUT, "gout", GT)
            F0.pe()
            pe_foxproj()
            pe_fox()
            pe_rows(FO, "fo", FT_)
            F1.pe()
            pe_second()

        @block.scalar
        def _(a):
            N0.act_first()
            act_qkv_step(0, True)
            with a.Fori(1, 6) as i:
                act_qkv_step(i, False)
            act_z()
            for c in range(TT):
                act_chunk(c)
            act_squared(TT - 1)
            GT.act_tile(0)
            act_root(TT - 1)
            for t in range(1, TT):
                GT.act_tile(t)
            act_rows(GOUT, "gout", NF0)
            F0.act()
            act_foxproj()
            act_attend([FOX])
            FT_.act()
            act_rows(FO, "fo", NF1)
            F1.act()
            act_second()

        @block.vector
        def _(v):
            for i in range(4):
                v.memset(cvb[i][:, 0:3], 0.0).then_inc(dve_step, 1)
            v.memset(pick[:, :], 0.0).then_inc(dve_step, 1)
            stepped(5)
            v.memset(pick[:, 15:16], 1.0).then_inc(sem("pick"), 1)
            N0.dve()
            v.wait_ge(sem("vec_in"), 32)
            dve_qkv_step(0, True)
            with v.Fori(1, 6) as i:
                dve_qkv_step(i, False)
            dve_gates()
            for c in range(TT):
                dve_chunk(c)
            dve_mean(TT - 1)
            GT.dve(0)
            dve_gated(TT - 1)
            for t in range(1, TT):
                GT.dve(t)
            dve_chain(GOUT, NF0)
            F0.dve()
            dve_foxproj()
            dve_attend([FOX])
            for t in range(TT):
                FT_.dve(t)
            dve_chain(FO, NF1)
            F1.dve()
            dve_second()

        def pool_low(n0, n1):
            p = nc.gpsimd

            def low(n, q, width=SLOT):
                p.wait_ge(w_hi, n + 1)
                p.tensor_tensor(wlo[q][:, 0:width], wraw[q][:, 0:width], whi[q][:, 0:width].bitcast(F32),
                                ALU.subtract).then_inc(w_lo, 1)

            if n0 in WIDTH:
                for n in range(n0, n1):
                    low(n, n % 2, WIDTH.get(n, SLOT))
                return

            if n0 % 2:
                low(n0, 1)
                n0 += 1
            if n1 - n0 >= 2:
                with p.Fori(0, (n1 - n0) // 2) as i:
                    low(n0 + 2 * i, 0)
                    low(n0 + 2 * i + 1, 1)
            if (n1 - n0) % 2:
                low(n1 - 1, 0)

        @block.gpsimd
        def _(p):
            pool_low(0, 2)
            p.wait_ge(sem("ws_hi"), 1)
            p.tensor_tensor(wslo[:, :], wsraw[:, :], wshi[:, :].bitcast(F32), ALU.subtract).then_inc(sem("ws_lo"), 1)
            pool_low(2, BASE["gout"] + 1)
            pool_decays(0)
            for c in range(TT):
                pool_chunk(c)
            pool_low(BASE["gout"] + 1, BASE["in2"])
            pool_low(BASE["in2"], BASE["in2b"])
            pool_low(BASE["in2b"], NSLOT)

        @block.sync
        def _(s):
            def load(n0, n1):

                def one(n, q, i=0):
                    if n >= 2:
                        s.wait_ge(w_lo, n - 1 + 2 * i)
                    s.dma_start(wraw[q][:, :], wpack[bass.ds(n + 2 * i, 1), :, :].rearrange("a p c -> (a p) c")).then_inc(w_loaded[q], 16)

                if n0 < 2:
                    one(0, 0)
                    one(1, 1)
                    n0 = 2
                if n0 % 2:
                    one(n0, 1)
                    n0 += 1
                if n1 - n0 >= 2:
                    with s.Fori(0, (n1 - n0) // 2) as i:
                        one(n0, 0, i)
                        one(n0 + 1, 1, i)
                if (n1 - n0) % 2:
                    one(n1 - 1, 0)

            def load_x(t):
                s.dma_start(x_sb[:, t, :], x_in[0, t * P:(t + 1) * P, :]).then_inc(sem(f"x_in{t}"), 16)

            load_x(0)
            gain_load(0, None)
            s.dma_start(csb[:, :], consts).then_inc(sem("const_in"), 16)
            load_x(1)
            s.dma_start(wraw[0][:, :], wpack[0]).then_inc(w_loaded[0], 16)
            s.dma_start(wraw[1][:, :], wpack[1]).then_inc(w_loaded[1], 16)
            load_x(2)
            load_x(3)
            s.dma_start(wsraw[:, 0:P], wba).then_inc(sem("ws_in"), 16)
            s.dma_start(wsraw[:, P:2 * P], wf).then_inc(sem("ws_in"), 16)
            s.dma_start(cw, convw).then_inc(sem("vec_in"), 16)
            s.dma_start(vc[:, :], vecs[0:1, 0:160].partition_broadcast(P)).then_inc(sem("vec_in"), 16)
            gain_load(1, None)
            load(2, BASE["gout"] + 2)
            s.wait_ge(sem("qk_ss"), 2 * GH)
            s.dma_start(msk[:, :, :], masks).then_inc(sem("msk_in"), 16)
            load(BASE["gout"] + 2, BASE["gout"] + 4)
            gain_load(2, lambda e: e.wait_ge(sem("g_og"), TT))
            load(BASE["gout"] + 4, BASE["fout0"])
            gain_load(3, lambda e: GOUT.x_ready(e, TT - 1))
            load(BASE["fout0"], BASE["fk"] + 2)
            gain_load(4, lambda e: NF0.T.done(e))
            gain_load(5, lambda e: FOUT0.x_ready(e, TT - 1))
            load(BASE["fk"] + 2, BASE["fo"])
            s.wait_ge(sem("c_rows"), 2)
            s.wait_ge(sem("rows1"), 2)
            s.dma_start(KA[64:65, :, :], crow[1][:, :]).then_inc(sem("crows_in"), 16)
            s.dma_start(QA[65:66, :, :], crow[0][:, :]).then_inc(sem("crows_in"), 16)
            load(BASE["fo"], BASE["fo"] + 4)
            gain_load(6, lambda e: NKV.T.done(e))
            gain_load(7, lambda e: NQ.T.done(e))
            load(BASE["fo"] + 4, BASE["fout1"])
            gain_load(8, lambda e: FO.x_ready(e, TT - 1))
            gain_load(9, lambda e: NF1.T.done(e))
            load(BASE["fout1"], BASE["in2"] + 2)
            sp_second(load)


def constants():
    i = np.arange(P)
    row, col = i[:, None], i[None, :]
    f = np.float32
    upto = np.ones((P, SEQ), f)
    upto[:, :P] = row <= col
    parts = {"ident": row == col, "upto": upto, "strict": row > col, "tril": row >= col,
             "negcausal": np.where(row >= col, 0.0, NEG), "negchunk": np.where((row // 64) >= (col // 64), 0.0, NEG)}
    pos = np.arange(SEQ).astype(f)
    for name, d in (("a", 64), ("b", 32)):
        freqs = np.power(f(10000.0), -np.arange(d // 2, dtype=f) * f(2.0) / f(d)).astype(f)
        ang = (pos[:, None] * freqs[None, :]).astype(f).reshape(TT, P, d // 2).transpose(1, 0, 2).reshape(P, -1)
        parts["cos" + name], parts["sin" + name] = np.cos(ang), np.sin(ang)
    table = np.concatenate([np.asarray(parts[n], f) for n, _ in CONSTS], axis=1)
    masks = []
    for l in range(LEVELS + 1):
        s = 1 << l
        m = ((row // (2 * s)) == (col // (2 * s))) & ((row // s) % 2 == 1) & ((col // s) % 2 == 0)
        if l == 0:
            masks.append(m)
        masks.append(m.T)
    return np.ascontiguousarray(table), np.ascontiguousarray(np.stack(masks, 1).astype(f))


def pack(inputs):
    n = {k: np.asarray(v) for k, v in inputs.items()}
    slots = []

    def add(a):
        a = a.reshape(P, -1)
        if a.shape[1] < SLOT:
            a = np.concatenate([a, np.zeros((P, SLOT - a.shape[1]), a.dtype)], axis=1)
        slots.append(a)

    def tiles(w, k0, nk, c0, c1):
        return w[k0 * P:(k0 + nk) * P, c0:c1].reshape(nk, P, c1 - c0).transpose(1, 0, 2)

    def by_features(w, c0, c1):
        for c in range(c0, c1, 256):
            add(tiles(w, 0, KT, c, c + 256))

    def by_tokens(w, blocks, nk=4):
        for c0, c1 in blocks:
            for k0 in range(0, KT, nk):
                add(tiles(w, k0, nk, c0, c1))

    def by_rows(w):
        for k0 in range(0, w.shape[0] // P, 2):
            add(tiles(w, k0, 2, 0, D))

    gin, kv = n["gdn_w_in"][0], n["w_kv"]
    by_features(gin, 0, 3072)
    by_tokens(gin, [(3072, 3584), (3584, 4096)])
    by_rows(n["gdn_w_out"][0])
    for l in range(2):
        if l == 1:
            by_features(kv, 0, D)
            by_tokens(kv, [(D, D + 512), (D + 512, 2 * D)])
            by_features(n["fox_w_q"][0], 0, D)
            by_rows(n["fox_w_o"][0])
        w = n["w_ffn_in"][l]
        for j in range(FT):
            g, u = tiles(w, 0, KT, j * P, (j + 1) * P), tiles(w, 0, KT, DFF + j * P, DFF + (j + 1) * P)
            add(np.concatenate([g, u], axis=2))
        by_rows(n["w_ffn_out"][l])
    by_tokens(n["w_in_2"][0], IN2_BLOCKS[:4])
    for h in range(2):
        add(tiles(n["w_uq_2"][0], 0, QL // P, 384 * h, 384 * (h + 1)))
    add(tiles(n["w_ukv_2"][0], 0, KVL // P, 0, D))
    by_tokens(n["w_in_2"][0], IN2_BLOCKS[4:])
    by_rows(n["w_out_2"][0])
    small = [tiles(w, 0, KT, c, c + 16).reshape(P, -1) for w, c in ((gin, 4096), (kv, 2 * D))]
    gains = np.stack([n["pre_mix_norm"][0], n["post_mix_norm"][0], n["pre_ffn_norm"][0], n["post_ffn_norm"][0],
                      n["kv_norm"], n["pre_mix_norm"][1], n["post_mix_norm"][1], n["pre_ffn_norm"][1],
                      n["post_ffn_norm"][1], n["norm_gain_2"][0]])
    convw = n["gdn_conv"][0].reshape(4, 3 * GH, P).transpose(2, 0, 1)
    vecs = np.concatenate([n["gdn_a_log"][0], n["gdn_dt_bias"][0], n["b_forget"], n["gdn_out_norm"][0],
                           n["a_q_norm_2"][0], n["a_k_norm_2"][0], n["b_q_latent_norm_2"][0],
                           n["b_kv_latent_norm_2"][0], n["b_q_norm_2"][0], n["b_k_norm_2"][0]])[None]
    assert len(slots) == NSLOT
    return {"wpack": np.stack(slots), "wba": small[0], "wf": small[1], "gains": gains,
            "convw": convw, "vecs": vecs}


def kernel(**inputs):
    import concourse.bacc as bacc
    from concourse.bass_utils import run_bass_kernel_spmd

    arrays = {"x": np.asarray(inputs["x"]), **pack(inputs)}
    arrays["consts"], arrays["masks"] = constants()
    arrays = {k: np.ascontiguousarray(v) for k, v in arrays.items()}
    nc = bacc.Bacc("TRN2", target_bir_lowering=False, num_devices=1, dynamic_dma_scratch_size=1024)
    aps = [nc.dram_tensor(k, a.shape, mybir.dt.from_np(a.dtype), kind="ExternalInput").ap() for k, a in arrays.items()]
    aps.append(nc.dram_tensor("out", (1, SEQ, D), F32, kind="ExternalOutput").ap())
    program(nc, *aps)
    return run_bass_kernel_spmd(nc, [arrays], core_ids=[0]).results[0]["out"]
```
